# Optimizing a Trainium2 kernel written in Bass

```python
import math
import functools
import jax
import jax.numpy as jnp
from jax import lax
import numpy as np

D_MODEL = 1024
BATCH = 1
SEQ = 256
DEPTH = 2

HEAD_DIM = 64
ROPE_DIM = HEAD_DIM // 4
NOPE_DIM = HEAD_DIM - ROPE_DIM
ROPE_THETA = 500000.0
N_HEADS_A = (3 * D_MODEL // 8) // HEAD_DIM
A_WIDTH = N_HEADS_A * HEAD_DIM
KV_LATENT = D_MODEL // 8
N_IDX_HEADS = 4
IDX_DIM = 64
IDX_ROPE_DIM = IDX_DIM // 4
TOPK_MAX = 256
N_POOL_GROUPS = 4
POOL_WINDOWS = (2, 4, 8, 16)
POOL_WIDTH = D_MODEL // 4
POOL_GROUP_DIM = POOL_WIDTH // N_POOL_GROUPS
N_HEADS_C = (D_MODEL // 4) // HEAD_DIM
C_WIDTH = N_HEADS_C * HEAD_DIM
N_BRANCHES = 3
IN_SIZES = (A_WIDTH, KV_LATENT, ROPE_DIM, N_IDX_HEADS * IDX_DIM, IDX_DIM, N_IDX_HEADS,
            POOL_WIDTH, C_WIDTH, C_WIDTH, C_WIDTH, N_BRANCHES * D_MODEL)
IN_WIDTH = sum(IN_SIZES)
Q_BLOCK = 128
N_SUPER = 4
D_FF = 2816
N_EXPERTS = 8
TOP_K = 2
D_FF_EXPERT = D_FF // TOP_K
RMS_EPS = 1e-6
N_DENSE = (DEPTH + 1) // 2
N_MOE = DEPTH // 2

kernel_name = "hybrid_dsa_pool_stickbreak_moe_block"

def rmsnorm(x, g):
    xf = x.astype(jnp.float32)
    y = xf * lax.rsqrt(jnp.mean(xf * xf, axis=-1, keepdims=True) + RMS_EPS)
    return (y * g.astype(jnp.float32)).astype(x.dtype)

def split_sizes(x, sizes):
    outs, off = [], 0
    for s in sizes:
        outs.append(x[..., off:off + s])
        off += s
    return outs

def rope_tables(positions, rot_dim):
    inv = ROPE_THETA ** (-jnp.arange(0, rot_dim, 2, dtype=jnp.float32) / rot_dim)
    ang = positions.astype(jnp.float32)[..., None] * inv
    return jnp.cos(ang)[:, :, None, :], jnp.sin(ang)[:, :, None, :]

def partial_rope(x, cos, sin):
    half = cos.shape[-1]
    r = 2 * half
    x1 = x[..., :half].astype(jnp.float32)
    x2 = x[..., half:r].astype(jnp.float32)
    rot = jnp.concatenate([x1 * cos - x2 * sin, x2 * cos + x1 * sin], axis=-1).astype(x.dtype)
    return jnp.concatenate([rot, x[..., r:]], axis=-1)

def to_blocks(a):
    b, l = a.shape[:2]
    a = a.reshape((b, l // Q_BLOCK, Q_BLOCK) + a.shape[2:])
    return jnp.moveaxis(a, 1, 0)

def from_blocks(a):
    a = jnp.moveaxis(a, 0, 1)
    return a.reshape((a.shape[0], a.shape[1] * a.shape[2]) + a.shape[3:])

def causal_chunks(L):
    n_super = math.gcd(N_SUPER, L // Q_BLOCK)
    return n_super, L // n_super

def _dsa_block(args, kc, vc, kic, k_sel):
    qb, qib, wib, start = args
    lk = kc.shape[1]
    key_pos = jnp.arange(lk, dtype=jnp.int32)
    qpos = start + jnp.arange(Q_BLOCK, dtype=jnp.int32)
    s = jnp.einsum('bqhd,bkd->bqhk', qib, kic).astype(jnp.float32) * IDX_DIM ** -0.5
    w = wib.astype(jnp.float32) * N_IDX_HEADS ** -0.5
    score = jnp.einsum('bqh,bqhk->bqk', w, jax.nn.relu(s))
    causal = key_pos[None, :] <= qpos[:, None]
    score = jnp.where(causal[None], score, -jnp.inf)
    _, idx = lax.top_k(score, k_sel)
    valid = idx <= qpos[None, :, None]
    kg = jax.vmap(lambda kk, ii: kk[ii])(kc, idx)
    vg = jax.vmap(lambda vv, ii: vv[ii])(vc, idx)
    logits = jnp.einsum('bqhd,bqkd->bqhk', qb, kg).astype(jnp.float32) * HEAD_DIM ** -0.5
    logits = jnp.where(valid[:, :, None, :], logits, -jnp.inf)
    p = jax.nn.softmax(logits, axis=-1).astype(vg.dtype)
    return jnp.einsum('bqhk,bqkd->bqhd', p, vg)

def dsa_attention(q, k, v, q_idx, k_idx, w_idx):
    L = q.shape[1]
    k_sel = min(TOPK_MAX, L // 4)
    n_super, chunk = causal_chunks(L)
    outs = []
    for ci in range(n_super):
        lk = (ci + 1) * chunk
        fn = functools.partial(_dsa_block, kc=k[:, :lk], vc=v[:, :lk], kic=k_idx[:, :lk], k_sel=k_sel)
        sl = slice(ci * chunk, (ci + 1) * chunk)
        starts = ci * chunk + jnp.arange(chunk // Q_BLOCK, dtype=jnp.int32) * Q_BLOCK
        out = lax.map(fn, (to_blocks(q[:, sl]), to_blocks(q_idx[:, sl]), to_blocks(w_idx[:, sl]), starts))
        outs.append(from_blocks(out))
    return jnp.concatenate(outs, axis=1)

def _stick_block(args, kc, vc):
    qb, start = args
    b, _, h, _ = qb.shape
    lk = kc.shape[1]
    nk = lk // Q_BLOCK
    key_pos = jnp.arange(lk, dtype=jnp.int32)
    qpos = start + jnp.arange(Q_BLOCK, dtype=jnp.int32)
    z = jnp.einsum('bqhd,bkhd->bhqk', qb, kc).astype(jnp.float32) * HEAD_DIM ** -0.5
    mask = (key_pos[None, :] < qpos[:, None])[None, None]
    log_keep = jnp.where(mask, jax.nn.log_sigmoid(-z), 0.0)
    blk = log_keep.reshape(b, h, Q_BLOCK, nk, Q_BLOCK)
    later = (jnp.arange(Q_BLOCK)[:, None] > jnp.arange(Q_BLOCK)[None, :]).astype(jnp.float32)
    within = jnp.einsum('bhqnj,js->bhqns', blk, later, precision=lax.Precision.HIGHEST)
    tot = jnp.sum(blk, axis=-1)
    after_blocks = lax.cumsum(tot, axis=3, reverse=True) - tot
    after = (within + after_blocks[..., None]).reshape(b, h, Q_BLOCK, lk)
    a = jnp.where(mask, jnp.exp(jax.nn.log_sigmoid(z) + after), 0.0).astype(vc.dtype)
    return jnp.einsum('bhqk,bkhd->bqhd', a, vc)

def stick_breaking_attention(q, k, v):
    L = q.shape[1]
    n_super, chunk = causal_chunks(L)
    outs = []
    for ci in range(n_super):
        lk = (ci + 1) * chunk
        fn = functools.partial(_stick_block, kc=k[:, :lk], vc=v[:, :lk])
        starts = ci * chunk + jnp.arange(chunk // Q_BLOCK, dtype=jnp.int32) * Q_BLOCK
        out = lax.map(fn, (to_blocks(q[:, ci * chunk:(ci + 1) * chunk]), starts))
        outs.append(from_blocks(out))
    return jnp.concatenate(outs, axis=1)

def multiscale_pool(u, w_pool, pool_scale):
    b, l, _ = u.shape
    ug = u.astype(jnp.float32).reshape(b, l, N_POOL_GROUPS, POOL_GROUP_DIM)
    csum = jnp.cumsum(ug, axis=1)
    count_base = jnp.arange(1, l + 1, dtype=jnp.float32)
    pooled = []
    for g, win in enumerate(POOL_WINDOWS):
        cg = csum[:, :, g]
        lagged = jnp.pad(cg, ((0, 0), (win, 0), (0, 0)))[:, :l]
        cnt = jnp.minimum(count_base, float(win))[None, :, None]
        pooled.append((cg - lagged) / cnt)
    p = (jnp.stack(pooled, axis=2) - ug).astype(u.dtype)
    y = jnp.einsum('blgc,gcd->blgd', p, w_pool) * pool_scale.reshape(N_POOL_GROUPS, POOL_GROUP_DIM)
    return y.reshape(b, l, POOL_WIDTH)

def hybrid_mixer(h, rope_a, rope_i, w_in, g_lat, w_uk, w_uv, w_pool, pool_scale,
                 w_br_a, w_br_b, w_br_c, w_out):
    b, l, _ = h.shape
    cos_a, sin_a = rope_a
    cos_i, sin_i = rope_i
    proj = h @ w_in
    (q_a, lat, k_rope, q_idx, k_idx, w_idx, u_pool, q_c, k_c, v_c, gates) = split_sizes(proj, IN_SIZES)
    q_a = partial_rope(q_a.reshape(b, l, N_HEADS_A, HEAD_DIM), cos_a, sin_a)
    lat = rmsnorm(lat, g_lat)
    k_a = jnp.concatenate([partial_rope(k_rope[:, :, None, :], cos_a, sin_a)[:, :, 0], lat @ w_uk], axis=-1)
    v_a = lat @ w_uv
    q_idx = partial_rope(q_idx.reshape(b, l, N_IDX_HEADS, IDX_DIM), cos_i, sin_i)
    k_idx = partial_rope(k_idx[:, :, None, :], cos_i, sin_i)[:, :, 0]
    y_a = dsa_attention(q_a, k_a, v_a, q_idx, k_idx, w_idx).reshape(b, l, A_WIDTH)
    y_b = multiscale_pool(u_pool, w_pool, pool_scale)
    y_c = stick_breaking_attention(q_c.reshape(b, l, N_HEADS_C, HEAD_DIM),
                                   k_c.reshape(b, l, N_HEADS_C, HEAD_DIM),
                                   v_c.reshape(b, l, N_HEADS_C, HEAD_DIM)).reshape(b, l, C_WIDTH)
    g_a, g_b, g_c = jnp.split(jax.nn.sigmoid(gates), N_BRANCHES, axis=-1)
    merged = g_a * (y_a @ w_br_a) + g_b * (y_b @ w_br_b) + g_c * (y_c @ w_br_c)
    return merged @ w_out

def swiglu(x, w_gate, w_up, w_down):
    return (jax.nn.silu(x @ w_gate) * (x @ w_up)) @ w_down

def moe_swiglu(h, w_router, w_gate, w_up, w_down):
    b, l, d = h.shape
    xf = h.reshape(b * l, d)
    logits = (xf @ w_router).astype(jnp.float32)
    top_val, top_idx = lax.top_k(logits, TOP_K)
    probs = jax.nn.softmax(top_val, axis=-1)
    combine = jnp.sum(jax.nn.one_hot(top_idx, N_EXPERTS, dtype=jnp.float32) * probs[..., None], axis=1)
    out = jnp.zeros_like(xf)
    for e in range(N_EXPERTS):
        out = out + combine[:, e:e + 1].astype(xf.dtype) * swiglu(xf, w_gate[e], w_up[e], w_down[e])
    return out.reshape(b, l, d)

def setup_inputs(seed: int = 0) -> dict:
    key = jax.random.key(seed)
    ks = jax.random.split(key, 22)
    f32 = jnp.float32

    def nrm(k, shape, fan_in):
        return jax.random.normal(k, shape, f32) * fan_in ** -0.5

    return {
        "x": jax.random.normal(ks[0], (BATCH, SEQ, D_MODEL), f32),
        "c": jax.random.normal(ks[1], (BATCH, D_MODEL), f32),
        "positions": jnp.broadcast_to(jnp.arange(SEQ, dtype=jnp.int32), (BATCH, SEQ)),
        "w_ada": nrm(ks[2], (DEPTH, D_MODEL, 6 * D_MODEL), D_MODEL),
        "b_ada": 0.02 * jax.random.normal(ks[3], (DEPTH, 6 * D_MODEL), f32),
        "norm_gains": 1.0 + 0.05 * jax.random.normal(ks[4], (DEPTH, 4, D_MODEL), f32),
        "w_in": nrm(ks[5], (DEPTH, D_MODEL, IN_WIDTH), D_MODEL),
        "g_kv_latent": 1.0 + 0.05 * jax.random.normal(ks[6], (DEPTH, KV_LATENT), f32),
        "w_uk": nrm(ks[7], (DEPTH, KV_LATENT, NOPE_DIM), KV_LATENT),
        "w_uv": nrm(ks[8], (DEPTH, KV_LATENT, HEAD_DIM), KV_LATENT),
        "w_pool": nrm(ks[9], (DEPTH, N_POOL_GROUPS, POOL_GROUP_DIM, POOL_GROUP_DIM), POOL_GROUP_DIM),
        "pool_scale": 1.0 + 0.1 * jax.random.normal(ks[10], (DEPTH, POOL_WIDTH), f32),
        "w_br_a": nrm(ks[11], (DEPTH, A_WIDTH, D_MODEL), A_WIDTH),
        "w_br_b": nrm(ks[12], (DEPTH, POOL_WIDTH, D_MODEL), POOL_WIDTH),
        "w_br_c": nrm(ks[13], (DEPTH, C_WIDTH, D_MODEL), C_WIDTH),
        "w_out": nrm(ks[14], (DEPTH, D_MODEL, D_MODEL), D_MODEL),
        "w_gate_dense": nrm(ks[15], (N_DENSE, D_MODEL, D_FF), D_MODEL),
        "w_up_dense": nrm(ks[16], (N_DENSE, D_MODEL, D_FF), D_MODEL),
        "w_down_dense": nrm(ks[17], (N_DENSE, D_FF, D_MODEL), D_FF),
        "w_router": nrm(ks[18], (N_MOE, D_MODEL, N_EXPERTS), D_MODEL),
        "w_gate_moe": nrm(ks[19], (N_MOE, N_EXPERTS, D_MODEL, D_FF_EXPERT), D_MODEL),
        "w_up_moe": nrm(ks[20], (N_MOE, N_EXPERTS, D_MODEL, D_FF_EXPERT), D_MODEL),
        "w_down_moe": nrm(ks[21], (N_MOE, N_EXPERTS, D_FF_EXPERT, D_MODEL), D_FF_EXPERT),
    }

def reference(x, c, positions, w_ada, b_ada, norm_gains, w_in, g_kv_latent, w_uk, w_uv,
              w_pool, pool_scale, w_br_a, w_br_b, w_br_c, w_out,
              w_gate_dense, w_up_dense, w_down_dense,
              w_router, w_gate_moe, w_up_moe, w_down_moe):
    rope_a = rope_tables(positions, ROPE_DIM)
    rope_i = rope_tables(positions, IDX_ROPE_DIM)
    cond = jax.nn.silu(c)
    for layer in range(DEPTH):
        mod = cond @ w_ada[layer] + b_ada[layer]
        sh1, sc1, gt1, sh2, sc2, gt2 = [m[:, None, :] for m in jnp.split(mod, 6, axis=-1)]
        h = rmsnorm(x, norm_gains[layer, 0]) * (1.0 + sc1) + sh1
        y = hybrid_mixer(h, rope_a, rope_i, w_in[layer], g_kv_latent[layer], w_uk[layer], w_uv[layer],
                         w_pool[layer], pool_scale[layer], w_br_a[layer], w_br_b[layer], w_br_c[layer],
                         w_out[layer])
        x = x + gt1 * rmsnorm(y, norm_gains[layer, 1])
        h = rmsnorm(x, norm_gains[layer, 2]) * (1.0 + sc2) + sh2
        i = layer // 2
        if layer % 2 == 0:
            y = swiglu(h, w_gate_dense[i], w_up_dense[i], w_down_dense[i])
        else:
            y = moe_swiglu(h, w_router[i], w_gate_moe[i], w_up_moe[i], w_down_moe[i])
        x = x + gt2 * rmsnorm(y, norm_gains[layer, 3])
    return x


_drawn_inputs = setup_inputs


def setup_inputs(seed=0):
    import zlib

    import numpy as np

    out = dict(_drawn_inputs(seed))
    spreads = {}
    factors = {}
    for name, (base, spread) in spreads.items():
        noise = np.random.default_rng([zlib.crc32(name.encode()), seed]).standard_normal(out[name].shape)
        drawn = base * np.exp(spread * noise) if base else spread * noise
        out[name] = jnp.asarray(drawn.astype(out[name].dtype))
    for name, factor in factors.items():
        out[name] = (out[name] * factor).astype(out[name].dtype)
    return out
```

```python
from contextlib import ExitStack

import numpy as np
import concourse.bass as bass
from concourse import mybir

P = 128
F32 = mybir.dt.float32
I32 = mybir.dt.int32
ALU = mybir.AluOpType
ACT = mybir.ActivationFunctionType
AX = mybir.AxisListType

HEAD = 64
ROPE = HEAD // 4
NOPE = HEAD - ROPE
HALF = ROPE // 2
THETA = 500000.0
WINDOWS = (2, 4, 8, 16)
TOPK = 64
EPS = 1e-6
NOT_CAUSAL = -3.0e38
TAKEN = -3.4e38
FAR = -1.0e30
ROUNDER = 1.5 * 2.0 ** 23
TWO_PI = (6.28125, 0.0019354820251464844, -1.7484556025237907e-07)
PI_BELOW = 3.1415925


def shape_constants():
    r = np.arange(P)
    row, col = r[:, None], r[None, :]
    parts = {
        "ident": (row == col).astype(np.float32),
        "ones": np.ones((P, P), np.float32),
        "neg_from": -(row >= col).astype(np.float32),
        "neg_ones": -np.ones((P, P), np.float32),
        "before": np.where(row < col, 0.0, FAR).astype(np.float32),
        "causal": (col <= row).astype(np.float32),
        "not_causal": np.where(col <= row, 0.0, NOT_CAUSAL).astype(np.float32),
        "earlier": (row < col).astype(np.float32),
        "place": np.broadcast_to(np.arange(P, dtype=np.float32)[None, :], (P, P)),
        "inv_freq": np.broadcast_to((np.float32(THETA) ** (-np.arange(0, ROPE, 2, dtype=np.float32) / np.float32(ROPE)))[None, :], (P, HALF)).astype(np.float32),
    }
    t = np.arange(2 * P)[None, :]
    for st in range(2):
        s = r[:, None] + P * st
        for g, w in enumerate(WINDOWS):
            inside = (s <= t) & (s > t - w)
            band = np.where(inside, np.float32(1) / np.minimum(t + 1, w).astype(np.float32), np.float32(0))
            parts[f"band{st}{g}"] = (band - (s == t)).astype(np.float32)
    e = np.arange(8)
    parts["earlier8"] = np.broadcast_to((e[None, :] < e[:, None]).astype(np.float32).reshape(1, 64), (P, 64))
    at, offsets = 0, {}
    for name, a in parts.items():
        offsets[name] = (at, a.shape[1])
        at += a.shape[1]
    return np.ascontiguousarray(np.concatenate(list(parts.values()), axis=1)), offsets


def build_trunk(nc, x_in, c, positions, w_ada, b_ada, norm_gains, w_in, g_kv_latent, w_uk, w_uv,
                w_pool, pool_scale, w_br_a, w_br_b, w_br_c, w_out, w_gate_dense, w_up_dense,
                w_down_dense, w_router, w_gate_moe, w_up_moe, w_down_moe, consts, const_at, out):
    DEPTH, D, IN_WIDTH = w_in.shape
    T = x_in.shape[1]
    TT = T // P
    KD = D // P
    WA, WB, WC = w_br_a.shape[1], w_br_b.shape[1], w_br_c.shape[1]
    LAT = w_uk.shape[1]
    HA, HC = WA // HEAD, WC // HEAD
    E, _, FE = w_gate_moe.shape[1:]
    FF = w_gate_dense.shape[2]
    HI = 4
    assert TT == 2 and DEPTH == 2 and FF % FE == 0 and LAT == P and WB == 256 and WC == 256

    C_QA, C_LAT = 0, WA
    C_KR = C_LAT + LAT
    C_QI = C_KR + ROPE
    C_KI = C_QI + HI * HEAD
    C_WI = C_KI + HEAD
    C_U = C_WI + HI
    C_QC = C_U + WB
    C_KC = C_QC + WC
    C_VC = C_KC + WC
    C_G = C_VC + WC
    NATW = C_QC

    NS, SLOTW = 9, KD * 256
    W_IN_SLOTS = [(0, 256), (256, 256), (512, 256), (768, C_U - 768), (C_U, 256), (C_QC, 256),
                  (C_KC, 256), (C_VC, 256)] + [(C_G + 256 * j, 256) for j in range(3 * D // 256)]
    NIN = len(W_IN_SLOTS)
    NADA = 6 * D // 256
    F_CHUNKS = [(256 * j, min(256, FE - 256 * j)) for j in range((FE + 255) // 256)]
    FT = FE // P
    UNIT = 3 * len(F_CHUNKS)
    assert UNIT % NS == 0
    DENSE_UNITS = FF // FE

    def mixer_slots(l):
        s = [("ada", 0, j) for j in range(8)] if l == 0 else []
        for j in range(NIN):
            s.append(("in", l, j))
            if l == 0 and j >= ADA_FROM:
                s += [("ada", 0, a) for a in ada_beside(j)]
        s += [("br", l, j) for j in range(4)]
        return s + [("out", l, j) for j in range(4)]

    ADA_FROM = NIN - (NADA - 8) // 2
    def ada_beside(j):
        return (8 + 2 * (j - ADA_FROM), 9 + 2 * (j - ADA_FROM)) if j >= ADA_FROM else ()

    NCH = len(F_CHUNKS)
    ADA_AFTER = {}
    for a in range(NADA):
        n = a // 2
        g = n // NCH * FT + 2 * (n % NCH) + 1 + a % 2
        ADA_AFTER.setdefault(min(g, DENSE_UNITS * FT - 1), []).append(a)

    def dense_slots():
        s = []
        for u in range(DENSE_UNITS):
            for ch in range(NCH):
                n = u * NCH + ch
                s += [("gate", u, ch), ("up", u, ch), ("down", u, ch)]
                s += [("ada", 1, 2 * n), ("ada", 1, 2 * n + 1)]
        return s

    LOADS = mixer_slots(0) + dense_slots() + mixer_slots(1)
    NUMBER = {key: n for n, key in enumerate(LOADS)}
    EXPERT0 = len(LOADS)
    TURNS = UNIT // NS
    KINDS = ("gate", "up", "down")

    def load_number(key):
        if key[1] == "moe":
            return EXPERT0 + 3 * key[2] + KINDS.index(key[0])
        return NUMBER[key]

    JOBS = []
    def job(bank, *key):
        JOBS.append((key, bank))
    for l in range(DEPTH):
        if l == 0:
            for a in range(8):
                job(2 + a % 2, "ada", 0, a)
        for j in range(4):
            job(j, "xT", l, j)
        for j in range(NIN):
            job(j % 2, "in", l, j)
            if l == 0:
                for a in ada_beside(j - 1):
                    job(2 + a % 2, "ada", 0, a)
            if j == 7:
                for n in range(4):
                    job(4 + n, "tr", l, n)
            if j == 9:
                for t in range(TT):
                    for par in range(2):
                        job(4 + 2 * t + par, "idx", l, t, par)
            if j == 10:
                job(4, "ukv", l)
                job(5, "pool", l)
                job(4, "kT", l)
                job(5, "yb", l)
            if 13 <= j < 13 + HC and j % 2 == 1:
                job(6, "yc", l, (j - 13) // 2)
            if 12 <= j < 12 + HC:
                job(4 + (j - 12) % 2, "stick2", l, j - 12)
            if 11 <= j < 11 + HC:
                job(4 + (j - 11) % 2, "stick", l, j - 11)
        if l == 0:
            for a in ada_beside(NIN - 1):
                job(2 + a % 2, "ada", 0, a)
        for t in range(TT):
            for b in ([4, 5] if t == 0 else [4, 5, 6, 7]):
                job(b, "logit", l, t, b)
            for kt in range(t + 1):
                for b in (0, 1):
                    job(b, "pT", l, t, kt, b)
            job(2, "av", l, t)
        for m in range(4):
            for b in (4, 5, 6):
                job(b, "br", l, m, b)
        for b in range(4):
            job(b, "y", l, b)
        for j in range(4):
            job(4 + j, "hT", l, j)
        if l == 1:
            job(2, "route", l)
            job(2, "count", l)
        if l == 0:
            for g in range(DENSE_UNITS * FT):
                u, f = g // FT, g % FT
                job(f % 3, "gu", u, f)
                if f == 0 and u > 0:
                    pass
                for a in ADA_AFTER.get(g - 1, ()):
                    job(3, "ada", 1, a)
                if f == FT - 1:
                    for b in range(4):
                        job(4 + b, "down", u, b)
            for a in ADA_AFTER.get(DENSE_UNITS * FT - 1, ()):
                job(3, "ada", 1, a)
    seen, ORD, BANK = [0] * 8, {}, {}
    for key, bank_no in JOBS:
        assert key not in ORD, key
        ORD[key], BANK[key] = seen[bank_no], bank_no
        seen[bank_no] += 1
    MOE_FIRST = list(seen)
    GU_PER = [len([f for f in range(FT) if f % 3 == b]) for b in range(3)]
    assert HC == 4 and NIN >= 18 and (NADA - 8) % 2 == 0

    ctx = ExitStack()
    with ctx:
        def sb(name, shape, dt=F32):
            return ctx.enter_context(nc.sbuf_tensor(name, shape, dt))

        def sem(name):
            return ctx.enter_context(nc.semaphore(name))

        ps = ctx.enter_context(nc.psum_tensor("ps", [P, 8, 512], F32))
        ring = sb("ring", [P, NS, SLOTW])
        cst = sb("cst", [P, consts.shape[1]])
        x = sb("x", [P, TT, D])
        xn = sb("xn", [P, TT, D])
        hT = sb("hT", [P, KD, T])
        big = sb("big", [P, 24 * T])
        gT = big[:, :].rearrange("p (m t) -> p m t", t=T)
        yacc = big[:, 0:TT * D].rearrange("p (t d) -> p t d", t=TT)
        hid = big[:, TT * D:TT * D + 2 * T].rearrange("p (b t) -> p b t", b=2)
        sig = big[:, TT * D + 2 * T:TT * D + 4 * T].rearrange("p (b t) -> p b t", b=2)
        gsig = big[:, TT * D + 4 * T:TT * D + 6 * T].rearrange("p (b t) -> p b t", b=2)
        resid = big[:, TT * D + 6 * T:TT * D + 6 * T + D]
        gtg = sb("gtg", [P, 3, D])
        acc = sb("acc", [P, 4, 256])
        natP = sb("natP", [P, TT, NATW])
        vc = sb("vc", [P, TT, WC])
        qkc = sb("qkc", [P, 4, T])
        trs = sb("trs", [P, 8, P])
        qT = sb("qT", [P, 3, T])
        kn = sb("kn", [P, TT, P])
        ki = sb("ki", [P, TT, P])
        latn = sb("latn", [P, TT, LAT])
        kT = sb("kT", [P, T])
        va = sb("va", [P, TT, HEAD])
        poolT = sb("poolT", [P, 2, T])
        yaT = sb("yaT", [P, 3, T])
        ybT = sb("ybT", [P, 2, T])
        ycT = sb("ycT", [P, 2, T])
        multi = sb("multi", [P, 3, 512])
        score = sb("score", [P, TT, T])
        take = sb("take", [P, TT, T])
        pT = sb("pT", [P, 2, HA * P])
        spl = pT[:, 0, :].rearrange("p (b n) -> p b n", b=2)
        rel = multi[:, :, :].rearrange("p a b -> p (a b)")[:, 0:768].rearrange("p (b n) -> p b n", b=2)
        aT = pT[:, 1, :].rearrange("p (b n) -> p b n", b=2)
        lg = xn[:, :, :].rearrange("p t d -> p (t d)")[:, 0:HA * T]
        c_col = sb("c_col", [P, KD])
        cond = sb("cond", [P, KD])
        pos_i = sb("pos_i", [P, TT], I32)
        pos_f = sb("pos_f", [P, TT])
        ang = sb("ang", [P, TT, HALF])
        turns = sb("turns", [P, TT, 2, HALF])
        red = sb("red", [P, TT, 2, HALF])
        cs = sb("cs", [P, TT, 2, HALF])
        rot = sb("rot", [P, 4, TT * 6 * HALF])
        gcol = sb("gcol", [P, DEPTH, 2, KD])
        modc = sb("modc", [P, DEPTH, 4, KD])
        glat = sb("glat", [P, DEPTH])
        pscale = sb("pscale", [P, DEPTH, 2])
        wukv = sb("wukv", [P, DEPTH, NOPE + HEAD])
        wpool = sb("wpool", [P, DEPTH, 2, P])
        wroute = sb("wroute", [P, KD, E])
        comb = sb("comb", [P, TT, E])
        ss = sb("ss", [P, DEPTH * 5, TT])
        var = sb("var", [P, DEPTH * 5, TT])
        guess = sb("guess", [P, DEPTH * 5, TT])
        newt = sb("newt", [P, 2, TT])
        rstd = sb("rstd", [P, DEPTH * 5, TT])
        nmax = sb("nmax", [P, DEPTH, TT, HA])
        psum_exp = sb("psum_exp", [P, DEPTH, TT, HA])
        pinv = sb("pinv", [P, DEPTH, TT, HA])
        top8 = sb("top8", [P, 8])
        rout = multi[:, :, :].rearrange("p a b -> p (a b)")[:, 768:768 + 3 * TT * E * E].rearrange("p (a n) -> p a n", a=3)
        rsm = sb("rsm", [P, 6, TT * E])
        picked = sb("picked", [P, TT, E])
        place_of = sb("place_of", [P, TT, E + 1])
        tokens_of = sb("tokens_of", [P, E], I32)
        xg = natP[:, :, :].rearrange("p t n -> p (t n)")[:, 0:KD * P].rearrange("p (k s) -> p k s", k=KD)
        yg = natP[:, :, :].rearrange("p t n -> p (t n)")[:, KD * P:KD * P + D]
        sel = qT[:, 0, :].rearrange("p (t s) -> p t s", t=TT)
        selT = qT[:, 1, :]
        hidT = trs[:, 0:4, :].rearrange("p (b r) s -> p b r s", b=2)

        def const(name):
            at, n = const_at[name]
            return cst[:, at:at + n]

        ident, ones = const("ident"), const("ones")


        loaded = [sem(f"slot_loaded{i}") for i in range(NS)]
        full = [sem(f"bank_full{i}") for i in range(8)]
        free = [sem(f"bank_emptied{i}") for i in range(8)]
        x_loaded = sem("x_loaded")
        c_loaded = sem("c_loaded")
        small_loaded = sem("small_loaded")
        gain_loaded = [sem(f"gain_loaded{i}") for i in range(3)]
        bias_loaded = [sem(f"bias_loaded{i}") for i in range(4)]
        acc_cleared = sem("acc_cleared")
        zeroed = sem("zeroed")
        acc_done = sem("ada_chunk_summed")
        cond_sig = sem("cond_sigmoid")
        angles = sem("angles_reduced")
        tables = sem("rope_tables")
        ss_done = sem("square_sums")
        var_done = sem("variances")
        guess_done = sem("rstd_guess")
        xn_done = sem("x_normed")
        qi_ready = sem("indexer_ready")
        lat_ready = sem("latent_normed")
        q_ready = sem("q_and_k_rope_ready")
        stick_abs = sem("stick_abs")
        stick_log = sem("stick_log")
        stick_sp = sem("stick_softplus")
        stick_av = sem("stick_av")
        gates_done = sem("gates_done")
        max_done = sem("neg_max")
        exp_done = sem("exp_done")
        prob_done = sem("prob_done")
        merged = sem("merged")
        out_used = sem("out_rows_used")
        x_added = sem("x_added")
        acc0 = sem("expert_sum_cleared")
        sig_done = sem("sigmoid_done")
        gate_prod = sem("gate_product")
        down_used = sem("down_rows_used")
        route_d = sem("route_difference")
        route_e = sem("route_exp")
        picked_done = sem("picked")
        sel_ready = sem("selection_ready")
        sel_turned = sem("selection_turned")
        selT_ready = sem("turned_selection_ready")
        gathered = sem("tokens_gathered")
        xg_ready = sem("gathered_tokens_ready")
        gu_used = sem("gate_and_up_weights_used")
        few_sig = sem("few_sigmoid")
        few_prod = sem("few_gate_product")
        few_hid = sem("few_hidden")
        few_turned = sem("few_hidden_turned")
        few_hidT = sem("few_turned_hidden_ready")
        few_sum = sem("few_down_products")
        few_yg = sem("few_result_ready")
        v_chain = sem("vector_chain")
        a_chain = sem("scalar_chain")
        stored = sem("stored")

        block = ctx.enter_context(nc.Block())

        def slot(key):
            return load_number(key) % NS

        def wait_loaded(eng, key, turn=0):
            n = load_number(key)
            eng.wait_ge(loaded[n % NS], turn * 16 + 16 * (n // NS + 1))

        def wait_full(eng, *key):
            eng.wait_ge(full[BANK[key]], ORD[key] + 1)

        def wait_free(eng, *key):
            if ORD[key]:
                eng.wait_ge(free[BANK[key]], ORD[key])

        def wait_read(eng, *key):
            eng.wait_ge(free[BANK[key]], ORD[key] + 1)

        def bank(*key):
            return ps[:, BANK[key], :]

        def full_of(*key):
            return full[BANK[key]]

        def free_of(*key):
            return free[BANK[key]]

        def ada_index(l, a):
            return l * NADA + a

        GTG = {(0, 2): 0, (0, 5): 1, (1, 2): 0, (1, 5): 2}
        ROWS = {(0, 2): 1, (0, 5): 1, (1, 2): 2, (1, 5): 1}
        LOGIT_ORDER = (0, 2, 4, 1, 3, 5)

        def logit_place(t, i):
            nk = P * (t + 1)
            if t == 0:
                return 4 + i // 3, (i % 3) * nk, i % 3 == 2
            return 4 + 2 * (i // 3) + (i % 3) // 2, (i % 3 % 2) * nk, i % 3 != 0

        def wait_released(eng, key):
            kind, l, j = key
            if kind == "ada":
                eng.wait_ge(acc_done, ada_index(l, j) + 1)
            elif kind == "in":
                wait_full(eng, "in", l, j)
            elif kind == "br":
                wait_full(eng, "br", l, 3, (4, 4, 5, 6)[j])
            elif kind == "out":
                if j < 3:
                    eng.wait_ge(out_used, 3 * l + j + 1)
                else:
                    wait_full(eng, "y", l, 3)
            elif kind == "down":
                if j < NCH - 1:
                    eng.wait_ge(down_used, l * (FT - 1) + 2 * j + 2)
                else:
                    wait_full(eng, "down", l, 3)
            else:
                wait_full(eng, "gu", l, min(2 * j + 1, FT - 1))

        def wait_released_moe(eng, kind, ch, e):
            if kind != "down":
                eng.wait_ge(gu_used, e * NCH + ch + 1)
            elif ch < NCH - 1:
                eng.wait_ge(down_used, e * (NCH - 1) + DENSE_UNITS * (FT - 1) + ch + 1)
            else:
                eng.wait_ge(full[7], e + MOE_FIRST[7] + 1)

        def relu_at(t, par):
            nk = P * (t + 1)
            m = multi[:, :, :].rearrange("p a b -> p (a b)")
            at = par * 2 * nk if t == 0 else 512 + par * 2 * nk
            return m[:, at:at + 2 * nk]

        FEW = {"tensor": [(few_turned, NCH), (few_sum, 2)],
               "scalar": [(few_sig, NCH), (few_hidT, NCH)],
               "vector": [(few_prod, NCH), (few_hid, NCH), (few_yg, 2)]}
        MANY = {"tensor": [(full[b], GU_PER[b]) for b in range(3)],
                "scalar": [(sig_done, FT)],
                "vector": [(free[b], GU_PER[b]) for b in range(3)] + [(gate_prod, FT)]}

        def stand_in(eng, signals):
            for s, n in signals:
                eng.sem_inc(s, n)

        def has_many(eng, e):
            return eng.value_load(tokens_of[0:1, bass.ds(e, 1)], min_val=0, max_val=T) > P

        small = [(cst[:, :], consts), (pos_i[:, :], positions[0].rearrange("(t p) -> p t", p=P))]
        for l in range(DEPTH):
            for n in range(2):
                small.append((gcol[:, l, n, :], norm_gains[l, 2 * n].rearrange("(k p) -> p k", p=P)))
            small.append((glat[:, l:l + 1], g_kv_latent[l].rearrange("(p a) -> p a", a=1)))
            small.append((pscale[:, l, :], pool_scale[l].rearrange("(k p) -> p k", p=P)))
            small.append((wukv[:, l, 0:NOPE], w_uk[l]))
            small.append((wukv[:, l, NOPE:NOPE + HEAD], w_uv[l]))
            for g in range(4):
                r = slice(HEAD * (g % 2), HEAD * (g % 2) + HEAD)
                small.append((wpool[r, l, g // 2, r], w_pool[l, g]))
        small.append((wroute[:, :, :], w_router[0].rearrange("(k p) e -> p k e", p=P)))
        SMALL = 16 * len(small)

        @block.sync
        def _(sp):
            def place(s, w, n=KD):
                return ring[:, s, 0:n * w].rearrange("p (k n) -> p k n", k=n)

            def columns(s, matrix, c0, w):
                return sp.dma_start(place(s, w), matrix[:, c0:c0 + w].rearrange("(k p) n -> p k n", p=P))

            def rows(s, matrix, r0, n):
                return sp.dma_start(place(s, D, n), matrix[r0:r0 + n * P, :].rearrange("(k p) n -> p k n", p=P))

            for n, key in enumerate(LOADS):
                s = n % NS
                if n >= NS:
                    wait_released(sp, LOADS[n - NS])
                kind, l, j = key
                if kind == "ada":
                    d = columns(s, w_ada[l], 256 * j, 256)
                elif kind == "in":
                    d = columns(s, w_in[l], *W_IN_SLOTS[j])
                elif kind == "br":
                    m, r0, k = [(w_br_a, 0, 2), (w_br_a, 2 * P, 1), (w_br_b, 0, 2), (w_br_c, 0, 2)][j]
                    d = rows(s, m[l], r0, k)
                elif kind == "out":
                    d = rows(s, w_out[l], 2 * P * j, 2)
                elif kind == "down":
                    c0, w = F_CHUNKS[j]
                    d = rows(s, w_down_dense[0], FE * l + c0, w // P)
                else:
                    c0, w = F_CHUNKS[j]
                    d = columns(s, (w_gate_dense if kind == "gate" else w_up_dense)[0], FE * l + c0, w)
                d.then_inc(loaded[s], 16)

            def expert_load(i, e):
                ch, kind = i // 3, KINDS[i % 3]
                c0, w = F_CHUNKS[ch]
                s = slot((kind, "moe", ch))
                if kind == "down":
                    src = w_down_moe[0].rearrange("e f n -> (e f) n")[bass.ds(e * FE + c0, w), :]
                    dst = place(s, D, w // P)
                else:
                    m = w_gate_moe if kind == "gate" else w_up_moe
                    src = m[0].rearrange("e d f -> (e d) f")[bass.ds(e * D, D), c0:c0 + w]
                    dst = place(s, w)
                sp.dma_start(dst, src.rearrange("(k p) n -> p k n", p=P)).then_inc(loaded[s], 16)

            for i in range(NS):
                wait_released(sp, LOADS[EXPERT0 + i - NS])
                expert_load(i, 0)
            with sp.Fori(0, E - 1) as e:
                for i in range(NS, UNIT):
                    wait_released_moe(sp, KINDS[(i - NS) % 3], (i - NS) // 3, e)
                    expert_load(i, e)
                for i in range(NS):
                    wait_released_moe(sp, KINDS[(i + NS) % 3], (i + NS) // 3, e)
                    expert_load(i, e + 1)
            for i in range(NS, UNIT):
                wait_released_moe(sp, KINDS[(i - NS) % 3], (i - NS) // 3, E - 1)
                expert_load(i, E - 1)

            for t in range(TT):
                sp.wait_ge(x_added, TT * (2 * DEPTH - 1) + t + 1)
                sp.dma_start(out[0, t * P:(t + 1) * P, :], x[:, t, :]).then_inc(stored, 16)
            sp.wait_ge(stored, 16 * TT)

        @block.gpsimd
        def _(pool):
            pool.dma_start(c_col[:, :], c[0].rearrange("(k p) -> p k", p=P), allow_slow_non_contiguous=True).then_inc(c_loaded, 16)
            pool.dma_start(x[:, :, :], x_in[0].rearrange("(t p) d -> p t d", p=P)).then_inc(x_loaded, 16)
            pool.memset(wpool[:, :, :, :], 0.0).then_inc(zeroed, 1)
            pool.memset(comb[:, :, :], 1.0).then_inc(zeroed, 1)
            pool.wait_ge(zeroed, 2)
            for dst, src in small:
                pool.dma_start(dst, src, allow_slow_non_contiguous=True).then_inc(small_loaded, 16)

            def gain_row(l, seg):
                b = GTG[(l, seg)]
                row = norm_gains[l, 1 if seg == 2 else 3]
                pool.dma_start(gtg[:, b, :], row.rearrange("(a n) -> a n", a=1).to_broadcast([P, D])).then_inc(gain_loaded[b], 16)

            def clear_expert_sum(l):
                pool.wait_ge(merged, 4 * l + 4)
                pool.memset(yacc, 0.0).then_inc(acc0, 1)

            for l in range(DEPTH):
                if l == 1:
                    clear_expert_sum(0)
                    pool.wait_ge(x_added, TT)
                    gain_row(1, 2)
                for a in range(NADA):
                    n = ada_index(l, a)
                    if n >= 4:
                        wait_full(pool, "ada", (n - 4) // NADA, (n - 4) % NADA)
                    pool.memset(acc[:, n % 4, :], 0.0).then_inc(acc_cleared, 1)
                    pool.wait_ge(acc_cleared, n + 1)
                    pool.dma_start(acc[0:1, n % 4, :], b_ada[l:l + 1, 256 * a:256 * a + 256]).then_inc(bias_loaded[n % 4], 16)
                    if n == 3:
                        gain_row(0, 2)
                        gain_row(0, 5)
                        gain_row(1, 5)
            clear_expert_sum(1)

        @block.tensor
        def _(pe):
            def mm(o, a, b, start, stop, **kw):
                return pe.matmul(o, a, b, start=start, stop=stop, **kw)

            def w_tile(key, w, n=KD):
                return ring[:, slot(key), 0:n * w].rearrange("p (k n) -> p k n", k=n)

            def half_rows(h):
                return slice(HEAD * (h % 2), HEAD * (h % 2) + HEAD)

            def ada_product(l, a):
                n = ada_index(l, a)
                pe.wait_ge(acc_done, n + 1)
                wait_free(pe, "ada", l, a)
                b = bank("ada", l, a)
                if a // 4 in (2, 5):
                    last = mm(b[:, 0:256], ones, acc[:, n % 4, :], True, True)
                else:
                    for m in range(2):
                        last = mm(b[:, m:m + 1], acc[:, n % 4, m * P:(m + 1) * P], ones[:, 0:1], True, True)
                last.then_inc(full_of("ada", l, a), 1)

            def transpose_x(name, l):
                for j in range(4):
                    wait_free(pe, name, l, j)
                    for i in range(4):
                        k, t = 2 * j + i // 2, i % 2
                        last = pe.transpose(bank(name, l, j)[:, i * P:(i + 1) * P], xn[:, t, k * P:(k + 1) * P], ident)
                    last.then_inc(full_of(name, l, j), 1)
                for j in range(4):
                    wait_read(pe, name, l, j)

            def transposes(l):
                groups = [[natP[:, t, C_QI + P * h:C_QI + P * (h + 1)] for h in range(2) for t in range(TT)],
                          [ki[:, t, :] for t in range(TT)] + [latn[:, t, :] for t in range(TT)],
                          [natP[:, t, P * h:P * (h + 1)] for h in range(2) for t in range(TT)],
                          [natP[:, t, 2 * P:3 * P] for t in range(TT)]]
                ready = [qi_ready, lat_ready, q_ready, q_ready]
                for n, group in enumerate(groups):
                    pe.wait_ge(ready[n], l + 1)
                    wait_free(pe, "tr", l, n)
                    for i, src in enumerate(group):
                        last = pe.transpose(bank("tr", l, n)[:, i * P:(i + 1) * P], src, ident)
                    last.then_inc(full_of("tr", l, n), 1)

            def indexer(l):
                wait_read(pe, "tr", l, 0)
                wait_read(pe, "tr", l, 1)
                keys = trs[:, 4:6, :].rearrange("p a b -> p (a b)")
                for t in range(TT):
                    nk = P * (t + 1)
                    for par in range(2):
                        wait_free(pe, "idx", l, t, par)
                        r = half_rows(par)
                        for h in range(2):
                            last = mm(bank("idx", l, t, par)[:, h * nk:(h + 1) * nk], trs[r, 2 * h + t, :], keys[r, 0:nk], True, True)
                        last.then_inc(full_of("idx", l, t, par), 1)

            def latent_and_pool(l):
                wait_free(pe, "ukv", l)
                for t in range(TT):
                    last = mm(bank("ukv", l)[:, t * P:t * P + NOPE + HEAD], trs[:, 6 + t, :], wukv[:, l, :], True, True)
                last.then_inc(full_of("ukv", l), 1)
                wait_read(pe, "in", l, 4)
                wait_free(pe, "pool", l)
                for g in range(4):
                    for s in range(TT):
                        last = mm(bank("pool", l)[half_rows(g), (g // 2) * T:(g // 2 + 1) * T],
                                  natP[:, s, C_U + HEAD * g:C_U + HEAD * (g + 1)], const(f"band{s}{g}"), s == 0, s == 1)
                last.then_inc(full_of("pool", l), 1)
                wait_read(pe, "ukv", l)
                wait_free(pe, "kT", l)
                for t in range(TT):
                    last = pe.transpose(bank("kT", l)[:, t * P:(t + 1) * P], kn[:, t, :], ident)
                last.then_inc(full_of("kT", l), 1)
                wait_read(pe, "pool", l)
                wait_free(pe, "yb", l)
                for g in range(2):
                    last = mm(bank("yb", l)[:, g * T:(g + 1) * T], wpool[:, l, g, :], poolT[:, g, :], True, True)
                last.then_inc(full_of("yb", l), 1)

            def stick_logits(l, h):
                if h == 0:
                    wait_read(pe, "in", l, 5)
                    wait_read(pe, "in", l, 6)
                    wait_read(pe, "in", l, 7)
                wait_free(pe, "stick", l, h)
                b, r, ft = bank("stick", l, h), half_rows(h), h // 2
                mm(b[:, 0:T], qkc[r, 2 + ft, 0:P], qkc[r, ft, :], True, False, skip_group_check=True)
                mm(b[:, T:T + P], qkc[r, 2 + ft, P:T], qkc[r, ft, P:T], False, False, skip_group_check=True)
                mm(b[:, 0:P], ident, const("before"), False, False, skip_group_check=True)
                mm(b[:, T:T + P], ident, const("before"), False, True, skip_group_check=True).then_inc(full_of("stick", l, h), 1)

            def stick_sums(l, h):
                pe.wait_ge(stick_sp, HC * l + h + 1)
                wait_free(pe, "stick2", l, h)
                b, s = bank("stick2", l, h), spl[:, h % 2, :]
                mm(b[:, 0:T], const("neg_from"), s[:, 0:T], False, False, skip_group_check=True)
                mm(b[:, P:T], const("neg_ones"), s[:, T:T + P], False, False, skip_group_check=True)
                mm(b[:, T:T + P], const("neg_from"), s[:, T:T + P], False, True, skip_group_check=True).then_inc(full_of("stick2", l, h), 1)

            def stick_values(l, h):
                wait_read(pe, "stick2", l, h)
                key = ("yc", l, h // 2)
                if h % 2 == 0:
                    wait_free(pe, *key)
                o, a = bank(*key)[half_rows(h), :], aT[:, h % 2, :]
                mm(o[:, 0:T], vc[:, 0, h * HEAD:(h + 1) * HEAD], a[:, 0:T], True, False, skip_group_check=True)
                last = mm(o[:, P:T], vc[:, 1, h * HEAD:(h + 1) * HEAD], a[:, T:T + P], False, True, skip_group_check=True)
                last.then_inc(stick_av if h % 2 == 0 else full_of(*key), 1)

            def softmax_head_products(l, t):
                nk = P * (t + 1)
                if t == 0:
                    wait_read(pe, "tr", l, 2)
                    wait_read(pe, "tr", l, 3)
                    wait_read(pe, "kT", l)
                for i, h in enumerate(LOGIT_ORDER):
                    b, at, ends = logit_place(t, i)
                    if at == 0:
                        wait_free(pe, "logit", l, t, b)
                    r = half_rows(h)
                    last = mm(ps[:, b, at:at + nk], qT[r, h // 2, t * P:(t + 1) * P], kT[r, 0:nk], True, True)
                    if ends:
                        last.then_inc(full[b], 1)
                for kt in range(t + 1):
                    for b in (0, 1):
                        if kt == 0:
                            pe.wait_ge(prob_done, 2 * (TT * l + t) + b + 1)
                        wait_free(pe, "pT", l, t, kt, b)
                        for i in range(3):
                            at = (3 * b + i) * nk + kt * P
                            last = pe.transpose(ps[:, b, i * P:(i + 1) * P], lg[:, at:at + P], ident)
                        last.then_inc(full[b], 1)
                wait_free(pe, "av", l, t)
                for b in (0, 1):
                    wait_read(pe, "pT", l, t, t, b)
                for i, h in enumerate(LOGIT_ORDER):
                    for kt in range(t + 1):
                        last = mm(bank("av", l, t)[half_rows(h), (h // 2) * P:(h // 2 + 1) * P],
                                  va[:, kt, :], pT[:, kt, i * P:(i + 1) * P], kt == 0, kt == t)
                last.then_inc(full_of("av", l, t), 1)

            def unit(name, e, turn):
                moe = name == "moe"

                def down(f):
                    ch, r = f // 2, f % 2
                    if r == 0:
                        wait_loaded(pe, ("down", name, ch), turn)
                    if moe:
                        pe.wait_ge(free[f % 3], e * GU_PER[f % 3] + MOE_FIRST[f % 3] + f // 3 + 1)
                    else:
                        wait_read(pe, "gu", name, f)
                    if f == 0:
                        for b in range(4):
                            if moe:
                                pe.wait_ge(free[4 + b], e + MOE_FIRST[4 + b])
                            else:
                                wait_free(pe, "down", name, b)
                    w = w_tile(("down", name, ch), D, F_CHUNKS[ch][1] // P)
                    for b in range(4):
                        t, half = b // 2, b % 2
                        last = mm(ps[:, 4 + b, :], hid[:, f % 2, t * P:(t + 1) * P],
                                  w[:, r, half * 512:(half + 1) * 512], f == 0, f == FT - 1)
                        if f == FT - 1:
                            last.then_inc(full[4 + b], 1)
                        elif moe and b == 0 and (r == 0 or f == FT - 2):
                            last.then_inc(gu_used, 1)
                    if f < FT - 1 and (r == 1 or not moe):
                        last.then_inc(down_used, 1)

                for f in range(FT):
                    ch, r, b = f // 2, f % 2, f % 3
                    if r == 0:
                        wait_loaded(pe, ("gate", name, ch), turn)
                        wait_loaded(pe, ("up", name, ch), turn)
                    if moe:
                        pe.wait_ge(free[b], e * GU_PER[b] + MOE_FIRST[b] + f // 3)
                    else:
                        wait_free(pe, "gu", name, f)
                    for half, kind in enumerate(("gate", "up")):
                        w = w_tile((kind, name, ch), F_CHUNKS[ch][1])
                        for k in range(KD):
                            last = mm(ps[:, b, half * T:(half + 1) * T], w[:, k, r * P:(r + 1) * P], hT[:, k, :], k == 0, k == KD - 1)
                    last.then_inc(full[b], 1)
                    if f > 0:
                        down(f - 1)
                    if not moe:
                        for a in ADA_AFTER.get(name * FT + f - 1, ()):
                            ada_product(1, a)
                down(FT - 1)

            def gather(e):
                pe.wait_ge(sel_ready, e + 1)
                for k in range(KD):
                    for t in range(TT):
                        last = mm(ps[:, k // 4, (k % 4) * P:(k % 4 + 1) * P], xn[:, t, k * P:(k + 1) * P], sel[:, t, :], t == 0, t == 1)
                last.then_inc(gathered, 1)

            def few_tokens(e, turn):
                def gate_up(ch):
                    w = F_CHUNKS[ch][1]
                    for half, kind in enumerate(("gate", "up")):
                        wait_loaded(pe, (kind, "moe", ch), turn)
                        wt = w_tile((kind, "moe", ch), w)
                        for k in range(KD):
                            last = mm(ps[:, ch % 2, half * 256:half * 256 + w], xg[:, k, :], wt[:, k, :], k == 0, k == KD - 1)
                    last.then_inc(gu_used, 1)

                def turn_hidden(ch):
                    pe.wait_ge(few_hid, e * NCH + ch + 1)
                    for r in range(F_CHUNKS[ch][1] // P):
                        last = pe.transpose(ps[:, 2, (2 * (ch % 2) + r) * P:(2 * (ch % 2) + r + 1) * P], hid[:, ch % 2, r * P:(r + 1) * P], ident)
                    last.then_inc(few_turned, 1)

                def down(ch):
                    n = F_CHUNKS[ch][1] // P
                    wait_loaded(pe, ("down", "moe", ch), turn)
                    w = w_tile(("down", "moe", ch), D, n)
                    pe.wait_ge(few_hidT, e * NCH + ch + 1)
                    if ch == 0:
                        pe.wait_ge(free[7], e + MOE_FIRST[7])
                    for half, b in enumerate((3, 7)):
                        for r in range(n):
                            last = mm(ps[:, b, :], hidT[:, ch % 2, r, :], w[:, r, half * 512:(half + 1) * 512],
                                      ch == 0 and r == 0, ch == NCH - 1 and r == n - 1)
                        if ch == NCH - 1:
                            last.then_inc(few_sum, 1)
                    if ch < NCH - 1:
                        last.then_inc(down_used, 1)

                for ch in range(NCH):
                    gate_up(ch)
                    if ch > 1:
                        down(ch - 2)
                    if ch > 0:
                        turn_hidden(ch - 1)
                down(NCH - 2)
                turn_hidden(NCH - 1)
                gather(e + 1)
                down(NCH - 1)
                for half in range(2):
                    pe.wait_ge(few_yg, 2 * e + half + 1)
                    for t in range(TT):
                        b = 4 + 2 * t + half
                        pe.wait_ge(free[b], e + MOE_FIRST[b])
                        mm(ps[:, b, :], selT[:, t * P:(t + 1) * P], yg[:, half * 512:(half + 1) * 512], True, True).then_inc(full[b], 1)
                stand_in(pe, MANY["tensor"])

            pe.wait_ge(small_loaded, SMALL)
            for l in range(DEPTH):
                if l == 0:
                    for a in range(8):
                        ada_product(0, a)
                pe.wait_ge(xn_done, 4 * l + 2)
                transpose_x("xT", l)
                for j, (c0, w) in enumerate(W_IN_SLOTS):
                    wait_loaded(pe, ("in", l, j))
                    wait_free(pe, "in", l, j)
                    wt, b = w_tile(("in", l, j), w), bank("in", l, j)
                    for m in range(2):
                        for k in range(KD):
                            if j <= 4 or j == 7:
                                last = mm(b[:, m * 256:m * 256 + w], hT[:, k, m * P:(m + 1) * P], wt[:, k, :], k == 0, k == KD - 1)
                            else:
                                last = mm(b[:, m * T:(m + 1) * T], wt[:, k, m * P:(m + 1) * P], hT[:, k, :], k == 0, k == KD - 1)
                    last.then_inc(full_of("in", l, j), 1)
                    if l == 0:
                        for a in ada_beside(j - 1):
                            ada_product(0, a)
                    if j == 7:
                        transposes(l)
                    if j == 9:
                        indexer(l)
                    if j == 10:
                        latent_and_pool(l)
                    if 13 <= j < 13 + HC:
                        stick_values(l, j - 13)
                    if 12 <= j < 12 + HC:
                        stick_sums(l, j - 12)
                    if 11 <= j < 11 + HC:
                        stick_logits(l, j - 11)
                if l == 0:
                    for a in ada_beside(NIN - 1):
                        ada_product(0, a)
                for t in range(TT):
                    softmax_head_products(l, t)

                for j in range(4):
                    wait_loaded(pe, ("br", l, j))
                wait_read(pe, "yb", l)
                wait_read(pe, "yc", l, 1)
                for t in range(TT):
                    wait_read(pe, "av", l, t)
                branch = {4: [(("br", l, 0), 2, 0, yaT[:, 0, :]), (("br", l, 0), 2, 1, yaT[:, 1, :]), (("br", l, 1), 1, 0, yaT[:, 2, :])],
                          5: [(("br", l, 2), 2, k, ybT[:, k, :]) for k in range(2)],
                          6: [(("br", l, 3), 2, k, ycT[:, k, :]) for k in range(2)]}
                for m in range(4):
                    for b, parts in branch.items():
                        wait_free(pe, "br", l, m, b)
                        for half in range(2):
                            d0 = (2 * m + half) * P
                            for i, (key, n, k, y) in enumerate(parts):
                                last = mm(ps[:, b, half * T:(half + 1) * T], w_tile(key, D, n)[:, k, d0:d0 + P], y,
                                          i == 0, i == len(parts) - 1)
                        last.then_inc(full[b], 1)
                for b in range(4):
                    wait_free(pe, "y", l, b)
                for j in range(4):
                    wait_loaded(pe, ("out", l, j))
                    pe.wait_ge(merged, 4 * l + j + 1)
                    for b in range(4):
                        t, half = b // 2, b % 2
                        for k in range(2):
                            last = mm(ps[:, b, :], hT[:, 2 * j + k, t * P:(t + 1) * P],
                                      w_tile(("out", l, j), D, 2)[:, k, half * 512:(half + 1) * 512],
                                      j == 0 and k == 0, j == 3 and k == 1)
                        if j == 3:
                            last.then_inc(full[b], 1)
                    if j < 3:
                        last.then_inc(out_used, 1)

                pe.wait_ge(xn_done, 4 * l + 4)
                transpose_x("hT", l)
                if l == 0:
                    for u in range(DENSE_UNITS):
                        unit(u, u, 0)
                    for a in ADA_AFTER.get(DENSE_UNITS * FT - 1, ()):
                        ada_product(1, a)
                else:
                    wait_free(pe, "route", l)
                    for t in range(TT):
                        for k in range(KD):
                            last = mm(bank("route", l)[:, t * E:(t + 1) * E], hT[:, k, t * P:(t + 1) * P], wroute[:, k, :], k == 0, k == KD - 1)
                    last.then_inc(full_of("route", l), 1)
                    pe.wait_ge(picked_done, 1)
                    o = bank("count", l)
                    for t in range(TT):
                        if t == 1:
                            mm(o[:, E:2 * E], ones, picked[:, 0, :], True, False)
                        mm(o[:, t * E:(t + 1) * E], const("earlier"), picked[:, t, :], t == 0, True)
                    for t in range(TT):
                        last = mm(o[:, 2 * E:3 * E], ones, picked[:, t, :], t == 0, t == 1)
                    last.then_inc(full_of("count", l), 1)
                    gather(0)
                    wait_read(pe, "count", 1)
                    with pe.Fori(0, E) as e:
                        pe.wait_ge(xg_ready, e + 1)
                        for t in range(TT):
                            last = pe.transpose(ps[:, 3, t * P:(t + 1) * P], sel[:, t, :], ident)
                        last.then_inc(sel_turned, 1)
                        pe.wait_ge(selT_ready, e + 1)
                        with pe.If(has_many(pe, e)):
                            unit("moe", e, e * TURNS)
                            gather(e + 1)
                            stand_in(pe, FEW["tensor"])
                        with pe.Else():
                            few_tokens(e, e * TURNS)

        @block.scalar
        def _(act):
            chain = [0]

            def link(ins):
                chain[0] += 1
                ins.then_inc(a_chain, 1)
                act.wait_ge(a_chain, chain[0])

            def squares(n, t, src, junk):
                act.activation(junk, src, ACT.Square, accum_out=ss[:, n, t:t + 1]).then_inc(ss_done, 1)

            def guess_rstd(n):
                act.wait_ge(var_done, n + 1)
                link(act.activation(guess[:, n, :], var[:, n, :], ACT.Ln))
                act.activation(guess[:, n, :], guess[:, n, :], ACT.Exp, scale=-0.5).then_inc(guess_done, 1)

            def modulate(name, l, which):
                for j in (1, 3):
                    wait_full(act, name, l, j)
                    for m in range(2):
                        k = 2 * j + m
                        last = act.activation(hT[:, k, :], bank(name, l, j)[:, m * T:(m + 1) * T], ACT.Identity,
                                              scale=modc[:, l, 2 * which + 1, k:k + 1], bias=modc[:, l, 2 * which, k:k + 1])
                    last.then_inc(free_of(name, l, j), 1)

            def copy_out(key, dst, src, scale=1.0):
                wait_full(act, *key)
                act.activation(dst, src, ACT.Copy, scale=scale).then_inc(free_of(*key), 1)

            def pairs(b, w=256, n=2, step=256):
                return b[:, 0:n * step].rearrange("p (m n) -> p m n", m=n)[:, :, 0:w]

            act.wait_ge(c_loaded, 16)
            act.activation(cond[:, :], c_col[:, :], ACT.Sigmoid).then_inc(cond_sig, 1)
            act.wait_ge(angles, 1)
            act.activation(cs[:, :, :, :], red[:, :, :, :], ACT.Sin).then_inc(tables, 1)
            for l in range(DEPTH):
                if l == 0:
                    act.wait_ge(x_loaded, 16)
                for t in range(TT):
                    if l > 0:
                        act.wait_ge(x_added, TT * (2 * l - 1) + t + 1)
                    squares(5 * l, t, x[:, t, :], xn[:, t, :])
                guess_rstd(5 * l)
                for a in range(8):
                    wait_read(act, "ada", l, a)
                modulate("xT", l, 0)
                for j in range(20):
                    key = ("in", l, j)
                    b = bank(*key)
                    if j < 5:
                        c0, w = W_IN_SLOTS[j]
                        copy_out(key, natP[:, :, c0:c0 + w], pairs(b, w))
                        if j == 1:
                            act.wait_ge(free_of(*key), ORD[key] + 1)
                            for t in range(TT):
                                squares(5 * l + 1, t, natP[:, t, C_LAT:C_LAT + LAT], latn[:, t, :])
                            guess_rstd(5 * l + 1)
                    elif j == 5:
                        copy_out(key, qkc[:, 0:2, :], pairs(b), HEAD ** -0.5)
                    elif j == 6:
                        copy_out(key, qkc[:, 2:4, :], pairs(b))
                    elif j == 7:
                        copy_out(key, vc[:, :, :], pairs(b))
                    else:
                        copy_out(key, gT[:, 2 * (j - 8):2 * (j - 8) + 2, :], pairs(b))
                    if j == 7:
                        copy_out(("tr", l, 0), trs[:, 0:4, :], pairs(bank("tr", l, 0), P, 4, P))
                        wait_full(act, "tr", l, 1)
                        act.activation(trs[:, 4:6, :], pairs(bank("tr", l, 1), P, 2, P), ACT.Copy)
                        act.activation(trs[:, 6:8, :], pairs(bank("tr", l, 1)[:, T:], P, 2, P), ACT.Copy,
                                       scale=glat[:, l:l + 1]).then_inc(free_of("tr", l, 1), 1)
                        copy_out(("tr", l, 2), qT[:, 0:2, :], pairs(bank("tr", l, 2)))
                        copy_out(("tr", l, 3), qT[:, 2, :], bank("tr", l, 3)[:, 0:T])
                    if j == 9:
                        for t in range(TT):
                            nk = P * (t + 1)
                            for par in range(2):
                                wait_full(act, "idx", l, t, par)
                                act.activation(relu_at(t, par), bank("idx", l, t, par)[:, 0:2 * nk], ACT.Relu)\
                                   .then_inc(free_of("idx", l, t, par), 1)
                    if j == 10:
                        wait_full(act, "ukv", l)
                        u = pairs(bank("ukv", l), NOPE + HEAD, 2, P)
                        act.wait_ge(q_ready, l + 1)
                        act.activation(kn[:, :, ROPE:HEAD], u[:, :, 0:NOPE], ACT.Copy)
                        act.activation(kn[:, :, HEAD + ROPE:P], u[:, :, 0:NOPE], ACT.Copy)
                        act.activation(va[:, :, :], u[:, :, NOPE:NOPE + HEAD], ACT.Copy).then_inc(free_of("ukv", l), 1)
                        copy_out(("pool", l), poolT[:, :, :], pairs(bank("pool", l)))
                        copy_out(("kT", l), kT[:, :], bank("kT", l)[:, 0:T])
                        wait_full(act, "yb", l)
                        for g in range(2):
                            last = act.activation(ybT[:, g, :], bank("yb", l)[:, g * T:(g + 1) * T], ACT.Copy, scale=pscale[:, l, g:g + 1])
                        last.then_inc(free_of("yb", l), 1)
                    if 12 <= j < 12 + HC:
                        h = j - 12
                        wait_full(act, "stick2", l, h)
                        act.activation(aT[:, h % 2, :], bank("stick2", l, h)[:, 0:384], ACT.Exp).then_inc(free_of("stick2", l, h), 1)
                    if 11 <= j < 11 + HC:
                        h = j - 11
                        wait_full(act, "stick", l, h)
                        s = spl[:, h % 2, :]
                        act.activation(s, bank("stick", l, h)[:, 0:384], ACT.Abs).then_inc(stick_abs, 1)
                        act.wait_ge(stick_abs, HC * l + h + 1)
                        link(act.activation(s, s, ACT.Exp, scale=-1.0))
                        act.activation(s, s, ACT.Ln, bias=1.0).then_inc(stick_log, 1)
                wait_read(act, "in", l, NIN - 1)
                act.activation(big[:, :], big[:, :], ACT.Sigmoid).then_inc(gates_done, 1)
                for t in range(TT):
                    nk = P * (t + 1)
                    act.wait_ge(max_done, TT * l + t + 1)
                    for i in range(HA):
                        s = lg[:, i * nk:(i + 1) * nk]
                        last = act.activation(s, s, ACT.Exp, bias=nmax[:, l, t, i:i + 1], accum_out=psum_exp[:, l, t, i:i + 1])
                    last.then_inc(exp_done, 1)
                    for kt in range(t + 1):
                        copy_out(("pT", l, t, kt, 1), pT[:, kt, 3 * P:6 * P], bank("pT", l, t, kt, 1)[:, 0:3 * P])
                    copy_out(("av", l, t), yaT[:, :, t * P:(t + 1) * P], pairs(bank("av", l, t), P, 3, P))
                for t in range(TT):
                    wait_full(act, "y", l, 2 * t)
                    wait_full(act, "y", l, 2 * t + 1)
                    squares(5 * l + 2, t, ps[:, 2 * t:2 * t + 2, :].rearrange("p a b -> p (a b)"), xn[:, t, :])
                guess_rstd(5 * l + 2)
                for t in range(TT):
                    act.wait_ge(x_added, TT * 2 * l + t + 1)
                    squares(5 * l + 3, t, x[:, t, :], xn[:, t, :])
                guess_rstd(5 * l + 3)
                for a in range(12, 20):
                    wait_read(act, "ada", l, a)
                modulate("hT", l, 1)
                if l == 0:
                    for u in range(DENSE_UNITS):
                        for f in range(FT):
                            wait_full(act, "gu", u, f)
                            act.activation(sig[:, f % 2, :], bank("gu", u, f)[:, 0:T], ACT.Sigmoid).then_inc(sig_done, 1)
                else:
                    act.wait_ge(route_d, 1)
                    act.activation(rsm[:, 5, 0:TT], rsm[:, 4, 0:TT], ACT.Exp).then_inc(route_e, 1)

                    def modulate_gathered(e):
                        act.wait_ge(gathered, e + 1)
                        for k in range(KD):
                            last = act.activation(xg[:, k, :], ps[:, k // 4, (k % 4) * P:(k % 4 + 1) * P], ACT.Identity,
                                                  scale=modc[:, l, 3, k:k + 1], bias=modc[:, l, 2, k:k + 1])
                        last.then_inc(xg_ready, 1)

                    def turned_hidden(e, ch):
                        act.wait_ge(few_turned, e * NCH + ch + 1)
                        w = F_CHUNKS[ch][1]
                        act.activation(hidT[:, ch % 2, 0:w // P, :].rearrange("p r s -> p (r s)"),
                                       ps[:, 2, 2 * (ch % 2) * P:2 * (ch % 2) * P + w], ACT.Copy).then_inc(few_hidT, 1)

                    modulate_gathered(0)
                    wait_read(act, "count", 1)
                    with act.Fori(0, E) as e:
                        act.wait_ge(sel_turned, e + 1)
                        act.activation(selT, ps[:, 3, 0:T], ACT.Copy).then_inc(selT_ready, 1)
                        with act.If(has_many(act, e)):
                            for f in range(FT):
                                b = f % 3
                                act.wait_ge(full[b], e * GU_PER[b] + MOE_FIRST[b] + f // 3 + 1)
                                act.activation(sig[:, f % 2, :], ps[:, b, 0:T], ACT.Sigmoid).then_inc(sig_done, 1)
                            stand_in(act, FEW["scalar"])
                        with act.Else():
                            for ch in range(NCH):
                                act.wait_ge(gu_used, e * NCH + ch + 1)
                                w = F_CHUNKS[ch][1]
                                act.activation(sig[:, ch % 2, 0:w], ps[:, ch % 2, 0:w], ACT.Sigmoid).then_inc(few_sig, 1)
                                if ch > 0:
                                    turned_hidden(e, ch - 1)
                            turned_hidden(e, NCH - 1)
                            stand_in(act, MANY["scalar"])
                        modulate_gathered(e + 1)
                for t in range(TT):
                    if l == 0:
                        wait_read(act, "down", DENSE_UNITS - 1, 2 * t)
                        wait_read(act, "down", DENSE_UNITS - 1, 2 * t + 1)
                    else:
                        act.wait_ge(free[4 + 2 * t], MOE_FIRST[4 + 2 * t] + E)
                        act.wait_ge(free[5 + 2 * t], MOE_FIRST[5 + 2 * t] + E)
                    squares(5 * l + 4, t, yacc[:, t, :], xn[:, t, :])
                guess_rstd(5 * l + 4)

        @block.vector
        def _(dve):
            chain = [0]

            def link(ins):
                chain[0] += 1
                ins.then_inc(v_chain, 1)
                dve.wait_ge(v_chain, chain[0])

            def finish_rstd(n, width):
                dve.wait_ge(ss_done, TT * (n + 1))
                dve.tensor_scalar(var[:, n, :], ss[:, n, :], 1.0 / width, EPS, ALU.mult, ALU.add).then_inc(var_done, 1)
                dve.wait_ge(guess_done, n + 1)
                g = guess[:, n, :]
                link(dve.tensor_tensor(newt[:, 0, :], g, g, ALU.mult))
                link(dve.tensor_tensor(newt[:, 1, :], newt[:, 0, :], var[:, n, :], ALU.mult))
                link(dve.tensor_scalar(newt[:, 0, :], newt[:, 1, :], -0.5, 1.5, ALU.mult, ALU.add))
                link(dve.tensor_tensor(rstd[:, n, :], g, newt[:, 0, :], ALU.mult))

            def normalize_x(n):
                finish_rstd(n, D)
                for t in range(TT):
                    dve.tensor_scalar(xn[:, t, :], x[:, t, :], rstd[:, n, t:t + 1], None, ALU.mult).then_inc(xn_done, 1)

            def modulate(name, l, which):
                for j in (0, 2):
                    wait_full(dve, name, l, j)
                    for m in range(2):
                        k = 2 * j + m
                        last = dve.tensor_scalar(hT[:, k, :], bank(name, l, j)[:, m * T:(m + 1) * T],
                                                 modc[:, l, 2 * which + 1, k:k + 1], modc[:, l, 2 * which, k:k + 1], ALU.mult, ALU.add)
                    last.then_inc(free_of(name, l, j), 1)

            def ada_sum(l, a):
                n = ada_index(l, a)
                dve.wait_ge(bias_loaded[n % 4], 16 * (n // 4 + 1))
                wait_loaded(dve, ("ada", l, a))
                w = ring[:, slot(("ada", l, a)), :].rearrange("p (k n) -> p k n", k=KD)
                o = acc[:, n % 4, :]
                for k in range(KD):
                    i = dve.scalar_tensor_tensor(out=o, in0=w[:, k, :], scalar=cond[:, k:k + 1], in1=o, op0=ALU.mult, op1=ALU.add)
                    if k < KD - 1:
                        link(i)
                    else:
                        i.then_inc(acc_done, 1)

            def ada_read(l, a):
                seg, q = a // 4, a % 4
                wait_full(dve, "ada", l, a)
                b = bank("ada", l, a)
                if seg in (2, 5):
                    g = GTG[(l, seg)]
                    dve.wait_ge(gain_loaded[g], 16 * ROWS[(l, seg)])
                    r = gtg[:, g, 256 * q:256 * (q + 1)]
                    i = dve.tensor_tensor(r, b[:, 0:256], r, ALU.mult)
                else:
                    which = 0 if seg < 2 else 1
                    scale = seg in (1, 4)
                    o = modc[:, l, 2 * which + scale, 2 * q:2 * q + 2]
                    if scale:
                        i = dve.scalar_tensor_tensor(out=o, in0=b[:, 0:2], scalar=1.0, in1=gcol[:, l, which, 2 * q:2 * q + 2],
                                                     op0=ALU.add, op1=ALU.mult)
                    else:
                        i = dve.tensor_copy(o, b[:, 0:2])
                i.then_inc(free_of("ada", l, a), 1)

            def rope(view, heads):
                def tab(i):
                    return cs[:, :, i:i + 1, :].to_broadcast([P, TT, heads, HALF])
                x1, x2 = view[:, :, :, 0:HALF], view[:, :, :, HALF:ROPE]
                r = [rot[:, i, 0:TT * heads * HALF].rearrange("p (t h c) -> p t h c", t=TT, h=heads) for i in range(4)]
                dve.tensor_tensor(r[0], x1, tab(0), ALU.mult)
                dve.tensor_tensor(r[1], x2, tab(1), ALU.mult)
                dve.tensor_tensor(r[2], x2, tab(0), ALU.mult)
                link(dve.tensor_tensor(r[3], x1, tab(1), ALU.mult))
                dve.tensor_tensor(x1, r[0], r[1], ALU.subtract)
                return dve.tensor_tensor(x2, r[2], r[3], ALU.add)

            def heads_view(c0, n, w=HEAD):
                return natP[:, :, c0:c0 + n * w].rearrange("p t (h c) -> p t h c", h=n)

            def choose(l, t):
                nk = P * (t + 1)
                s, tk = score[:, t, 0:nk], take[:, t, 0:nk]
                for i, h in enumerate((0, 1, 2, 3)):
                    wait_read(dve, "idx", l, t, h % 2)
                    r = relu_at(t, h % 2)[:, (h // 2) * nk:(h // 2 + 1) * nk]
                    w = natP[:, t, C_WI + h:C_WI + h + 1]
                    if i == 0:
                        link(dve.tensor_scalar(s, r, w, None, ALU.mult))
                    else:
                        link(dve.scalar_tensor_tensor(out=s, in0=r, scalar=w, in1=s, op0=ALU.mult, op1=ALU.add))
                diag = score[:, t, nk - P:nk]
                link(dve.tensor_tensor(diag, diag, const("not_causal"), ALU.add))
                for _ in range(TOPK // 8):
                    link(dve.max(top8[:, :], s))
                    link(dve.match_replace(s, top8[:, :], s, TAKEN))
                link(dve.tensor_scalar(tk, s, TAKEN, None, ALU.is_equal))
                diag = take[:, t, nk - P:nk]
                link(dve.tensor_tensor(diag, diag, const("causal"), ALU.mult))
                link(dve.tensor_scalar(tk, tk, -FAR, FAR, ALU.mult, ALU.add))

            def stick(l, h):
                dve.wait_ge(stick_abs, HC * l + h + 1)
                r, s = rel[:, h % 2, :], spl[:, h % 2, :]
                dve.tensor_scalar(r, bank("stick", l, h)[:, 0:384], 0.0, None, ALU.max).then_inc(free_of("stick", l, h), 1)
                dve.wait_ge(free_of("stick", l, h), ORD[("stick", l, h)] + 1)
                dve.wait_ge(stick_log, HC * l + h + 1)
                dve.tensor_tensor(s, r, s, ALU.add).then_inc(stick_sp, 1)

            def softmax(l, t):
                nk = P * (t + 1)
                for b in ([4, 5] if t == 0 else [4, 5, 6, 7]):
                    idx = [i for i in range(HA) if logit_place(t, i)[0] == b]
                    wait_full(dve, "logit", l, t, b)
                    n = len(idx)
                    o = lg[:, idx[0] * nk:(idx[0] + n) * nk].rearrange("p (h k) -> p h k", h=n)
                    i = ps[:, b, 0:n * nk].rearrange("p (h k) -> p h k", h=n)
                    dve.scalar_tensor_tensor(out=o, in0=i, scalar=HEAD ** -0.5, in1=take[:, t:t + 1, 0:nk].to_broadcast([P, n, nk]),
                                             op0=ALU.mult, op1=ALU.add).then_inc(free[b], 1)
                    dve.wait_ge(free[b], ORD[("logit", l, t, b)] + 1)
                v = lg[:, 0:HA * nk].rearrange("p (h k) -> p h k", h=HA)
                dve.tensor_reduce(nmax[:, l, t, :], v, AX.X, ALU.max, negate=True).then_inc(max_done, 1)
                dve.wait_ge(exp_done, TT * l + t + 1)
                link(dve.reciprocal(pinv[:, l, t, :], psum_exp[:, l, t, :]))
                for half in range(2):
                    o = v[:, 3 * half:3 * half + 3, :]
                    dve.tensor_tensor(o, o, pinv[:, l, t, 3 * half:3 * half + 3].unsqueeze(2).to_broadcast([P, 3, nk]), ALU.mult)\
                       .then_inc(prob_done, 1)
                for kt in range(t + 1):
                    wait_full(dve, "pT", l, t, kt, 0)
                    dve.tensor_copy(pT[:, kt, 0:3 * P], bank("pT", l, t, kt, 0)[:, 0:3 * P]).then_inc(free_of("pT", l, t, kt, 0), 1)

            def merge(l):
                dve.wait_ge(gates_done, l + 1)
                for m in range(4):
                    if m > 0:
                        dve.wait_ge(merged, 4 * l + m)
                    for i, b in enumerate((4, 5, 6)):
                        wait_full(dve, "br", l, m, b)
                        g = gT[:, 8 * i + 2 * m:8 * i + 2 * m + 2, :].rearrange("p a t -> p (a t)")
                        dve.tensor_tensor(multi[:, i, :], ps[:, b, :], g, ALU.mult).then_inc(free[b], 1)
                    wait_read(dve, "br", l, m, 6)
                    link(dve.tensor_tensor(multi[:, 0, :], multi[:, 0, :], multi[:, 1, :], ALU.add))
                    dve.tensor_tensor(hT[:, 2 * m:2 * m + 2, :].rearrange("p a t -> p (a t)"), multi[:, 0, :], multi[:, 2, :], ALU.add)\
                       .then_inc(merged, 1)

            def add_residual(n, t, halves, g):
                for half, (src, raises) in enumerate(halves):
                    c = slice(512 * half, 512 * half + 512)
                    i = dve.scalar_tensor_tensor(out=resid[:, c], in0=src, scalar=rstd[:, n, t:t + 1], in1=gtg[:, g, c],
                                                 op0=ALU.mult, op1=ALU.mult)
                    if raises is None:
                        link(i)
                    else:
                        i.then_inc(raises[0], 1)
                        dve.wait_ge(*raises)
                dve.tensor_tensor(x[:, t, :], x[:, t, :], resid, ALU.add).then_inc(x_added, 1)
                dve.wait_ge(x_added, TT * ((n // 5) * 2 + (1 if n % 5 == 4 else 0)) + t + 1)

            def route():
                wait_full(dve, "route", 1)
                lgt = rsm[:, 0, :]
                link_free = dve.tensor_copy(lgt, bank("route", 1)[:, 0:TT * E])
                link_free.then_inc(free_of("route", 1), 1)
                wait_read(dve, "route", 1)
                l3 = lgt.rearrange("p (t e) -> p t e", t=TT)
                v4 = [rout[:, i, :].rearrange("p (t e o) -> p t e o", t=TT, e=E) for i in range(2)]
                other = l3.unsqueeze(2).to_broadcast([P, TT, E, E])
                own = l3.unsqueeze(3).to_broadcast([P, TT, E, E])
                early = const("earlier8").rearrange("p (a e o) -> p a e o", a=1, e=E).to_broadcast([P, TT, E, E])
                dve.tensor_tensor(v4[0], other, own, ALU.is_gt)
                link(dve.tensor_tensor(v4[1], other, own, ALU.is_equal))
                link(dve.tensor_tensor(v4[1], v4[1], early, ALU.mult))
                link(dve.tensor_tensor(v4[0], v4[0], v4[1], ALU.add))
                rank = rsm[:, 1, :]
                link(dve.tensor_reduce(rank, v4[0].rearrange("p t e o -> p (t e) o"), AX.X, ALU.add))
                pick = [rsm[:, 2 + i, :] for i in range(2)]
                for i in range(2):
                    link(dve.tensor_scalar(pick[i], rank, float(i), None, ALU.is_equal))
                both = [rout[:, 2, TT * E * i:TT * E * (i + 1)] for i in range(2)]
                vals = rout[:, 2, 4 * TT * E:4 * TT * E + 2 * TT].rearrange("p (i t) -> p i t", i=2)
                for i in range(2):
                    if i == 0:
                        dve.tensor_tensor(picked[:, :, :].rearrange("p t e -> p (t e)"), pick[0], pick[1], ALU.add).then_inc(picked_done, 1)
                    link(dve.tensor_tensor(both[i], pick[i], lgt, ALU.mult))
                    link(dve.tensor_reduce(vals[:, i, :], both[i].rearrange("p (t e) -> p t e", t=TT), AX.X, ALU.add))
                dve.tensor_tensor(rsm[:, 4, 0:TT], vals[:, 1, :], vals[:, 0, :], ALU.subtract).then_inc(route_d, 1)
                dve.wait_ge(route_e, 1)
                e2, p1, p2 = rsm[:, 5, 0:TT], rsm[:, 5, TT:2 * TT], rsm[:, 5, 2 * TT:3 * TT]
                link(dve.tensor_scalar(p2, e2, 1.0, None, ALU.add))
                link(dve.reciprocal(p1, p2))
                link(dve.tensor_tensor(p2, e2, p1, ALU.mult))
                for i, p in enumerate((p1, p2)):
                    link(dve.tensor_tensor(both[i].rearrange("p (t e) -> p t e", t=TT), pick[i].rearrange("p (t e) -> p t e", t=TT),
                                           p.unsqueeze(2).to_broadcast([P, TT, E]), ALU.mult))
                link(dve.tensor_tensor(comb[:, :, :], both[0].rearrange("p (t e) -> p t e", t=TT),
                                       both[1].rearrange("p (t e) -> p t e", t=TT), ALU.add))
                wait_full(dve, "count", 1)
                before = bank("count", 1)[:, 0:TT * E].rearrange("p (t e) -> p t e", t=TT)
                own = place_of[:, :, 0:E]
                link(dve.scalar_tensor_tensor(out=own, in0=before, scalar=1.0, in1=picked[:, :, :], op0=ALU.add, op1=ALU.mult))
                link(dve.tensor_scalar(own, own, -1.0, None, ALU.add))
                dve.tensor_copy(tokens_of[:, :], bank("count", 1)[:, 2 * E:3 * E]).then_inc(free_of("count", 1), 1)

            def select(e):
                for t in range(TT):
                    last = dve.tensor_scalar(sel[:, t, :], const("place"), place_of[:, t, bass.ds(e, 1)] if not isinstance(e, int) else place_of[:, t, e:e + 1],
                                             None, ALU.is_equal)
                last.then_inc(sel_ready, 1)

            def few_hidden(e, ch):
                w = F_CHUNKS[ch][1]
                dve.wait_ge(few_sig, e * NCH + ch + 1)
                dve.tensor_tensor(gsig[:, ch % 2, 0:w], ps[:, ch % 2, 0:w], sig[:, ch % 2, 0:w], ALU.mult).then_inc(few_prod, 1)
                dve.wait_ge(few_prod, e * NCH + ch + 1)
                dve.tensor_tensor(hid[:, ch % 2, 0:w], ps[:, ch % 2, 256:256 + w], gsig[:, ch % 2, 0:w], ALU.mult).then_inc(few_hid, 1)

            def hidden(b, f, count):
                dve.wait_ge(sig_done, count + 1)
                dve.tensor_tensor(gsig[:, f % 2, :], ps[:, b, 0:T], sig[:, f % 2, :], ALU.mult).then_inc(gate_prod, 1)
                dve.wait_ge(gate_prod, count + 1)
                dve.tensor_tensor(hid[:, f % 2, :], ps[:, b, T:2 * T], gsig[:, f % 2, :], ALU.mult).then_inc(free[b], 1)

            def add_unit(b, e):
                t, half = b // 2, b % 2
                o = yacc[:, t, half * 512:(half + 1) * 512]
                dve.scalar_tensor_tensor(out=o, in0=ps[:, 4 + b, :], scalar=comb[:, t, bass.ds(e, 1)] if not isinstance(e, int) else comb[:, t, e:e + 1],
                                         in1=o, op0=ALU.mult, op1=ALU.add).then_inc(free[4 + b], 1)

            dve.wait_ge(cond_sig, 1)
            link(dve.tensor_tensor(cond[:, :], cond[:, :], c_col[:, :], ALU.mult))
            for a in range(8):
                ada_sum(0, a)
                if a > 0:
                    if a == 1:
                        dve.wait_ge(small_loaded, SMALL)
                    ada_read(0, a - 1)
            ada_read(0, 7)
            link(dve.tensor_copy(pos_f[:, :], pos_i[:, :]))
            for t in range(TT):
                link(dve.tensor_scalar(ang[:, t, :], const("inv_freq"), pos_f[:, t:t + 1], None, ALU.mult))
            for i, quarter in enumerate((0.25, 0.0)):
                link(dve.tensor_scalar(turns[:, :, i, :], ang[:, :, :], 1.0 / (2.0 * np.pi), quarter, ALU.mult, ALU.add))
            link(dve.tensor_scalar(turns[:, :, :, :], turns[:, :, :, :], ROUNDER, None, ALU.add))
            link(dve.tensor_scalar(turns[:, :, :, :], turns[:, :, :, :], -ROUNDER, None, ALU.add))
            for i, shift in enumerate((np.pi / 2, 0.0)):
                src = ang[:, :, :]
                for part in TWO_PI:
                    link(dve.scalar_tensor_tensor(out=red[:, :, i, :], in0=turns[:, :, i, :], scalar=-part, in1=src, op0=ALU.mult, op1=ALU.add))
                    src = red[:, :, i, :]
                link(dve.tensor_scalar(red[:, :, i, :], red[:, :, i, :], shift, None, ALU.add))
            dve.tensor_scalar(red[:, :, :, :], red[:, :, :, :], PI_BELOW, -PI_BELOW, ALU.min, ALU.max).then_inc(angles, 1)

            for l in range(DEPTH):
                def beside(j):
                    if l == 0:
                        for a in ada_beside(j - 1):
                            ada_read(0, a)
                        for a in ada_beside(j):
                            ada_sum(0, a)

                normalize_x(5 * l)
                modulate("xT", l, 0)
                dve.wait_ge(tables, 1)
                wait_read(dve, "in", l, 1)
                finish_rstd(5 * l + 1, LAT)
                for t in range(TT):
                    last = dve.tensor_scalar(latn[:, t, :], natP[:, t, C_LAT:C_LAT + LAT], rstd[:, 5 * l + 1, t:t + 1], None, ALU.mult)
                last.then_inc(lat_ready, 1)
                link(rope(heads_view(C_QA, HA), HA))
                wait_read(dve, "in", l, 2)
                link(rope(natP[:, :, C_KR:C_KR + ROPE].unsqueeze(2), 1))
                dve.tensor_copy(kn[:, :, 0:ROPE], natP[:, :, C_KR:C_KR + ROPE])
                dve.tensor_copy(kn[:, :, HEAD:HEAD + ROPE], natP[:, :, C_KR:C_KR + ROPE]).then_inc(q_ready, 1)
                wait_read(dve, "in", l, 3)
                link(rope(heads_view(C_QI, HI + 1), HI + 1))
                dve.tensor_copy(ki[:, :, 0:HEAD], natP[:, :, C_KI:C_KI + HEAD])
                dve.tensor_copy(ki[:, :, HEAD:P], natP[:, :, C_KI:C_KI + HEAD]).then_inc(qi_ready, 1)
                for t in range(TT):
                    choose(l, t)
                for j in range(11, NIN):
                    beside(j)
                    if 11 <= j < 11 + HC:
                        stick(l, j - 11)
                    if 13 <= j < 13 + HC and j % 2 == 0:
                        g = (j - 14) // 2
                        wait_full(dve, "yc", l, g)
                        dve.tensor_copy(ycT[:, g, :], bank("yc", l, g)[:, 0:T]).then_inc(free_of("yc", l, g), 1)
                if l == 0:
                    for a in ada_beside(NIN - 1):
                        ada_read(0, a)
                for t in range(TT):
                    softmax(l, t)
                merge(l)
                finish_rstd(5 * l + 2, D)
                for t in range(TT):
                    add_residual(5 * l + 2, t, [(ps[:, 2 * t + h, :], (free[2 * t + h], ORD[("y", l, 2 * t + h)] + 1)) for h in range(2)], GTG[(l, 2)])
                normalize_x(5 * l + 3)
                modulate("hT", l, 1)
                dve.wait_ge(acc0, l + 1)
                if l == 0:
                    for u in range(DENSE_UNITS):
                        for f in range(FT):
                            g = u * FT + f
                            hidden(f % 3, f, g)
                            for a in ADA_AFTER.get(g - 1, ()):
                                ada_read(1, a)
                            for a in ADA_AFTER.get(g, ()):
                                ada_sum(1, a)
                        for b in range(4):
                            wait_full(dve, "down", u, b)
                            add_unit(b, u)
                    for a in ADA_AFTER.get(DENSE_UNITS * FT - 1, ()):
                        ada_read(1, a)
                else:
                    link(dve.memset(place_of[:, :, E:E + 1], -1.0))
                    route()
                    wait_read(dve, "count", 1)
                    select(0)
                    with dve.Fori(0, E) as e:
                        dve.wait_ge(sel_turned, e + 1)
                        select(e + 1)
                        with dve.If(has_many(dve, e)):
                            for f in range(FT):
                                hidden(f % 3, f, e * FT + (DENSE_UNITS * FT + f))
                            stand_in(dve, FEW["vector"])
                        with dve.Else():
                            for ch in range(NCH):
                                few_hidden(e, ch)
                            for half, b in enumerate((3, 7)):
                                dve.wait_ge(few_sum, 2 * e + half + 1)
                                dve.tensor_copy(yg[:, half * 512:(half + 1) * 512], ps[:, b, :]).then_inc(few_yg, 1)
                            stand_in(dve, MANY["vector"])
                        for b in range(4):
                            dve.wait_ge(full[4 + b], e + MOE_FIRST[4 + b] + 1)
                            add_unit(b, e)
                finish_rstd(5 * l + 4, D)
                for t in range(TT):
                    add_residual(5 * l + 4, t, [(yacc[:, t, 512 * h:512 * h + 512], None) for h in range(2)], GTG[(l, 5)])


_NAMES = ["x", "c", "positions", "w_ada", "b_ada", "norm_gains", "w_in", "g_kv_latent", "w_uk", "w_uv", "w_pool",
          "pool_scale", "w_br_a", "w_br_b", "w_br_c", "w_out", "w_gate_dense", "w_up_dense", "w_down_dense",
          "w_router", "w_gate_moe", "w_up_moe", "w_down_moe"]


def kernel(**inputs):
    import concourse.bacc as bacc
    from concourse.bass_utils import run_bass_kernel_spmd

    nc = bacc.Bacc("TRN2", target_bir_lowering=False, num_devices=1)
    arrays, aps = {}, []
    consts, const_at = shape_constants()
    for name in _NAMES + ["consts"]:
        a = consts if name == "consts" else np.ascontiguousarray(inputs[name])
        arrays["in_" + name] = a
        aps.append(nc.dram_tensor("in_" + name, a.shape, mybir.dt.from_np(a.dtype), kind="ExternalInput").ap())
    y = nc.dram_tensor("y", inputs["x"].shape, F32, kind="ExternalOutput").ap()
    build_trunk(nc, *aps, const_at, y)
    r = run_bass_kernel_spmd(nc, [arrays], core_ids=[0])
    return r.results[0]["y"]
```

```python
from contextlib import ExitStack

import numpy as np
import concourse.bass as bass
from concourse import mybir

P = 128
F32 = mybir.dt.float32
F32R = mybir.dt.float32r
I32 = mybir.dt.int32
ALU = mybir.AluOpType
ACT = mybir.ActivationFunctionType
AX = mybir.AxisListType

HEAD = 64
ROPE = HEAD // 4
NOPE = HEAD - ROPE
HALF = ROPE // 2
THETA = 500000.0
WINDOWS = (2, 4, 8, 16)
TOPK = 64
EPS = 1e-6
NOT_CAUSAL = -3.0e38
TAKEN = -3.4e38
FAR = -1.0e30
ROUNDER = 1.5 * 2.0 ** 23
TWO_PI = (6.28125, 0.0019354820251464844, -1.7484556025237907e-07)
PI_BELOW = 3.1415925


def shape_constants():
    r = np.arange(P)
    row, col = r[:, None], r[None, :]
    parts = {
        "ident": (row == col).astype(np.float32),
        "ones": np.ones((P, P), np.float32),
        "neg_from": -(row >= col).astype(np.float32),
        "neg_ones": -np.ones((P, P), np.float32),
        "before": np.where(row < col, 0.0, FAR).astype(np.float32),
        "causal": (col <= row).astype(np.float32),
        "not_causal": np.where(col <= row, 0.0, NOT_CAUSAL).astype(np.float32),
        "earlier": (row < col).astype(np.float32),
        "place": np.broadcast_to(np.arange(P, dtype=np.float32)[None, :], (P, P)),
        "inv_freq": np.broadcast_to((np.float32(THETA) ** (-np.arange(0, ROPE, 2, dtype=np.float32) / np.float32(ROPE)))[None, :], (P, HALF)).astype(np.float32),
    }
    e = np.arange(8)
    parts["earlier8"] = np.broadcast_to((e[None, :] < e[:, None]).astype(np.float32).reshape(1, 64), (P, 64))
    t = np.arange(2 * P)[None, :]
    for st in range(2):
        s = r[:, None] + P * st
        for g, w in enumerate(WINDOWS):
            inside = (s <= t) & (s > t - w)
            band = np.where(inside, np.float32(1) / np.minimum(t + 1, w).astype(np.float32), np.float32(0))
            parts[f"band{st}{g}"] = (band - (s == t)).astype(np.float32)
    at, offsets = 0, {}
    for name, a in parts.items():
        offsets[name] = (at, a.shape[1])
        at += a.shape[1]
    return np.ascontiguousarray(np.concatenate(list(parts.values()), axis=1)), offsets


def build_trunk(nc, x_in, c, positions, w_ada, b_ada, norm_gains, w_in, g_kv_latent, w_uk, w_uv,
                w_pool, pool_scale, w_br_a, w_br_b, w_br_c, w_out, w_gate_dense, w_up_dense,
                w_down_dense, w_router, w_gate_moe, w_up_moe, w_down_moe, consts, const_at, out):
    DEPTH, D, IN_WIDTH = w_in.shape
    T = x_in.shape[1]
    TT = T // P
    KD = D // P
    WA, WB, WC = w_br_a.shape[1], w_br_b.shape[1], w_br_c.shape[1]
    LAT = w_uk.shape[1]
    HA, HC = WA // HEAD, WC // HEAD
    E, _, FE = w_gate_moe.shape[1:]
    FF = w_gate_dense.shape[2]
    HI = 4
    assert TT == 2 and DEPTH == 2 and FF % FE == 0 and LAT == P and WB == 256 and WC == 256

    C_QA, C_LAT = 0, WA
    C_KR = C_LAT + LAT
    C_QI = C_KR + ROPE
    C_KI = C_QI + HI * HEAD
    C_WI = C_KI + HEAD
    C_U = C_WI + HI
    C_QC = C_U + WB
    C_KC = C_QC + WC
    C_VC = C_KC + WC
    C_G = C_VC + WC
    NATW = C_QC

    NS, NP, SLOTW = 6, 3, KD * 256
    W_IN_SLOTS = [(0, 256), (256, 256), (512, 256), (768, C_U - 768), (C_U, 256), (C_QC, 256),
                  (C_KC, 256), (C_VC, 256)] + [(C_G + 256 * j, 256) for j in range(3 * D // 256)]
    NIN = len(W_IN_SLOTS)
    NADA = 6 * D // 256
    F_CHUNKS = [(256 * j, min(256, FE - 256 * j)) for j in range((FE + 255) // 256)]
    FT = FE // P
    UNIT = 3 * len(F_CHUNKS)
    assert UNIT % NS == 0
    DENSE_UNITS = FF // FE

    NCH = len(F_CHUNKS)
    ORDER = [("gate", 0), ("up", 0)]
    for ch in range(1, NCH):
        ORDER += [("gate", ch), ("up", ch), ("down", ch - 1)]
    ORDER.append(("down", NCH - 1))

    def ada_beside(j):
        return (8 + j,) if 0 <= j < 8 else (16 + j - 12,) if 12 <= j < 20 else ()

    def mixer_slots(l):
        s = [("ada", 0, j) for j in range(8)] if l == 0 else []
        for j in range(NIN):
            s.append(("in", l, j))
            if l == 0:
                s += [("ada", 0, a) for a in ada_beside(j)]
        return s + [("br", l, 0), ("out", l, 0), ("out", l, 1), ("br", l, 1), ("br", l, 2), ("br", l, 3), ("out", l, 2), ("out", l, 3)]

    def dense_slots():
        s = []
        for u in range(DENSE_UNITS):
            for i, (kind, ch) in enumerate(ORDER):
                s.append((kind, u, ch))
                if i + 1 < len(ORDER) and ORDER[i + 1][0] == "gate" or i + 1 == len(ORDER):
                    n = u * NCH + ch + (1 if kind == "down" and i + 1 < len(ORDER) else 0)
                    s += [("ada", 1, 2 * n), ("ada", 1, 2 * n + 1)]
        return s

    LOADS = mixer_slots(0) + dense_slots() + mixer_slots(1)
    NUMBER = {key: n for n, key in enumerate(LOADS)}
    EXPERT0 = len(LOADS)
    TURNS = UNIT // NS

    def load_number(key):
        if key[1] == "moe":
            return EXPERT0 + ORDER.index((key[0], key[2]))
        return NUMBER[key]

    SPLITS = [key for key in LOADS if key[0] in ("in", "out", "gate", "up", "down")] + [(kind, "moe", ch) for kind, ch in ORDER]
    SPLIT0 = len(SPLITS) - UNIT
    def lower_by(key):
        if key[1] == "moe":
            return {"gpsimd": (0, 3), "vector": (3, KD)}
        return {"vector" if key[0] == "gate" else "gpsimd": (0, KD)}
    LOWERS = ("vector", "gpsimd")
    LOWER_NO = {(w, key): sum(w in lower_by(k) for k in SPLITS[:n + 1]) for n, key in enumerate(SPLITS) for w in LOWERS}
    LOWER_PER = {w: sum(w in lower_by((kind, "moe", ch)) for kind, ch in ORDER) for w in LOWERS}
    assert UNIT % NP == 0

    def ada_of_step(n):
        return (2 * n, 2 * n + 1) if n >= 0 else ()

    JOBS = []
    def job(bank, *key):
        JOBS.append((key, bank))
    for l in range(DEPTH):
        if l == 0:
            for a in range(9):
                if a < 8:
                    job(4 + a % 2, "adarow", a)
                if a > 0:
                    job(2 + (a - 1) % 2, "ada", 0, a - 1)
        for j in range(4):
            job(j, "xT", l, j)
        for j in range(NIN):
            job(j % 2, "in", l, j)
            if l == 0:
                for a in ada_beside(j - 1):
                    job(2 + a % 2, "ada", 0, a)
            if j == 7:
                for n in range(4):
                    job(4 + n, "tr", l, n)
            if j == 9:
                for t in range(TT):
                    for par in range(2):
                        job(4 + 2 * t + par, "idx", l, t, par)
            if j == 10:
                job(4, "ukv", l)
                job(5, "pool", l)
                job(4, "kT", l)
                job(5, "yb", l)
            if 13 <= j < 13 + HC and j % 2 == 1:
                job(6, "yc", l, (j - 13) // 2)
            if 12 <= j < 12 + HC:
                job(4 + (j - 12) % 2, "stick2", l, j - 12)
            if 11 <= j < 11 + HC:
                job(4 + (j - 11) % 2, "stick", l, j - 11)
        if l == 0:
            for a in ada_beside(NIN - 1):
                job(2 + a % 2, "ada", 0, a)
        for t in range(TT):
            for b in ([4, 5] if t == 0 else [4, 5, 6, 7]):
                job(b, "logit", l, t, b)
            for kt in range(t + 1):
                for b in (0, 1):
                    job(b, "pT", l, t, kt, b)
            job(2, "av", l, t)
        for i in range(3):
            for m in range(4):
                job(4 + m if i != 1 else m, "br", l, i, m)
        for b in range(4):
            job(b, "y", l, b)
        for j in range(4):
            job(4 + j, "hT", l, j)
        if l == 1:
            job(2, "route", l)
            job(2, "count", l)
        if l == 0:
            for n in range(DENSE_UNITS * NCH):
                u, ch = n // NCH, n % NCH
                if n > 0:
                    job(3, "ada", 1, 2 * n - 2)
                if ch == NCH - 1:
                    for b in range(4):
                        job(4 + b, "down", u, b)
            job(3, "ada", 1, NADA - 2)
    seen, ORD, BANK = [0] * 8, {}, {}
    for key, bank_no in JOBS:
        assert key not in ORD, key
        ORD[key], BANK[key] = seen[bank_no], bank_no
        seen[bank_no] += 1
    MOE_FIRST = list(seen)
    assert F_CHUNKS[-1][1] == P and HC == 4 and NIN == 20 and NADA == 24 and NCH * DENSE_UNITS * 2 == NADA

    ctx = ExitStack()
    with ctx:
        def sb(name, shape, dt=F32):
            return ctx.enter_context(nc.sbuf_tensor(name, shape, dt))

        def sem(name):
            return ctx.enter_context(nc.semaphore(name))

        NACC = 3
        ps = ctx.enter_context(nc.psum_tensor("ps", [P, 8, 512], F32))
        with ExitStack() as under:
            wl = under.enter_context(nc.sbuf_tensor("wl", [P, NS, SLOTW], F32R))
        ring = sb("ring", [P, NS, SLOTW])
        wh = sb("wh", [P, NP, SLOTW], F32R)
        with ExitStack() as under:
            def lower(name, shape):
                return under.enter_context(nc.sbuf_tensor(name, shape, F32R))
            hidh, hidl = lower("hidh", [P, 2, 512]), lower("hidl", [P, 2, 512])
            xgh, xgl = lower("xgh", [P, KD, P]), lower("xgl", [P, KD, P])
        natP = sb("natP", [P, TT, NATW])
        vc = sb("vc", [P, TT, WC])
        qkc = sb("qkc", [P, 4, T])
        trs = sb("trs", [P, 8, P])
        cst = sb("cst", [P, consts.shape[1]])
        x = sb("x", [P, TT, D])
        xn = sb("xn", [P, TT, D])
        hTh, hTl = sb("hTh", [P, KD, T], F32R), sb("hTl", [P, KD, T], F32R)
        big = sb("big", [P, 24 * T])
        gT = big[:, :].rearrange("p (m t) -> p m t", t=T)
        yacc = big[:, 0:TT * D].rearrange("p (t d) -> p t d", t=TT)
        sig = big[:, TT * D:TT * D + 512]
        gsig = big[:, TT * D + 512:TT * D + 1024]
        hid = big[:, TT * D + 1024:TT * D + 1536]
        resid = big[:, TT * D + 1536:TT * D + 1536 + D]
        xraw = big[:, 5 * D:6 * D]
        hraw = big[:, 4 * D:6 * D].rearrange("p (j n) -> p j n", j=4)
        gtg = sb("gtg", [P, 3, D])
        acc = sb("acc", [P, NACC, 256])
        qT = sb("qT", [P, 3, T])
        kT = sb("kT", [P, T])
        va = sb("va", [P, TT, HEAD])
        yaT = sb("yaT", [P, 3, T])
        ybT = sb("ybT", [P, 2, T])
        ycT = sb("ycT", [P, 2, T])
        multi = sb("multi", [P, 3, 512])
        pT = sb("pT", [P, 2, HA * P])
        poolT = pT[:, :, 0:T]
        mraw = pT[:, :, 0:512]
        spl = pT[:, 0, :].rearrange("p (b n) -> p b n", b=2)
        rel = multi[:, :, :].rearrange("p a b -> p (a b)")[:, 0:768].rearrange("p (b n) -> p b n", b=2)
        aT = pT[:, 1, :].rearrange("p (b n) -> p b n", b=2)
        flat = xn[:, :, :].rearrange("p t d -> p (t d)")
        def tiled(at, width):
            return flat[:, at:at + TT * width].rearrange("p (t n) -> p t n", t=TT)
        kn = tiled(0, P)
        ki = tiled(TT * P, P)
        latn = tiled(2 * TT * P, LAT)
        score = tiled(3 * TT * P, T)
        lg = flat[:, 0:HA * T]
        take = tiled(HA * T, T)
        c_col = sb("c_col", [P, KD])
        cond = sb("cond", [P, KD])
        pos_i = sb("pos_i", [P, TT], I32)
        pos_f = sb("pos_f", [P, TT])
        ang = sb("ang", [P, TT, HALF])
        turns = sb("turns", [P, TT, 2, HALF])
        red = sb("red", [P, TT, 2, HALF])
        cs = sb("cs", [P, TT, 2, HALF])
        rot = sb("rot", [P, 4, TT * 6 * HALF])
        gcol = sb("gcol", [P, DEPTH, 2, KD])
        modc = sb("modc", [P, DEPTH, 4, KD])
        bias = sb("bias", [NADA, DEPTH, 256])
        glat = sb("glat", [P, DEPTH])
        pscale = sb("pscale", [P, DEPTH, 2])
        wukv = sb("wukv", [P, DEPTH, NOPE + HEAD])
        wpool = sb("wpool", [P, DEPTH, 2, P])
        wroute = sb("wroute", [P, KD, E])
        comb = sb("comb", [P, TT, E])
        ss = sb("ss", [P, DEPTH * 5, TT])
        var = sb("var", [P, DEPTH * 5, TT])
        guess = sb("guess", [P, DEPTH * 5, TT])
        newt = sb("newt", [P, 2, TT])
        rstd = sb("rstd", [P, DEPTH * 5, TT])
        nmax = sb("nmax", [P, DEPTH, TT, HA])
        psum_exp = sb("psum_exp", [P, DEPTH, TT, HA])
        pinv = sb("pinv", [P, DEPTH, TT, HA])
        top8 = sb("top8", [P, 8])
        rout = multi[:, :, :].rearrange("p a b -> p (a b)")[:, 768:768 + 3 * TT * E * E].rearrange("p (a n) -> p a n", a=3)
        rsm = sb("rsm", [P, 6, TT * E])
        picked = sb("picked", [P, TT, E])
        place_of = sb("place_of", [P, TT, E + 1])
        tokens_of = sb("tokens_of", [P, E], I32)
        yg = multi[:, 0:2, :].rearrange("p a b -> p (a b)")
        sel = qT[:, 0, :].rearrange("p (t s) -> p t s", t=TT)
        selT = qT[:, 1, :]

        def const(name):
            at, n = const_at[name]
            return cst[:, at:at + n]

        ident, ones = const("ident"), const("ones")


        loaded = [sem(f"slot_loaded{i}") for i in range(NS)]
        full = [sem(f"bank_full{i}") for i in range(8)]
        free = [sem(f"bank_emptied{i}") for i in range(8)]
        x_loaded = sem("x_loaded")
        c_loaded = sem("c_loaded")
        columns_loaded = sem("gain_columns_and_positions_loaded")
        small_loaded = sem("small_loaded")
        gain_loaded = [sem(f"gain_loaded{i}") for i in range(3)]
        cond_done = sem("condition")
        consts_loaded = sem("consts_loaded")
        zeroed = sem("zeroed")
        acc_done = sem("ada_chunk_summed")
        cond_sig = sem("cond_sigmoid")
        angles = sem("angles_reduced")
        tables = sem("rope_tables")
        ss_done = sem("square_sums")
        var_done = sem("variances")
        guess_done = sem("rstd_guess")
        xn_done = sem("x_normed")
        qi_ready = sem("indexer_ready")
        lat_ready = sem("latent_normed")
        q_ready = sem("q_and_k_rope_ready")
        stick_abs = sem("stick_abs")
        stick_log = sem("stick_log")
        stick_sp = sem("stick_softplus")
        stick_av = sem("stick_av")
        gates_done = sem("gates_done")
        max_done = sem("neg_max")
        exp_done = sem("exp_done")
        prob_done = sem("prob_done")
        high = sem("weights_high_parts")
        low = {w: sem("weights_low_parts_by_" + w) for w in ("vector", "gpsimd")}
        hT_high = sem("h_high_parts")
        hT_low = sem("h_low_parts")
        br_used = sem("first_branch_weights_used")
        merged_raw = sem("merged_unsplit")
        merged_high = sem("merged_high_parts")
        merged = sem("merged")
        out_used = sem("out_rows_used")
        x_added = sem("x_added")
        acc0 = sem("expert_sum_cleared")
        sig_done = sem("sigmoid_done")
        gate_prod = sem("gate_product")
        down_used = sem("down_rows_used")
        route_d = sem("route_difference")
        route_e = sem("route_exp")
        picked_done = sem("picked")
        sel_ready = sem("selection_ready")
        sel_turned = sem("selection_turned")
        selT_ready = sem("turned_selection_ready")
        gathered = sem("tokens_gathered")
        xg_ready = sem("gathered_tokens_ready")
        gate_used = sem("gate_weights_used")
        up_used = sem("up_weights_used")
        hid_done = sem("hidden_unsplit")
        hid_high = sem("hidden_high_parts")
        hid_low = sem("hidden_low_parts")
        few_turned = sem("few_hidden_turned")
        xraw_ready = sem("gathered_tokens_unsplit")
        xg_high = sem("gathered_tokens_high_parts")
        few_sum = sem("few_down_products")
        few_yg = sem("few_result_ready")
        v_chain = sem("vector_chain")
        a_chain = sem("scalar_chain")
        stored = sem("stored")

        block = ctx.enter_context(nc.Block())

        def slot(key):
            return load_number(key) % NS

        def wait_loaded(eng, key, turn=0):
            n = load_number(key)
            eng.wait_ge(loaded[n % NS], turn * 16 + 16 * (n // NS + 1))

        def wait_full(eng, *key):
            eng.wait_ge(full[BANK[key]], ORD[key] + 1)

        def wait_free(eng, *key):
            if ORD[key]:
                eng.wait_ge(free[BANK[key]], ORD[key])

        def wait_read(eng, *key):
            eng.wait_ge(free[BANK[key]], ORD[key] + 1)

        def bank(*key):
            return ps[:, BANK[key], :]

        def full_of(*key):
            return full[BANK[key]]

        def free_of(*key):
            return free[BANK[key]]

        BY_TENSOR = 8

        def ada_job(l, a):
            return ("ada", l, a - a % 2 if l else a)

        def ada_bank(l, a):
            b = bank(*ada_job(l, a))
            return b[:, 256:512] if l and a % 2 else b[:, 0:256]

        def ada_index(l, a):
            return l * NADA + a

        GTG = {(0, 2): 0, (0, 5): 1, (1, 2): 0, (1, 5): 2}
        ROWS = {(0, 2): 1, (0, 5): 1, (1, 2): 2, (1, 5): 1}
        LOGIT_ORDER = (0, 2, 4, 1, 3, 5)

        def logit_place(t, i):
            nk = P * (t + 1)
            if t == 0:
                return 4 + i // 3, (i % 3) * nk, i % 3 == 2
            return 4 + 2 * (i // 3) + (i % 3) // 2, (i % 3 % 2) * nk, i % 3 != 0

        def count(un, per, k):
            return un[0] * per + (un[1] * per + k)

        def unit_of(key, e=0):
            return (e, DENSE_UNITS) if key[1] == "moe" else (key[1], 0)

        def wait_used(eng, key, e=0):
            kind, l, j = key
            if kind == "ada" and ada_index(l, j) < BY_TENSOR:
                wait_full(eng, "adarow", j)
            elif kind == "ada":
                eng.wait_ge(acc_done, ada_index(l, j) - BY_TENSOR + 1)
            elif kind == "in":
                wait_full(eng, "in", l, j)
            elif kind == "br" and j == 0:
                eng.wait_ge(br_used, l + 1)
            elif kind == "br":
                wait_full(eng, "br", l, j - 1, 3)
            elif kind == "out" and j < 3:
                eng.wait_ge(out_used, 3 * l + j + 1)
            elif kind == "out":
                wait_full(eng, "y", l, 3)
            elif kind == "gate":
                eng.wait_ge(gate_used, count(unit_of(key, e), NCH, j + 1))
            elif kind == "up":
                eng.wait_ge(up_used, count(unit_of(key, e), NCH, j + 1))
            elif j < NCH - 1:
                eng.wait_ge(down_used, count(unit_of(key, e), NCH - 1, j + 1))
            elif l == "moe":
                eng.wait_ge(full[7], e + MOE_FIRST[7] + 1)
            else:
                wait_full(eng, "down", l, 3)

        def wait_split(eng, key, e=0):
            for w in lower_by(key):
                eng.wait_ge(low[w], e * LOWER_PER[w] + LOWER_NO[(w, key)])

        def width(key):
            if key[0] == "in":
                return KD * W_IN_SLOTS[key[2]][1]
            return SLOTW if key[0] == "out" else KD * F_CHUNKS[key[2]][1]

        def high_of(key):
            return wh[:, SPLITS.index(key) % NP, 0:width(key)]

        def low_of(key):
            return wl[:, slot(key), 0:width(key)]

        def lower_part(eng, w, key, e=0):
            a, b = [x * width(key) // KD for x in lower_by(key)[w]]
            eng.wait_ge(high, e * UNIT + SPLITS.index(key) + 1)
            eng.tensor_tensor(low_of(key)[:, a:b], ring[:, slot(key), a:b], high_of(key)[:, a:b].bitcast(F32), ALU.subtract)\
               .then_inc(low[w], 1)

        def relu_at(t, par):
            nk = P * (t + 1)
            m = multi[:, :, :].rearrange("p a b -> p (a b)")
            at = par * 2 * nk if t == 0 else 512 + par * 2 * nk
            return m[:, at:at + 2 * nk]

        def stand_in(eng, signals):
            for s, n in signals:
                eng.sem_inc(s, n)

        def has_many(eng, e):
            return eng.value_load(tokens_of[0:1, bass.ds(e, 1)], min_val=0, max_val=T) > P

        FIRST = const_at["band00"][0]
        cols = [(pos_i[:, :], positions[0].rearrange("(t p) -> p t", p=P))]
        small = [(cst[:, FIRST:], consts[:, FIRST:])]
        for l in range(DEPTH):
            for n in range(2):
                cols.append((gcol[:, l, n, :], norm_gains[l, 2 * n].rearrange("(k p) -> p k", p=P)))
            small.append((glat[:, l:l + 1], g_kv_latent[l].rearrange("(p a) -> p a", a=1)))
            small.append((pscale[:, l, :], pool_scale[l].rearrange("(k p) -> p k", p=P)))
            small.append((wukv[:, l, 0:NOPE], w_uk[l]))
            small.append((wukv[:, l, NOPE:NOPE + HEAD], w_uv[l]))
            for g in range(4):
                r = slice(HEAD * (g % 2), HEAD * (g % 2) + HEAD)
                small.append((wpool[r, l, g // 2, r], w_pool[l, g]))
        small.append((wroute[:, :, :], w_router[0].rearrange("(k p) e -> p k e", p=P)))
        SMALL = 16 * len(small)

        @block.sync
        def _(sp):
            def place(s, w, n=KD):
                return ring[:, s, 0:n * w].rearrange("p (k n) -> p k n", k=n)

            def columns(s, matrix, c0, w):
                return sp.dma_start(place(s, w), matrix[:, c0:c0 + w].rearrange("(k p) n -> p k n", p=P))

            def rows(s, matrix, r0, n):
                return sp.dma_start(place(s, D, n), matrix[r0:r0 + n * P, :].rearrange("(k p) n -> p k n", p=P))

            sp.dma_start(c_col[:, :], c[0].rearrange("(k p) -> p k", p=P), allow_slow_non_contiguous=True).then_inc(c_loaded, 16)
            sp.dma_start(cst[:, 0:FIRST], consts[:, 0:FIRST]).then_inc(consts_loaded, 16)
            sp.dma_start(bias[:, :, :], b_ada.rearrange("l (a n) -> a l n", a=NADA)).then_inc(consts_loaded, 16)
            for n, key in enumerate(LOADS):
                s = n % NS
                if n >= NS:
                    wait_used(sp, LOADS[n - NS])
                kind, l, j = key
                if kind == "ada":
                    d = columns(s, w_ada[l], 256 * j, 256)
                elif kind == "in":
                    d = columns(s, w_in[l], *W_IN_SLOTS[j])
                elif kind == "br":
                    m, r0, k = [(w_br_a, 0, 2), (w_br_a, 2 * P, 1), (w_br_b, 0, 2), (w_br_c, 0, 2)][j]
                    d = rows(s, m[l], r0, k)
                elif kind == "out":
                    d = rows(s, w_out[l], 2 * P * j, 2)
                elif kind == "down":
                    c0, w = F_CHUNKS[j]
                    d = rows(s, w_down_dense[0], FE * l + c0, w // P)
                else:
                    c0, w = F_CHUNKS[j]
                    d = columns(s, (w_gate_dense if kind == "gate" else w_up_dense)[0], FE * l + c0, w)
                d.then_inc(loaded[s], 16)

            def expert_load(i, e):
                kind, ch = ORDER[i]
                c0, w = F_CHUNKS[ch]
                s = slot((kind, "moe", ch))
                if kind == "down":
                    src = w_down_moe[0].rearrange("e f n -> (e f) n")[bass.ds(e * FE + c0, w), :]
                    dst = place(s, D, w // P)
                else:
                    m = w_gate_moe if kind == "gate" else w_up_moe
                    src = m[0].rearrange("e d f -> (e d) f")[bass.ds(e * D, D), c0:c0 + w]
                    dst = place(s, w)
                sp.dma_start(dst, src.rearrange("(k p) n -> p k n", p=P)).then_inc(loaded[s], 16)

            def moe_key(i):
                kind, ch = ORDER[i]
                return kind, "moe", ch

            for i in range(NS):
                wait_used(sp, LOADS[EXPERT0 + i - NS])
                expert_load(i, 0)
            with sp.Fori(0, E - 1) as e:
                for i in range(NS, UNIT):
                    wait_used(sp, moe_key(i - NS), e)
                    expert_load(i, e)
                for i in range(NS):
                    wait_used(sp, moe_key(i - NS), e)
                    expert_load(i, e + 1)
            for i in range(NS, UNIT):
                wait_used(sp, moe_key(i - NS), E - 1)
                expert_load(i, E - 1)

            for t in range(TT):
                sp.wait_ge(x_added, TT * (2 * DEPTH - 1) + t + 1)
                sp.dma_start(out[0, t * P:(t + 1) * P, :], x[:, t, :]).then_inc(stored, 16)
            sp.wait_ge(stored, 16 * TT)

        @block.gpsimd
        def _(pool):
            pool.dma_start(x[:, :, :], x_in[0].rearrange("(t p) d -> p t d", p=P)).then_inc(x_loaded, 16)
            for dst, src in cols:
                pool.dma_start(dst, src, allow_slow_non_contiguous=True).then_inc(columns_loaded, 16)
            pool.memset(wpool[:, :, :, :], 0.0).then_inc(zeroed, 1)
            pool.memset(comb[:, :, :], 1.0).then_inc(zeroed, 1)
            pool.wait_ge(zeroed, 2)
            for dst, src in small:
                pool.dma_start(dst, src, allow_slow_non_contiguous=True).then_inc(small_loaded, 16)

            def gain_row(l, seg):
                b = GTG[(l, seg)]
                row = norm_gains[l, 1 if seg == 2 else 3]
                pool.dma_start(gtg[:, b, :], row.rearrange("(a n) -> a n", a=1).to_broadcast([P, D])).then_inc(gain_loaded[b], 16)

            def clear_expert_sum(l):
                pool.wait_ge(merged, 4 * l + 4)
                pool.memset(yacc, 0.0).then_inc(acc0, 1)

            def lower_parts(keys):
                for key in keys:
                    if "gpsimd" in lower_by(key):
                        lower_part(pool, "gpsimd", key)

            gain_row(0, 2)
            gain_row(0, 5)
            gain_row(1, 5)
            for l in range(DEPTH):
                lower_parts([("in", l, j) for j in range(NIN)] + [("out", l, j) for j in range(4)])
                clear_expert_sum(l)
                if l == 0:
                    for u in range(DENSE_UNITS):
                        lower_parts([(kind, u, ch) for kind, ch in ORDER])
                        if u == 0:
                            pool.wait_ge(x_added, TT)
                            gain_row(1, 2)
            with pool.Fori(0, E) as e:
                for kind, ch in ORDER:
                    lower_part(pool, "gpsimd", (kind, "moe", ch), e)

        @block.tensor
        def _(pe):
            def mm(o, a, b, start, stop, **kw):
                return pe.matmul(o, a, b, start=start, stop=stop, **kw)

            def w_tile(key, w, n=KD):
                return ring[:, slot(key), 0:n * w].rearrange("p (k n) -> p k n", k=n)

            def pair_tile(key, w, n=KD):
                return [t[:, 0:n * w].rearrange("p (k n) -> p k n", k=n) for t in (high_of(key), low_of(key))]

            def mm3(o, a, b, start, stop, **kw):
                mm(o, a[0], b[0], start, False, **kw)
                mm(o, a[0], b[1], False, False, **kw)
                return mm(o, a[1], b[0], False, stop, **kw)

            def tokens(k, cols):
                return hTh[:, k, cols], hTl[:, k, cols]

            def half_rows(h):
                return slice(HEAD * (h % 2), HEAD * (h % 2) + HEAD)

            def ada_product(l, a):
                n = ada_index(l, a)
                pick = ident[0:NADA, a:a + 1]
                if l == 0 or a % 2 == 0:
                    wait_free(pe, *ada_job(l, a))
                b = ada_bank(l, a)
                if n < BY_TENSOR:
                    wait_read(pe, "adarow", a)
                    for m in range(2):
                        last = mm(b[:, m:m + 1], acc[0:1, a % NACC, m * P:(m + 1) * P], ones[0:1, 0:1], True, True)
                    last.then_inc(full_of("ada", l, a), 1)
                    return
                pe.wait_ge(acc_done, n - BY_TENSOR + 1)
                if a // 4 in (2, 5):
                    mm(b[:, 0:256], ones, acc[:, n % NACC, :], True, False)
                    last = mm(b[:, 0:256], pick.to_broadcast([NADA, P]), bias[:, l, :], False, True)
                else:
                    for m in range(2):
                        cols = slice(m * P, (m + 1) * P)
                        mm(b[:, m:m + 1], acc[:, n % NACC, cols], ones[:, 0:1], True, False)
                        last = mm(b[:, m:m + 1], bias[:, l, cols], pick, False, True)
                if l == 0 or a % 2:
                    last.then_inc(full_of(*ada_job(l, a)), 1)

            def ada_row(a):
                wait_loaded(pe, ("ada", 0, a))
                wait_free(pe, "adarow", a)
                w, o = w_tile(("ada", 0, a), 256), bank("adarow", a)[0:1, 0:256]
                for k in range(KD):
                    mm(o, cond[:, k:k + 1], w[:, k, :], k == 0, False)
                mm(o, ident[0:NADA, a:a + 1], bias[:, 0, :], False, True).then_inc(full_of("adarow", a), 1)

            def transpose_x(name, l):
                for j in range(4):
                    wait_free(pe, name, l, j)
                    for i in range(4):
                        k, t = 2 * j + i // 2, i % 2
                        last = pe.transpose(bank(name, l, j)[:, i * P:(i + 1) * P], xn[:, t, k * P:(k + 1) * P], ident)
                    last.then_inc(full_of(name, l, j), 1)

            def transposes(l):
                groups = [[natP[:, t, C_QI + P * h:C_QI + P * (h + 1)] for h in range(2) for t in range(TT)],
                          [ki[:, t, :] for t in range(TT)] + [latn[:, t, :] for t in range(TT)],
                          [natP[:, t, P * h:P * (h + 1)] for h in range(2) for t in range(TT)],
                          [natP[:, t, 2 * P:3 * P] for t in range(TT)]]
                ready = [qi_ready, lat_ready, q_ready, q_ready]
                for n, group in enumerate(groups):
                    pe.wait_ge(ready[n], l + 1)
                    wait_free(pe, "tr", l, n)
                    for i, src in enumerate(group):
                        last = pe.transpose(bank("tr", l, n)[:, i * P:(i + 1) * P], src, ident)
                    last.then_inc(full_of("tr", l, n), 1)

            def indexer(l):
                wait_read(pe, "tr", l, 0)
                wait_read(pe, "tr", l, 1)
                keys = trs[:, 4:6, :].rearrange("p a b -> p (a b)")
                for t in range(TT):
                    nk = P * (t + 1)
                    for par in range(2):
                        wait_free(pe, "idx", l, t, par)
                        r = half_rows(par)
                        for h in range(2):
                            last = mm(bank("idx", l, t, par)[:, h * nk:(h + 1) * nk], trs[r, 2 * h + t, :], keys[r, 0:nk], True, True)
                        last.then_inc(full_of("idx", l, t, par), 1)

            def latent_and_pool(l):
                wait_free(pe, "ukv", l)
                for t in range(TT):
                    last = mm(bank("ukv", l)[:, t * P:t * P + NOPE + HEAD], trs[:, 6 + t, :], wukv[:, l, :], True, True)
                last.then_inc(full_of("ukv", l), 1)
                wait_read(pe, "in", l, 4)
                wait_free(pe, "pool", l)
                for g in range(4):
                    for s in range(TT):
                        last = mm(bank("pool", l)[half_rows(g), (g // 2) * T:(g // 2 + 1) * T],
                                  natP[:, s, C_U + HEAD * g:C_U + HEAD * (g + 1)], const(f"band{s}{g}"), s == 0, s == 1)
                last.then_inc(full_of("pool", l), 1)
                wait_read(pe, "ukv", l)
                wait_free(pe, "kT", l)
                for t in range(TT):
                    last = pe.transpose(bank("kT", l)[:, t * P:(t + 1) * P], kn[:, t, :], ident)
                last.then_inc(full_of("kT", l), 1)
                wait_read(pe, "pool", l)
                wait_free(pe, "yb", l)
                for g in range(2):
                    last = mm(bank("yb", l)[:, g * T:(g + 1) * T], wpool[:, l, g, :], poolT[:, g, :], True, True)
                last.then_inc(full_of("yb", l), 1)

            def stick_logits(l, h):
                if h == 0:
                    wait_read(pe, "in", l, 5)
                    wait_read(pe, "in", l, 6)
                    wait_read(pe, "in", l, 7)
                wait_free(pe, "stick", l, h)
                b, r, ft = bank("stick", l, h), half_rows(h), h // 2
                mm(b[:, 0:T], qkc[r, 2 + ft, 0:P], qkc[r, ft, :], True, False, skip_group_check=True)
                mm(b[:, T:T + P], qkc[r, 2 + ft, P:T], qkc[r, ft, P:T], False, False, skip_group_check=True)
                mm(b[:, 0:P], ident, const("before"), False, False, skip_group_check=True)
                mm(b[:, T:T + P], ident, const("before"), False, True, skip_group_check=True).then_inc(full_of("stick", l, h), 1)

            def stick_sums(l, h):
                pe.wait_ge(stick_sp, HC * l + h + 1)
                wait_free(pe, "stick2", l, h)
                b, s = bank("stick2", l, h), spl[:, h % 2, :]
                mm(b[:, 0:T], const("neg_from"), s[:, 0:T], False, False, skip_group_check=True)
                mm(b[:, P:T], const("neg_ones"), s[:, T:T + P], False, False, skip_group_check=True)
                mm(b[:, T:T + P], const("neg_from"), s[:, T:T + P], False, True, skip_group_check=True).then_inc(full_of("stick2", l, h), 1)

            def stick_values(l, h):
                wait_read(pe, "stick2", l, h)
                key = ("yc", l, h // 2)
                if h % 2 == 0:
                    wait_free(pe, *key)
                o, a = bank(*key)[half_rows(h), :], aT[:, h % 2, :]
                mm(o[:, 0:T], vc[:, 0, h * HEAD:(h + 1) * HEAD], a[:, 0:T], True, False, skip_group_check=True)
                last = mm(o[:, P:T], vc[:, 1, h * HEAD:(h + 1) * HEAD], a[:, T:T + P], False, True, skip_group_check=True)
                last.then_inc(stick_av if h % 2 == 0 else full_of(*key), 1)

            def softmax_head_products(l, t):
                nk = P * (t + 1)
                if t == 0:
                    wait_read(pe, "tr", l, 2)
                    wait_read(pe, "tr", l, 3)
                    wait_read(pe, "kT", l)
                for i, h in enumerate(LOGIT_ORDER):
                    b, at, ends = logit_place(t, i)
                    if at == 0:
                        wait_free(pe, "logit", l, t, b)
                    r = half_rows(h)
                    last = mm(ps[:, b, at:at + nk], qT[r, h // 2, t * P:(t + 1) * P], kT[r, 0:nk], True, True)
                    if ends:
                        last.then_inc(full[b], 1)
                for kt in range(t + 1):
                    for b in (0, 1):
                        if kt == 0:
                            pe.wait_ge(prob_done, 2 * (TT * l + t) + b + 1)
                        wait_free(pe, "pT", l, t, kt, b)
                        for i in range(3):
                            at = (3 * b + i) * nk + kt * P
                            last = pe.transpose(ps[:, b, i * P:(i + 1) * P], lg[:, at:at + P], ident)
                        last.then_inc(full[b], 1)
                wait_free(pe, "av", l, t)
                for b in (0, 1):
                    wait_read(pe, "pT", l, t, t, b)
                for i, h in enumerate(LOGIT_ORDER):
                    for kt in range(t + 1):
                        last = mm(bank("av", l, t)[half_rows(h), (h // 2) * P:(h // 2 + 1) * P],
                                  va[:, kt, :], pT[:, kt, i * P:(i + 1) * P], kt == 0, kt == t)
                last.then_inc(full_of("av", l, t), 1)

            def unit(name, e):
                un = unit_of((None, name), e)
                e = e if name == "moe" else 0

                def gate_up(ch):
                    w = F_CHUNKS[ch][1]
                    for half, kind in enumerate(("gate", "up")):
                        wait_split(pe, (kind, name, ch), e)
                        wt = pair_tile((kind, name, ch), w)
                        for r in range(w // P):
                            f = 2 * ch + r
                            if half == 0 and not (name == 0 and ch == 0):
                                pe.wait_ge(hid_done, count(un, NCH, ch - 1 + r))
                            for k in range(KD):
                                if name == 0 and ch == 0 and half == 0 and r == 0:
                                    wait_h(0, 1, k)
                                last = mm3(ps[:, f % 3, half * T:(half + 1) * T], [x[:, k, r * P:(r + 1) * P] for x in wt],
                                           tokens(k, slice(0, T)), k == 0, k == KD - 1)
                        last.then_inc(up_used if half else gate_used, 1)

                def down(ch):
                    n = F_CHUNKS[ch][1] // P
                    wait_split(pe, ("down", name, ch), e)
                    w = pair_tile(("down", name, ch), D, n)
                    pe.wait_ge(hid_low, count(un, NCH, ch + 1))
                    if ch == 0:
                        for b in range(4):
                            if name == "moe":
                                pe.wait_ge(free[4 + b], e + MOE_FIRST[4 + b])
                            else:
                                wait_free(pe, "down", name, b)
                    for r in range(n):
                        for b in range(4):
                            t, half = b // 2, b % 2
                            h = [x[:, ch % 2, r * T + t * P:r * T + (t + 1) * P] for x in (hidh, hidl)]
                            last = mm3(ps[:, 4 + b, :], h, [x[:, r, half * 512:(half + 1) * 512] for x in w],
                                       ch == 0 and r == 0, ch == NCH - 1 and r == n - 1)
                            if ch == NCH - 1:
                                last.then_inc(full[4 + b], 1)
                    if ch < NCH - 1:
                        last.then_inc(down_used, 1)

                for ch in range(NCH):
                    if name != "moe":
                        for a in ada_of_step(name * NCH + ch - 1):
                            ada_product(1, a)
                    gate_up(ch)
                    if ch > 0:
                        down(ch - 1)
                down(NCH - 1)

            def gather(e):
                pe.wait_ge(sel_ready, e + 1)
                for k in range(KD):
                    for t in range(TT):
                        last = mm(ps[:, k // 4, (k % 4) * P:(k % 4 + 1) * P], xn[:, t, k * P:(k + 1) * P], sel[:, t, :], t == 0, t == 1)
                last.then_inc(gathered, 1)

            def few_tokens(e):
                un = (e, DENSE_UNITS)

                def products(kind, ch):
                    w, half = F_CHUNKS[ch][1], int(kind == "up")
                    wait_split(pe, (kind, "moe", ch), e)
                    wt = pair_tile((kind, "moe", ch), w)
                    for k in range(KD):
                        last = mm3(ps[:, ch % 2, half * 256:half * 256 + w], (xgh[:, k, :], xgl[:, k, :]), [x[:, k, :] for x in wt], k == 0, k == KD - 1)
                    last.then_inc(up_used if half else gate_used, 1)

                def turn_hidden(ch):
                    pe.wait_ge(hid_done, count(un, NCH, ch + 1))
                    for r in range(F_CHUNKS[ch][1] // P):
                        last = pe.transpose(ps[:, 2, r * P:(r + 1) * P], hid[:, r * P:(r + 1) * P], ident)
                    last.then_inc(few_turned, 1)

                def down(ch):
                    n = F_CHUNKS[ch][1] // P
                    wait_split(pe, ("down", "moe", ch), e)
                    w = pair_tile(("down", "moe", ch), D, n)
                    pe.wait_ge(hid_low, count(un, NCH, ch + 1))
                    if ch == 0:
                        pe.wait_ge(free[7], e + MOE_FIRST[7])
                    for half, b in enumerate((3, 7)):
                        for r in range(n):
                            last = mm3(ps[:, b, :], [x[:, ch % 2, r * P:(r + 1) * P] for x in (hidh, hidl)],
                                       [x[:, r, half * 512:(half + 1) * 512] for x in w], ch == 0 and r == 0, ch == NCH - 1 and r == n - 1)
                        if ch == NCH - 1:
                            last.then_inc(few_sum, 1)
                    if ch < NCH - 1:
                        last.then_inc(down_used, 1)

                for ch in range(NCH):
                    pe.wait_ge(hid_done, count(un, NCH, ch - 1))
                    products("gate", ch)
                    if ch > 0:
                        turn_hidden(ch - 1)
                    products("up", ch)
                    if ch > 0:
                        down(ch - 1)
                turn_hidden(NCH - 1)
                gather(e + 1)
                down(NCH - 1)
                for half in range(2):
                    pe.wait_ge(few_yg, 2 * e + half + 1)
                    for t in range(TT):
                        b = 4 + 2 * t + half
                        pe.wait_ge(free[b], e + MOE_FIRST[b])
                        mm(ps[:, b, :], selT[:, t * P:(t + 1) * P], yg[:, half * 512:(half + 1) * 512], True, True).then_inc(full[b], 1)

            def wait_h(l, which, k):
                if k % 2 == 0:
                    pe.wait_ge(hT_low, 4 * (2 * l + which) + k // 2 + 1)

            pe.wait_ge(consts_loaded, 32)
            pe.wait_ge(cond_done, 1)
            for l in range(DEPTH):
                if l == 0:
                    for a in range(BY_TENSOR + 1):
                        if a < BY_TENSOR:
                            ada_row(a)
                        if a > 0:
                            ada_product(0, a - 1)
                pe.wait_ge(xn_done, 4 * l + 2)
                transpose_x("xT", l)
                for j, (c0, w) in enumerate(W_IN_SLOTS):
                    wait_split(pe, ("in", l, j))
                    wait_free(pe, "in", l, j)
                    wt, b = pair_tile(("in", l, j), w), bank("in", l, j)
                    for m in range(2):
                        for k in range(KD):
                            if j == 0 and m == 0:
                                wait_h(l, 0, k)
                            if j <= 4 or j == 7:
                                last = mm3(b[:, m * 256:m * 256 + w], tokens(k, slice(m * P, (m + 1) * P)), [x[:, k, :] for x in wt], k == 0, k == KD - 1)
                            else:
                                last = mm3(b[:, m * T:(m + 1) * T], [x[:, k, m * P:(m + 1) * P] for x in wt], tokens(k, slice(0, T)), k == 0, k == KD - 1)
                    last.then_inc(full_of("in", l, j), 1)
                    if l == 0:
                        for a in ada_beside(j - 1):
                            ada_product(0, a)
                    if j == 7:
                        transposes(l)
                        pe.wait_ge(small_loaded, SMALL)
                    if j == 9:
                        indexer(l)
                    if j == 10:
                        latent_and_pool(l)
                    if 13 <= j < 13 + HC:
                        stick_values(l, j - 13)
                    if 12 <= j < 12 + HC:
                        stick_sums(l, j - 12)
                    if 11 <= j < 11 + HC:
                        stick_logits(l, j - 11)
                if l == 0:
                    for a in ada_beside(NIN - 1):
                        ada_product(0, a)
                for t in range(TT):
                    softmax_head_products(l, t)

                for t in range(TT):
                    wait_read(pe, "av", l, t)
                wait_read(pe, "yb", l)
                wait_read(pe, "yc", l, 1)
                branches = [[(("br", l, 0), 2, 0, yaT[:, 0, :]), (("br", l, 0), 2, 1, yaT[:, 1, :]), (("br", l, 1), 1, 0, yaT[:, 2, :])],
                            [(("br", l, 2), 2, k, ybT[:, k, :]) for k in range(2)],
                            [(("br", l, 3), 2, k, ycT[:, k, :]) for k in range(2)]]
                for i, parts in enumerate(branches):
                    for n_part, (key, n, k, y) in enumerate(parts):
                        first, final = n_part == 0, n_part == len(parts) - 1
                        wait_loaded(pe, key)
                        for m in range(4):
                            if first:
                                wait_free(pe, "br", l, i, m)
                            for half in range(2):
                                d0 = (2 * m + half) * P
                                last = mm(bank("br", l, i, m)[:, half * T:(half + 1) * T], w_tile(key, D, n)[:, k, d0:d0 + P], y,
                                          first and half == 0, final and half == 1, skip_group_check=True)
                            if final:
                                last.then_inc(full_of("br", l, i, m), 1)
                        if key[2] == 0 and k == 1:
                            last.then_inc(br_used, 1)
                for b in range(4):
                    wait_free(pe, "y", l, b)
                for j in range(4):
                    wait_split(pe, ("out", l, j))
                    pe.wait_ge(merged, 4 * l + j + 1)
                    w = pair_tile(("out", l, j), D, 2)
                    for b in range(4):
                        t, half = b // 2, b % 2
                        for k in range(2):
                            last = mm3(ps[:, b, :], tokens(2 * j + k, slice(t * P, (t + 1) * P)),
                                       [x[:, k, half * 512:(half + 1) * 512] for x in w], j == 0 and k == 0, j == 3 and k == 1)
                        if j == 3:
                            last.then_inc(full[b], 1)
                    if j < 3:
                        last.then_inc(out_used, 1)

                pe.wait_ge(xn_done, 4 * l + 4)
                transpose_x("hT", l)
                if l == 0:
                    for u in range(DENSE_UNITS):
                        unit(u, u)
                    for a in ada_of_step(DENSE_UNITS * NCH - 1):
                        ada_product(1, a)
                else:
                    wait_free(pe, "route", l)
                    for t in range(TT):
                        for k in range(KD):
                            wait_h(l, 1, k)
                            for i, h in enumerate(tokens(k, slice(t * P, (t + 1) * P))):
                                last = mm(bank("route", l)[:, t * E:(t + 1) * E], h.bitcast(F32), wroute[:, k, :], k == 0 and i == 0, k == KD - 1 and i == 1)
                    last.then_inc(full_of("route", l), 1)
                    pe.wait_ge(picked_done, 1)
                    o = bank("count", l)
                    for t in range(TT):
                        if t == 1:
                            mm(o[:, E:2 * E], ones, picked[:, 0, :], True, False)
                        mm(o[:, t * E:(t + 1) * E], const("earlier"), picked[:, t, :], t == 0, True)
                    for t in range(TT):
                        last = mm(o[:, 2 * E:3 * E], ones, picked[:, t, :], t == 0, t == 1)
                    last.then_inc(full_of("count", l), 1)
                    gather(0)
                    wait_read(pe, "count", 1)
                    with pe.Fori(0, E) as e:
                        pe.wait_ge(xg_ready, e + 1)
                        for t in range(TT):
                            last = pe.transpose(ps[:, 3, t * P:(t + 1) * P], sel[:, t, :], ident)
                        last.then_inc(sel_turned, 1)
                        pe.wait_ge(selT_ready, e + 1)
                        with pe.If(has_many(pe, e)):
                            unit("moe", e)
                            gather(e + 1)
                            stand_in(pe, [(few_turned, NCH), (few_sum, 2)])
                        with pe.Else():
                            few_tokens(e)

        @block.scalar
        def _(act):
            chain = [0]

            def link(ins):
                chain[0] += 1
                ins.then_inc(a_chain, 1)
                act.wait_ge(a_chain, chain[0])

            def squares(n, t, src, junk):
                act.activation(junk, src, ACT.Square, accum_out=ss[:, n, t:t + 1]).then_inc(ss_done, 1)

            def guess_rstd(n):
                act.wait_ge(var_done, n + 1)
                link(act.activation(guess[:, n, :], var[:, n, :], ACT.Ln))
                act.activation(guess[:, n, :], guess[:, n, :], ACT.Exp, scale=-0.5).then_inc(guess_done, 1)

            def modulate(name, l, which):
                for j in (1, 3):
                    wait_full(act, name, l, j)
                    for m in range(2):
                        k = 2 * j + m
                        last = act.activation(hraw[:, j, m * T:(m + 1) * T], bank(name, l, j)[:, m * T:(m + 1) * T], ACT.Identity,
                                              scale=modc[:, l, 2 * which + 1, k:k + 1], bias=modc[:, l, 2 * which, k:k + 1])
                    last.then_inc(free_of(name, l, j), 1)
                    for i in (j - 1, j):
                        wait_read(act, name, l, i)
                        act.activation(hTh[:, 2 * i:2 * i + 2, :].rearrange("p a t -> p (a t)"), hraw[:, i, :], ACT.Copy).then_inc(hT_high, 1)

            def high_part(key, e=0):
                n = SPLITS.index(key)
                wait_loaded(act, key, e * TURNS if key[1] == "moe" else 0)
                if key[1] == "moe" and n - NP >= SPLIT0:
                    wait_used(act, SPLITS[n - NP], e)
                elif key[1] == "moe" and not isinstance(e, int):
                    wait_used(act, SPLITS[n - NP + UNIT], e - 1)
                elif n >= NP:
                    wait_used(act, SPLITS[n - NP])
                act.activation(high_of(key), ring[:, slot(key), 0:width(key)], ACT.Copy).then_inc(high, 1)

            def high_after(key, e=0):
                high_part(SPLITS[SPLITS.index(key) + NP], e)

            def walk(name, e, few=False):
                un = unit_of((None, name), e)
                e = e if name == "moe" else 0
                for i, (kind, ch) in enumerate(ORDER):
                    w = F_CHUNKS[ch][1]
                    if few and (kind == "gate" and ch > 0 or i == UNIT - 1):
                        turned = ch - 1 if kind == "gate" else ch
                        n = F_CHUNKS[turned][1]
                        act.wait_ge(few_turned, e * NCH + turned + 1)
                        act.activation(hidh[:, turned % 2, 0:n], ps[:, 2, 0:n], ACT.Copy).then_inc(hid_high, 1)
                    if kind == "up":
                        act.wait_ge(up_used, count(un, NCH, ch + 1))
                        if few:
                            last = act.activation(sig[:, 0:w], ps[:, ch % 2, 0:w], ACT.Sigmoid)
                        else:
                            for r in range(w // P):
                                last = act.activation(sig[:, r * T:(r + 1) * T], ps[:, (2 * ch + r) % 3, 0:T], ACT.Sigmoid)
                        last.then_inc(sig_done, 1)
                    if name != "moe" or i + NP < UNIT:
                        high_after((kind, name, ch), e)
                    if kind == "up" and not few:
                        n = w // P * T
                        act.wait_ge(hid_done, count(un, NCH, ch + 1))
                        act.activation(hidh[:, ch % 2, 0:n], hid[:, 0:n], ACT.Copy).then_inc(hid_high, 1)

            def high_next(e, items):
                with act.If(e < E - 1):
                    for i in items:
                        high_part(SPLITS[SPLIT0 + i], e + 1)

            def copy_out(key, dst, src, scale=1.0):
                wait_full(act, *key)
                act.activation(dst, src, ACT.Copy, scale=scale).then_inc(free_of(*key), 1)

            def pairs(b, w=256, n=2, step=256):
                return b[:, 0:n * step].rearrange("p (m n) -> p m n", m=n)[:, :, 0:w]

            act.wait_ge(c_loaded, 16)
            act.activation(cond[:, :], c_col[:, :], ACT.Sigmoid).then_inc(cond_sig, 1)
            for l in range(DEPTH):
                if l == 0:
                    act.wait_ge(x_loaded, 16)
                for t in range(TT):
                    if l > 0:
                        act.wait_ge(x_added, TT * (2 * l - 1) + t + 1)
                    squares(5 * l, t, x[:, t, :], xn[:, t, :])
                guess_rstd(5 * l)
                if l == 0:
                    for a in range(BY_TENSOR):
                        copy_out(("adarow", a), acc[0:1, a % NACC, :], bank("adarow", a)[0:1, 0:256])
                if l == 0:
                    high_part(SPLITS[0])
                    high_part(SPLITS[1])
                for a in range(8):
                    wait_read(act, *ada_job(l, a))
                modulate("xT", l, 0)
                if l == 0:
                    high_part(SPLITS[2])
                if l == 0:
                    act.wait_ge(angles, 1)
                    act.activation(cs[:, :, :, :], red[:, :, :, :], ACT.Sin).then_inc(tables, 1)
                for j in range(20):
                    key = ("in", l, j)
                    b = bank(*key)
                    if j < 5:
                        c0, w = W_IN_SLOTS[j]
                        copy_out(key, natP[:, :, c0:c0 + w], pairs(b, w))
                        if j == 1:
                            act.wait_ge(free_of(*key), ORD[key] + 1)
                            for t in range(TT):
                                squares(5 * l + 1, t, natP[:, t, C_LAT:C_LAT + LAT], latn[:, t, :])
                            guess_rstd(5 * l + 1)
                    elif j == 5:
                        copy_out(key, qkc[:, 0:2, :], pairs(b), HEAD ** -0.5)
                    elif j == 6:
                        copy_out(key, qkc[:, 2:4, :], pairs(b))
                    elif j == 7:
                        copy_out(key, vc[:, :, :], pairs(b))
                    else:
                        copy_out(key, gT[:, 2 * (j - 8):2 * (j - 8) + 2, :], pairs(b))
                    if j < NIN - 1:
                        high_after(key)
                    if j == 7:
                        act.wait_ge(small_loaded, SMALL)
                        copy_out(("tr", l, 0), trs[:, 0:4, :], pairs(bank("tr", l, 0), P, 4, P))
                        wait_full(act, "tr", l, 1)
                        act.activation(trs[:, 4:6, :], pairs(bank("tr", l, 1), P, 2, P), ACT.Copy)
                        act.activation(trs[:, 6:8, :], pairs(bank("tr", l, 1)[:, T:], P, 2, P), ACT.Copy,
                                       scale=glat[:, l:l + 1]).then_inc(free_of("tr", l, 1), 1)
                        copy_out(("tr", l, 2), qT[:, 0:2, :], pairs(bank("tr", l, 2)))
                        copy_out(("tr", l, 3), qT[:, 2, :], bank("tr", l, 3)[:, 0:T])
                    if j == 9:
                        for t in range(TT):
                            nk = P * (t + 1)
                            for par in range(2):
                                wait_full(act, "idx", l, t, par)
                                act.activation(relu_at(t, par), bank("idx", l, t, par)[:, 0:2 * nk], ACT.Relu)\
                                   .then_inc(free_of("idx", l, t, par), 1)
                    if j == 10:
                        wait_full(act, "ukv", l)
                        u = pairs(bank("ukv", l), NOPE + HEAD, 2, P)
                        act.wait_ge(q_ready, l + 1)
                        act.activation(kn[:, :, ROPE:HEAD], u[:, :, 0:NOPE], ACT.Copy)
                        act.activation(kn[:, :, HEAD + ROPE:P], u[:, :, 0:NOPE], ACT.Copy)
                        act.activation(va[:, :, :], u[:, :, NOPE:NOPE + HEAD], ACT.Copy).then_inc(free_of("ukv", l), 1)
                        copy_out(("pool", l), poolT[:, :, :], pairs(bank("pool", l)))
                        copy_out(("kT", l), kT[:, :], bank("kT", l)[:, 0:T])
                        wait_full(act, "yb", l)
                        for g in range(2):
                            last = act.activation(ybT[:, g, :], bank("yb", l)[:, g * T:(g + 1) * T], ACT.Copy, scale=pscale[:, l, g:g + 1])
                        last.then_inc(free_of("yb", l), 1)
                    if 12 <= j < 12 + HC:
                        h = j - 12
                        wait_full(act, "stick2", l, h)
                        act.activation(aT[:, h % 2, :], bank("stick2", l, h)[:, 0:384], ACT.Exp).then_inc(free_of("stick2", l, h), 1)
                    if 11 <= j < 11 + HC:
                        h = j - 11
                        wait_full(act, "stick", l, h)
                        s = spl[:, h % 2, :]
                        act.activation(s, bank("stick", l, h)[:, 0:384], ACT.Abs).then_inc(stick_abs, 1)
                        act.wait_ge(stick_abs, HC * l + h + 1)
                        link(act.activation(s, s, ACT.Exp, scale=-1.0))
                        act.activation(s, s, ACT.Ln, bias=1.0).then_inc(stick_log, 1)
                wait_read(act, "in", l, NIN - 1)
                act.activation(big[:, :], big[:, :], ACT.Sigmoid).then_inc(gates_done, 1)
                for t in range(TT):
                    nk = P * (t + 1)
                    act.wait_ge(max_done, TT * l + t + 1)
                    for i in range(HA):
                        s = lg[:, i * nk:(i + 1) * nk]
                        last = act.activation(s, s, ACT.Exp, bias=nmax[:, l, t, i:i + 1], accum_out=psum_exp[:, l, t, i:i + 1])
                    last.then_inc(exp_done, 1)
                    for kt in range(t + 1):
                        copy_out(("pT", l, t, kt, 1), pT[:, kt, 3 * P:6 * P], bank("pT", l, t, kt, 1)[:, 0:3 * P])
                    copy_out(("av", l, t), yaT[:, :, t * P:(t + 1) * P], pairs(bank("av", l, t), P, 3, P))
                high_part(("out", l, 2))
                for m in range(4):
                    act.wait_ge(merged_raw, 4 * l + m + 1)
                    act.activation(hTh[:, 2 * m:2 * m + 2, :].rearrange("p a t -> p (a t)"), mraw[:, m % 2, :], ACT.Copy).then_inc(merged_high, 1)
                for j in range(3):
                    high_after(("out", l, j))
                for t in range(TT):
                    wait_full(act, "y", l, 2 * t)
                    wait_full(act, "y", l, 2 * t + 1)
                    squares(5 * l + 2, t, ps[:, 2 * t:2 * t + 2, :].rearrange("p a b -> p (a b)"), xn[:, t, :])
                guess_rstd(5 * l + 2)
                high_after(("out", l, 3))
                for t in range(TT):
                    act.wait_ge(x_added, TT * 2 * l + t + 1)
                    squares(5 * l + 3, t, x[:, t, :], xn[:, t, :])
                guess_rstd(5 * l + 3)
                for a in range(12, 20):
                    wait_read(act, *ada_job(l, a))
                modulate("hT", l, 1)
                if l == 0:
                    for u in range(DENSE_UNITS):
                        walk(u, u)
                else:
                    act.wait_ge(route_d, 1)
                    act.activation(rsm[:, 5, 0:TT], rsm[:, 4, 0:TT], ACT.Exp).then_inc(route_e, 1)

                    def gathered_high(e):
                        for half in range(2):
                            act.wait_ge(xraw_ready, 2 * e + half + 1)
                            act.activation(xgh[:, 4 * half:4 * half + 4, :].rearrange("p k s -> p (k s)"), xraw[:, half * 512:(half + 1) * 512], ACT.Copy)\
                               .then_inc(xg_high, 1)

                    gathered_high(0)
                    wait_read(act, "count", 1)
                    with act.Fori(0, E) as e:
                        act.wait_ge(sel_turned, e + 1)
                        act.activation(selT, ps[:, 3, 0:T], ACT.Copy).then_inc(selT_ready, 1)
                        with act.If(has_many(act, e)):
                            walk("moe", e)
                        with act.Else():
                            walk("moe", e, few=True)
                        high_next(e, [0])
                        gathered_high(e + 1)
                        high_next(e, [1, 2])
                for t in range(TT):
                    if l == 0:
                        wait_read(act, "down", DENSE_UNITS - 1, 2 * t)
                        wait_read(act, "down", DENSE_UNITS - 1, 2 * t + 1)
                    else:
                        act.wait_ge(free[4 + 2 * t], MOE_FIRST[4 + 2 * t] + E)
                        act.wait_ge(free[5 + 2 * t], MOE_FIRST[5 + 2 * t] + E)
                    squares(5 * l + 4, t, yacc[:, t, :], xn[:, t, :])
                guess_rstd(5 * l + 4)

        @block.vector
        def _(dve):
            chain = [0]

            def link(ins):
                chain[0] += 1
                ins.then_inc(v_chain, 1)
                dve.wait_ge(v_chain, chain[0])

            def finish_rstd(n, width):
                dve.wait_ge(ss_done, TT * (n + 1))
                dve.tensor_scalar(var[:, n, :], ss[:, n, :], 1.0 / width, EPS, ALU.mult, ALU.add).then_inc(var_done, 1)
                dve.wait_ge(guess_done, n + 1)
                g = guess[:, n, :]
                link(dve.tensor_tensor(newt[:, 0, :], g, g, ALU.mult))
                link(dve.tensor_tensor(newt[:, 1, :], newt[:, 0, :], var[:, n, :], ALU.mult))
                link(dve.tensor_scalar(newt[:, 0, :], newt[:, 1, :], -0.5, 1.5, ALU.mult, ALU.add))
                link(dve.tensor_tensor(rstd[:, n, :], g, newt[:, 0, :], ALU.mult))

            def normalize_x(n):
                finish_rstd(n, D)
                for t in range(TT):
                    dve.tensor_scalar(xn[:, t, :], x[:, t, :], rstd[:, n, t:t + 1], None, ALU.mult).then_inc(xn_done, 1)

            def modulate(name, l, which):
                for j in (0, 2):
                    wait_full(dve, name, l, j)
                    for m in range(2):
                        k = 2 * j + m
                        last = dve.tensor_scalar(hraw[:, j, m * T:(m + 1) * T], bank(name, l, j)[:, m * T:(m + 1) * T],
                                                 modc[:, l, 2 * which + 1, k:k + 1], modc[:, l, 2 * which, k:k + 1], ALU.mult, ALU.add)
                    last.then_inc(free_of(name, l, j), 1)
                for j in range(4):
                    dve.wait_ge(hT_high, 4 * (2 * l + which) + j + 1)
                    h = [x[:, 2 * j:2 * j + 2, :].rearrange("p a t -> p (a t)") for x in (hTh, hTl)]
                    dve.tensor_tensor(h[1], hraw[:, j, :], h[0].bitcast(F32), ALU.subtract).then_inc(hT_low, 1)

            def ada_sum(l, a):
                n = ada_index(l, a)
                if n >= NACC:
                    wait_full(dve, *ada_job((n - NACC) // NADA, (n - NACC) % NADA))
                wait_loaded(dve, ("ada", l, a))
                w = ring[:, slot(("ada", l, a)), :].rearrange("p (k n) -> p k n", k=KD)
                o = acc[:, n % NACC, :]
                for k in range(KD):
                    if k == 0:
                        i = dve.tensor_scalar(o, w[:, k, :], cond[:, k:k + 1], None, ALU.mult)
                    else:
                        i = dve.scalar_tensor_tensor(out=o, in0=w[:, k, :], scalar=cond[:, k:k + 1], in1=o, op0=ALU.mult, op1=ALU.add)
                    if k < KD - 1:
                        link(i)
                    else:
                        i.then_inc(acc_done, 1)

            def ada_read(l, a):
                seg, q = a // 4, a % 4
                wait_full(dve, *ada_job(l, a))
                b = ada_bank(l, a)
                if seg in (2, 5):
                    g = GTG[(l, seg)]
                    dve.wait_ge(gain_loaded[g], 16 * ROWS[(l, seg)])
                    r = gtg[:, g, 256 * q:256 * (q + 1)]
                    i = dve.tensor_tensor(r, b[:, 0:256], r, ALU.mult)
                else:
                    which = 0 if seg < 2 else 1
                    scale = seg in (1, 4)
                    o = modc[:, l, 2 * which + scale, 2 * q:2 * q + 2]
                    if scale:
                        i = dve.scalar_tensor_tensor(out=o, in0=b[:, 0:2], scalar=1.0, in1=gcol[:, l, which, 2 * q:2 * q + 2],
                                                     op0=ALU.add, op1=ALU.mult)
                    else:
                        i = dve.tensor_copy(o, b[:, 0:2])
                if l == 0 or a % 2:
                    i.then_inc(free_of(*ada_job(l, a)), 1)

            def rope(view, heads):
                def tab(i):
                    return cs[:, :, i:i + 1, :].to_broadcast([P, TT, heads, HALF])
                x1, x2 = view[:, :, :, 0:HALF], view[:, :, :, HALF:ROPE]
                r = [rot[:, i, 0:TT * heads * HALF].rearrange("p (t h c) -> p t h c", t=TT, h=heads) for i in range(4)]
                dve.tensor_tensor(r[0], x1, tab(0), ALU.mult)
                dve.tensor_tensor(r[1], x2, tab(1), ALU.mult)
                dve.tensor_tensor(r[2], x2, tab(0), ALU.mult)
                link(dve.tensor_tensor(r[3], x1, tab(1), ALU.mult))
                dve.tensor_tensor(x1, r[0], r[1], ALU.subtract)
                return dve.tensor_tensor(x2, r[2], r[3], ALU.add)

            def heads_view(c0, n, w=HEAD):
                return natP[:, :, c0:c0 + n * w].rearrange("p t (h c) -> p t h c", h=n)

            def choose(l, t):
                nk = P * (t + 1)
                s, tk = score[:, t, 0:nk], take[:, t, 0:nk]
                for i, h in enumerate((0, 1, 2, 3)):
                    wait_read(dve, "idx", l, t, h % 2)
                    r = relu_at(t, h % 2)[:, (h // 2) * nk:(h // 2 + 1) * nk]
                    w = natP[:, t, C_WI + h:C_WI + h + 1]
                    if i == 0:
                        link(dve.tensor_scalar(s, r, w, None, ALU.mult))
                    else:
                        link(dve.scalar_tensor_tensor(out=s, in0=r, scalar=w, in1=s, op0=ALU.mult, op1=ALU.add))
                diag = score[:, t, nk - P:nk]
                link(dve.tensor_tensor(diag, diag, const("not_causal"), ALU.add))
                for _ in range(TOPK // 8):
                    link(dve.max(top8[:, :], s))
                    link(dve.match_replace(s, top8[:, :], s, TAKEN))
                link(dve.tensor_scalar(tk, s, TAKEN, None, ALU.is_equal))
                diag = take[:, t, nk - P:nk]
                link(dve.tensor_tensor(diag, diag, const("causal"), ALU.mult))
                link(dve.tensor_scalar(tk, tk, -FAR, FAR, ALU.mult, ALU.add))

            def stick(l, h):
                dve.wait_ge(stick_abs, HC * l + h + 1)
                r, s = rel[:, h % 2, :], spl[:, h % 2, :]
                dve.tensor_scalar(r, bank("stick", l, h)[:, 0:384], 0.0, None, ALU.max).then_inc(free_of("stick", l, h), 1)
                dve.wait_ge(free_of("stick", l, h), ORD[("stick", l, h)] + 1)
                dve.wait_ge(stick_log, HC * l + h + 1)
                dve.tensor_tensor(s, r, s, ALU.add).then_inc(stick_sp, 1)

            def softmax(l, t):
                nk = P * (t + 1)
                for b in ([4, 5] if t == 0 else [4, 5, 6, 7]):
                    idx = [i for i in range(HA) if logit_place(t, i)[0] == b]
                    wait_full(dve, "logit", l, t, b)
                    n = len(idx)
                    o = lg[:, idx[0] * nk:(idx[0] + n) * nk].rearrange("p (h k) -> p h k", h=n)
                    i = ps[:, b, 0:n * nk].rearrange("p (h k) -> p h k", h=n)
                    dve.scalar_tensor_tensor(out=o, in0=i, scalar=HEAD ** -0.5, in1=take[:, t:t + 1, 0:nk].to_broadcast([P, n, nk]),
                                             op0=ALU.mult, op1=ALU.add).then_inc(free[b], 1)
                    dve.wait_ge(free[b], ORD[("logit", l, t, b)] + 1)
                v = lg[:, 0:HA * nk].rearrange("p (h k) -> p h k", h=HA)
                dve.tensor_reduce(nmax[:, l, t, :], v, AX.X, ALU.max, negate=True).then_inc(max_done, 1)
                dve.wait_ge(exp_done, TT * l + t + 1)
                link(dve.reciprocal(pinv[:, l, t, :], psum_exp[:, l, t, :]))
                for half in range(2):
                    o = v[:, 3 * half:3 * half + 3, :]
                    dve.tensor_tensor(o, o, pinv[:, l, t, 3 * half:3 * half + 3].unsqueeze(2).to_broadcast([P, 3, nk]), ALU.mult)\
                       .then_inc(prob_done, 1)
                for kt in range(t + 1):
                    wait_full(dve, "pT", l, t, kt, 0)
                    dve.tensor_copy(pT[:, kt, 0:3 * P], bank("pT", l, t, kt, 0)[:, 0:3 * P]).then_inc(free_of("pT", l, t, kt, 0), 1)

            def merge(l):
                def gate(i, m):
                    return gT[:, 8 * i + 2 * m:8 * i + 2 * m + 2, :].rearrange("p a t -> p (a t)")

                def low_merged(m):
                    dve.wait_ge(merged_high, 4 * l + m + 1)
                    h = [x[:, 2 * m:2 * m + 2, :].rearrange("p a t -> p (a t)") for x in (hTh, hTl)]
                    dve.tensor_tensor(h[1], mraw[:, m % 2, :], h[0].bitcast(F32), ALU.subtract).then_inc(merged, 1)

                dve.wait_ge(gates_done, l + 1)
                for i in range(3):
                    for m in range(4):
                        wait_full(dve, "br", l, i, m)
                        dve.tensor_tensor(gate(i, m), bank("br", l, i, m), gate(i, m), ALU.mult).then_inc(free_of("br", l, i, m), 1)
                        if i > 0:
                            wait_read(dve, "br", l, i, m)
                        if i == 1:
                            link(dve.tensor_tensor(gate(0, m), gate(0, m), gate(1, m), ALU.add))
                        if i == 2:
                            if m > 1:
                                dve.wait_ge(merged, 4 * l + m - 1)
                            dve.tensor_tensor(mraw[:, m % 2, :], gate(0, m), gate(2, m), ALU.add).then_inc(merged_raw, 1)
                            if m > 0:
                                low_merged(m - 1)
                low_merged(3)

            def add_residual(n, t, halves, g):
                for half, (src, raises) in enumerate(halves):
                    c = slice(512 * half, 512 * half + 512)
                    i = dve.scalar_tensor_tensor(out=resid[:, c], in0=src, scalar=rstd[:, n, t:t + 1], in1=gtg[:, g, c],
                                                 op0=ALU.mult, op1=ALU.mult)
                    if raises is None:
                        link(i)
                    else:
                        i.then_inc(raises[0], 1)
                        dve.wait_ge(*raises)
                dve.tensor_tensor(x[:, t, :], x[:, t, :], resid, ALU.add).then_inc(x_added, 1)
                dve.wait_ge(x_added, TT * ((n // 5) * 2 + (1 if n % 5 == 4 else 0)) + t + 1)

            def route():
                wait_full(dve, "route", 1)
                lgt = rsm[:, 0, :]
                link_free = dve.tensor_copy(lgt, bank("route", 1)[:, 0:TT * E])
                link_free.then_inc(free_of("route", 1), 1)
                wait_read(dve, "route", 1)
                l3 = lgt.rearrange("p (t e) -> p t e", t=TT)
                v4 = [rout[:, i, :].rearrange("p (t e o) -> p t e o", t=TT, e=E) for i in range(2)]
                other = l3.unsqueeze(2).to_broadcast([P, TT, E, E])
                own = l3.unsqueeze(3).to_broadcast([P, TT, E, E])
                early = const("earlier8").rearrange("p (a e o) -> p a e o", a=1, e=E).to_broadcast([P, TT, E, E])
                dve.tensor_tensor(v4[0], other, own, ALU.is_gt)
                link(dve.tensor_tensor(v4[1], other, own, ALU.is_equal))
                link(dve.tensor_tensor(v4[1], v4[1], early, ALU.mult))
                link(dve.tensor_tensor(v4[0], v4[0], v4[1], ALU.add))
                rank = rsm[:, 1, :]
                link(dve.tensor_reduce(rank, v4[0].rearrange("p t e o -> p (t e) o"), AX.X, ALU.add))
                pick = [rsm[:, 2 + i, :] for i in range(2)]
                for i in range(2):
                    link(dve.tensor_scalar(pick[i], rank, float(i), None, ALU.is_equal))
                both = [rout[:, 2, TT * E * i:TT * E * (i + 1)] for i in range(2)]
                vals = rout[:, 2, 4 * TT * E:4 * TT * E + 2 * TT].rearrange("p (i t) -> p i t", i=2)
                for i in range(2):
                    if i == 0:
                        dve.tensor_tensor(picked[:, :, :].rearrange("p t e -> p (t e)"), pick[0], pick[1], ALU.add).then_inc(picked_done, 1)
                    link(dve.tensor_tensor(both[i], pick[i], lgt, ALU.mult))
                    link(dve.tensor_reduce(vals[:, i, :], both[i].rearrange("p (t e) -> p t e", t=TT), AX.X, ALU.add))
                dve.tensor_tensor(rsm[:, 4, 0:TT], vals[:, 1, :], vals[:, 0, :], ALU.subtract).then_inc(route_d, 1)
                dve.wait_ge(route_e, 1)
                e2, p1, p2 = rsm[:, 5, 0:TT], rsm[:, 5, TT:2 * TT], rsm[:, 5, 2 * TT:3 * TT]
                link(dve.tensor_scalar(p2, e2, 1.0, None, ALU.add))
                link(dve.reciprocal(p1, p2))
                link(dve.tensor_tensor(p2, e2, p1, ALU.mult))
                for i, p in enumerate((p1, p2)):
                    link(dve.tensor_tensor(both[i].rearrange("p (t e) -> p t e", t=TT), pick[i].rearrange("p (t e) -> p t e", t=TT),
                                           p.unsqueeze(2).to_broadcast([P, TT, E]), ALU.mult))
                link(dve.tensor_tensor(comb[:, :, :], both[0].rearrange("p (t e) -> p t e", t=TT),
                                       both[1].rearrange("p (t e) -> p t e", t=TT), ALU.add))
                wait_full(dve, "count", 1)
                before = bank("count", 1)[:, 0:TT * E].rearrange("p (t e) -> p t e", t=TT)
                own = place_of[:, :, 0:E]
                link(dve.scalar_tensor_tensor(out=own, in0=before, scalar=1.0, in1=picked[:, :, :], op0=ALU.add, op1=ALU.mult))
                link(dve.tensor_scalar(own, own, -1.0, None, ALU.add))
                dve.tensor_copy(tokens_of[:, :], bank("count", 1)[:, 2 * E:3 * E]).then_inc(free_of("count", 1), 1)

            def select(e):
                for t in range(TT):
                    last = dve.tensor_scalar(sel[:, t, :], const("place"), place_of[:, t, bass.ds(e, 1)] if not isinstance(e, int) else place_of[:, t, e:e + 1],
                                             None, ALU.is_equal)
                last.then_inc(sel_ready, 1)

            def hidden(un, ch, few=False):
                w = F_CHUNKS[ch][1]
                dve.wait_ge(sig_done, count(un, NCH, ch + 1))
                if few:
                    tiles = [(ps[:, ch % 2, 0:w], ps[:, ch % 2, 256:256 + w], slice(0, w))]
                else:
                    tiles = [(ps[:, (2 * ch + r) % 3, 0:T], ps[:, (2 * ch + r) % 3, T:2 * T], slice(r * T, (r + 1) * T)) for r in range(w // P)]
                for g, _, c in tiles:
                    last = dve.tensor_tensor(gsig[:, c], g, sig[:, c], ALU.mult)
                last.then_inc(gate_prod, 1)
                dve.wait_ge(gate_prod, count(un, NCH, ch + 1))
                for _, u, c in tiles:
                    last = dve.tensor_tensor(hid[:, c], u, gsig[:, c], ALU.mult)
                last.then_inc(hid_done, 1)

            def hidden_low(un, ch, few=False):
                w = F_CHUNKS[ch][1]
                n = w if few else w // P * T
                dve.wait_ge(hid_high, count(un, NCH, ch + 1))
                src = ps[:, 2, 0:n] if few else hid[:, 0:n]
                dve.tensor_tensor(hidl[:, ch % 2, 0:n], src, hidh[:, ch % 2, 0:n].bitcast(F32), ALU.subtract).then_inc(hid_low, 1)

            def gathered_raw(e):
                dve.wait_ge(gathered, e + 1)
                for k in range(KD):
                    last = dve.tensor_scalar(xraw[:, k * P:(k + 1) * P], ps[:, k // 4, (k % 4) * P:(k % 4 + 1) * P],
                                             modc[:, 1, 3, k:k + 1], modc[:, 1, 2, k:k + 1], ALU.mult, ALU.add)
                    if k % 4 == 3:
                        last.then_inc(xraw_ready, 1)

            def gathered_low(e):
                for half in range(2):
                    dve.wait_ge(xg_high, 2 * e + half + 1)
                    h = [x[:, 4 * half:4 * half + 4, :].rearrange("p k s -> p (k s)") for x in (xgh, xgl)]
                    last = dve.tensor_tensor(h[1], xraw[:, half * 512:(half + 1) * 512], h[0].bitcast(F32), ALU.subtract)
                last.then_inc(xg_ready, 1)

            def add_unit(b, e):
                t, half = b // 2, b % 2
                o = yacc[:, t, half * 512:(half + 1) * 512]
                dve.scalar_tensor_tensor(out=o, in0=ps[:, 4 + b, :], scalar=comb[:, t, bass.ds(e, 1)] if not isinstance(e, int) else comb[:, t, e:e + 1],
                                         in1=o, op0=ALU.mult, op1=ALU.add).then_inc(free[4 + b], 1)

            def reduce_angles():
                dve.wait_ge(consts_loaded, 32)
                link(dve.tensor_copy(pos_f[:, :], pos_i[:, :]))
                for t in range(TT):
                    link(dve.tensor_scalar(ang[:, t, :], const("inv_freq"), pos_f[:, t:t + 1], None, ALU.mult))
                for i, quarter in enumerate((0.25, 0.0)):
                    link(dve.tensor_scalar(turns[:, :, i, :], ang[:, :, :], 1.0 / (2.0 * np.pi), quarter, ALU.mult, ALU.add))
                link(dve.tensor_scalar(turns[:, :, :, :], turns[:, :, :, :], ROUNDER, None, ALU.add))
                link(dve.tensor_scalar(turns[:, :, :, :], turns[:, :, :, :], -ROUNDER, None, ALU.add))
                for i, shift in enumerate((np.pi / 2, 0.0)):
                    src = ang[:, :, :]
                    for part in TWO_PI:
                        link(dve.scalar_tensor_tensor(out=red[:, :, i, :], in0=turns[:, :, i, :], scalar=-part, in1=src, op0=ALU.mult, op1=ALU.add))
                        src = red[:, :, i, :]
                    link(dve.tensor_scalar(red[:, :, i, :], red[:, :, i, :], shift, None, ALU.add))
                dve.tensor_scalar(red[:, :, :, :], red[:, :, :, :], PI_BELOW, -PI_BELOW, ALU.min, ALU.max).then_inc(angles, 1)

            dve.wait_ge(cond_sig, 1)
            dve.tensor_tensor(cond[:, :], cond[:, :], c_col[:, :], ALU.mult).then_inc(cond_done, 1)
            dve.wait_ge(cond_done, 1)
            for l in range(DEPTH):
                def sum_beside(j):
                    if l == 0:
                        for a in ada_beside(j):
                            ada_sum(0, a)

                def read_beside(j):
                    if l == 0:
                        for a in ada_beside(j):
                            ada_read(0, a)

                normalize_x(5 * l)
                if l == 0:
                    dve.wait_ge(columns_loaded, 16 * len(cols))
                    for a in range(BY_TENSOR):
                        ada_read(0, a)
                modulate("xT", l, 0)
                if l == 0:
                    reduce_angles()
                sum_beside(0)
                sum_beside(1)
                dve.wait_ge(tables, 1)
                read_beside(0)
                wait_read(dve, "in", l, 1)
                finish_rstd(5 * l + 1, LAT)
                for t in range(TT):
                    last = dve.tensor_scalar(latn[:, t, :], natP[:, t, C_LAT:C_LAT + LAT], rstd[:, 5 * l + 1, t:t + 1], None, ALU.mult)
                last.then_inc(lat_ready, 1)
                link(rope(heads_view(C_QA, HA), HA))
                sum_beside(2)
                read_beside(1)
                wait_read(dve, "in", l, 2)
                link(rope(natP[:, :, C_KR:C_KR + ROPE].unsqueeze(2), 1))
                dve.tensor_copy(kn[:, :, 0:ROPE], natP[:, :, C_KR:C_KR + ROPE])
                dve.tensor_copy(kn[:, :, HEAD:HEAD + ROPE], natP[:, :, C_KR:C_KR + ROPE]).then_inc(q_ready, 1)
                sum_beside(3)
                read_beside(2)
                wait_read(dve, "in", l, 3)
                link(rope(heads_view(C_QI, HI + 1), HI + 1))
                dve.tensor_copy(ki[:, :, 0:HEAD], natP[:, :, C_KI:C_KI + HEAD])
                dve.tensor_copy(ki[:, :, HEAD:P], natP[:, :, C_KI:C_KI + HEAD]).then_inc(qi_ready, 1)
                for j in range(4, 9):
                    sum_beside(j)
                    read_beside(j - 1)
                for t in range(TT):
                    choose(l, t)
                sum_beside(11)
                sum_beside(12)
                for j in range(11, NIN):
                    if j > 11:
                        sum_beside(j + 1)
                    if 11 <= j < 11 + HC:
                        stick(l, j - 11)
                    read_beside(j - 1)
                    if 13 <= j < 13 + HC and j % 2 == 0:
                        g = (j - 14) // 2
                        wait_full(dve, "yc", l, g)
                        dve.tensor_copy(ycT[:, g, :], bank("yc", l, g)[:, 0:T]).then_inc(free_of("yc", l, g), 1)
                read_beside(NIN - 1)
                for t in range(TT):
                    softmax(l, t)
                merge(l)
                lower_part(dve, "vector", ("gate", 0 if l == 0 else "moe", 0))
                if l == 1:
                    lower_part(dve, "vector", ("up", "moe", 0))
                finish_rstd(5 * l + 2, D)
                for t in range(TT):
                    add_residual(5 * l + 2, t, [(ps[:, 2 * t + h, :], (free[2 * t + h], ORD[("y", l, 2 * t + h)] + 1)) for h in range(2)], GTG[(l, 2)])
                normalize_x(5 * l + 3)
                modulate("hT", l, 1)
                dve.wait_ge(acc0, l + 1)
                if l == 0:
                    for u in range(DENSE_UNITS):
                        for ch in range(NCH):
                            n = u * NCH + ch
                            for a in ada_of_step(n):
                                ada_sum(1, a)
                            if ch < NCH - 1:
                                lower_part(dve, "vector", ("gate", u, ch + 1))
                            hidden((u, 0), ch)
                            for a in ada_of_step(n - 1):
                                ada_read(1, a)
                            hidden_low((u, 0), ch)
                        if u < DENSE_UNITS - 1:
                            lower_part(dve, "vector", ("gate", u + 1, 0))
                        for b in range(4):
                            wait_full(dve, "down", u, b)
                            add_unit(b, u)
                    for a in ada_of_step(DENSE_UNITS * NCH - 1):
                        ada_read(1, a)
                else:
                    link(dve.memset(place_of[:, :, E:E + 1], -1.0))
                    route()
                    wait_read(dve, "count", 1)
                    select(0)
                    gathered_raw(0)
                    gathered_low(0)
                    with dve.Fori(0, E) as e:
                        un = (e, DENSE_UNITS)

                        dve.wait_ge(sel_turned, e + 1)
                        select(e + 1)
                        with dve.If(has_many(dve, e)):
                            for ch in range(NCH):
                                if ch < NCH - 1:
                                    lower_part(dve, "vector", ("gate", "moe", ch + 1), e)
                                hidden(un, ch)
                                if ch < NCH - 1:
                                    lower_part(dve, "vector", ("up", "moe", ch + 1), e)
                                hidden_low(un, ch)
                                lower_part(dve, "vector", ("down", "moe", ch), e)
                            gathered_raw(e + 1)
                            gathered_low(e + 1)
                            stand_in(dve, [(few_yg, 2)])
                        with dve.Else():
                            for ch in range(NCH):
                                if ch > 0:
                                    hidden_low(un, ch - 1, few=True)
                                if ch < NCH - 1:
                                    lower_part(dve, "vector", ("gate", "moe", ch + 1), e)
                                hidden(un, ch, few=True)
                                if ch < NCH - 1:
                                    lower_part(dve, "vector", ("up", "moe", ch + 1), e)
                                lower_part(dve, "vector", ("down", "moe", ch), e)
                            hidden_low(un, NCH - 1, few=True)
                            gathered_raw(e + 1)
                            gathered_low(e + 1)
                            for half, b in enumerate((3, 7)):
                                dve.wait_ge(few_sum, 2 * e + half + 1)
                                dve.tensor_copy(yg[:, half * 512:(half + 1) * 512], ps[:, b, :]).then_inc(few_yg, 1)
                        with dve.If(e < E - 1):
                            for kind in ("gate", "up"):
                                lower_part(dve, "vector", (kind, "moe", 0), e + 1)
                        for b in range(4):
                            dve.wait_ge(full[4 + b], e + MOE_FIRST[4 + b] + 1)
                            add_unit(b, e)
                finish_rstd(5 * l + 4, D)
                for t in range(TT):
                    add_residual(5 * l + 4, t, [(yacc[:, t, 512 * h:512 * h + 512], None) for h in range(2)], GTG[(l, 5)])


_NAMES = ["x", "c", "positions", "w_ada", "b_ada", "norm_gains", "w_in", "g_kv_latent", "w_uk", "w_uv", "w_pool",
          "pool_scale", "w_br_a", "w_br_b", "w_br_c", "w_out", "w_gate_dense", "w_up_dense", "w_down_dense",
          "w_router", "w_gate_moe", "w_up_moe", "w_down_moe"]


def kernel(**inputs):
    import concourse.bacc as bacc
    from concourse.bass_utils import run_bass_kernel_spmd

    nc = bacc.Bacc("TRN2", target_bir_lowering=False, num_devices=1)
    arrays, aps = {}, []
    consts, const_at = shape_constants()
    for name in _NAMES + ["consts"]:
        a = consts if name == "consts" else np.ascontiguousarray(inputs[name])
        arrays["in_" + name] = a
        aps.append(nc.dram_tensor("in_" + name, a.shape, mybir.dt.from_np(a.dtype), kind="ExternalInput").ap())
    y = nc.dram_tensor("y", inputs["x"].shape, F32, kind="ExternalOutput").ap()
    build_trunk(nc, *aps, const_at, y)
    r = run_bass_kernel_spmd(nc, [arrays], core_ids=[0])
    return r.results[0]["y"]
```

```python
from contextlib import ExitStack

import numpy as np
import concourse.bass as bass
from concourse import mybir

P = 128
F32 = mybir.dt.float32
F32R = mybir.dt.float32r
I32 = mybir.dt.int32
ALU = mybir.AluOpType
ACT = mybir.ActivationFunctionType
AX = mybir.AxisListType

HEAD = 64
ROPE = HEAD // 4
NOPE = HEAD - ROPE
HALF = ROPE // 2
THETA = 500000.0
WINDOWS = (2, 4, 8, 16)
TOPK = 64
EPS = 1e-6
NOT_CAUSAL = -3.0e38
TAKEN = -3.4e38
FAR = -1.0e30
ROUNDER = 1.5 * 2.0 ** 23
TWO_PI = (6.28125, 0.0019354820251464844, -1.7484556025237907e-07)
PI_BELOW = 3.1415925


def shape_constants():
    r = np.arange(P)
    row, col = r[:, None], r[None, :]
    parts = {
        "ident": (row == col).astype(np.float32),
        "ones": np.ones((P, P), np.float32),
        "neg_from": -(row >= col).astype(np.float32),
        "neg_ones": -np.ones((P, P), np.float32),
        "before": np.where(row < col, 0.0, FAR).astype(np.float32),
        "causal": (col <= row).astype(np.float32),
        "not_causal": np.where(col <= row, 0.0, NOT_CAUSAL).astype(np.float32),
        "earlier": (row < col).astype(np.float32),
        "place": np.broadcast_to(np.arange(P, dtype=np.float32)[None, :], (P, P)),
        "inv_freq": np.broadcast_to((np.float32(THETA) ** (-np.arange(0, ROPE, 2, dtype=np.float32) / np.float32(ROPE)))[None, :], (P, HALF)).astype(np.float32),
    }
    e = np.arange(8)
    parts["earlier8"] = np.broadcast_to((e[None, :] < e[:, None]).astype(np.float32).reshape(1, 64), (P, 64))
    t = np.arange(2 * P)[None, :]
    for st in range(2):
        s = r[:, None] + P * st
        for g, w in enumerate(WINDOWS):
            inside = (s <= t) & (s > t - w)
            band = np.where(inside, np.float32(1) / np.minimum(t + 1, w).astype(np.float32), np.float32(0))
            parts[f"band{st}{g}"] = (band - (s == t)).astype(np.float32)
    at, offsets = 0, {}
    for name, a in parts.items():
        offsets[name] = (at, a.shape[1])
        at += a.shape[1]
    return np.ascontiguousarray(np.concatenate(list(parts.values()), axis=1)), offsets


def build_trunk(nc, x_in, c, positions, w_ada, b_ada, norm_gains, w_in, g_kv_latent, w_uk, w_uv,
                w_pool, pool_scale, w_br_a, w_br_b, w_br_c, w_out, w_gate_dense, w_up_dense,
                w_down_dense, w_router, w_gate_moe, w_up_moe, w_down_moe, consts, const_at, out):
    DEPTH, D, _ = w_in.shape
    T = x_in.shape[1]
    TT = T // P
    KD = D // P
    WA, WB, WC = w_br_a.shape[1], w_br_b.shape[1], w_br_c.shape[1]
    LAT = w_uk.shape[1]
    HA, HC = WA // HEAD, WC // HEAD
    E, _, FE = w_gate_moe.shape[1:]
    FF = w_gate_dense.shape[2]
    HI = 4
    assert TT == 2 and DEPTH == 2 and FF % FE == 0 and LAT == P and WB == 256 and WC == 256

    C_QA, C_LAT = 0, WA
    C_KR = C_LAT + LAT
    C_QI = C_KR + ROPE
    C_KI = C_QI + HI * HEAD
    C_WI = C_KI + HEAD
    C_U = C_WI + HI
    C_QC = C_U + WB
    C_KC = C_QC + WC
    C_VC = C_KC + WC
    C_G = C_VC + WC
    NATW = C_QC

    NS, NP, SLOTW = 6, 3, KD * 256
    W_IN_SLOTS = [(0, 256), (256, 256), (512, 256), (768, C_U - 768), (C_U, 256), (C_QC, 256),
                  (C_KC, 256), (C_VC, 256)] + [(C_G + 256 * j, 256) for j in range(3 * D // 256)]
    NIN = len(W_IN_SLOTS)
    NADA = 6 * D // 256
    F_CHUNKS = [(256 * j, min(256, FE - 256 * j)) for j in range((FE + 255) // 256)]
    UNIT = 3 * len(F_CHUNKS)
    assert UNIT % NS == 0
    DENSE_UNITS = FF // FE

    NCH = len(F_CHUNKS)
    ORDER = [("gate", 0), ("up", 0)]
    for ch in range(1, NCH):
        ORDER += [("gate", ch), ("up", ch), ("down", ch - 1)]
    ORDER.append(("down", NCH - 1))

    def ada_beside(j):
        return (8 + j,) if 0 <= j < 8 else (16 + j - 12,) if 12 <= j < 20 else ()

    def mixer_slots(l):
        s = [("ada", 0, j) for j in range(8)] if l == 0 else []
        for j in range(NIN):
            s.append(("in", l, j))
            if l == 0:
                s += [("ada", 0, a) for a in ada_beside(j)]
        return s + [("br", l, 0), ("out", l, 0), ("out", l, 1), ("br", l, 1), ("br", l, 2), ("br", l, 3), ("out", l, 2), ("out", l, 3)]

    def dense_slots():
        s = []
        for u in range(DENSE_UNITS):
            for i, (kind, ch) in enumerate(ORDER):
                s.append((kind, u, ch))
                if i + 1 < len(ORDER) and ORDER[i + 1][0] == "gate" or i + 1 == len(ORDER):
                    n = u * NCH + ch + (1 if kind == "down" and i + 1 < len(ORDER) else 0)
                    s += [("ada", 1, 2 * n), ("ada", 1, 2 * n + 1)]
        return s

    LOADS = mixer_slots(0) + dense_slots() + mixer_slots(1)
    NUMBER = {key: n for n, key in enumerate(LOADS)}
    EXPERT0 = len(LOADS)
    TURNS = UNIT // NS

    def load_number(key):
        if key[1] == "moe":
            return EXPERT0 + ORDER.index((key[0], key[2]))
        return NUMBER[key]

    SPLITS = [key for key in LOADS if key[0] in ("in", "out", "gate", "up", "down")] + [(kind, "moe", ch) for kind, ch in ORDER]
    SPLIT0 = len(SPLITS) - UNIT
    def lower_by(key):
        if key[1] == "moe":
            return {"gpsimd": (0, 4), "vector": (4, KD)}
        return {"vector" if key[0] == "gate" else "gpsimd": (0, KD)}
    LOWERS = ("vector", "gpsimd")
    LOWER_NO = {(w, key): sum(w in lower_by(k) for k in SPLITS[:n + 1]) for n, key in enumerate(SPLITS) for w in LOWERS}
    LOWER_PER = {w: sum(w in lower_by((kind, "moe", ch)) for kind, ch in ORDER) for w in LOWERS}
    assert UNIT % NP == 0

    def ada_of_step(n):
        return (2 * n, 2 * n + 1) if n >= 0 else ()

    SOFTMAX = (15, 17)
    ROW_SUMS = (0, 1, 3, 4, 6)
    JOBS = []
    def job(bank, *key):
        JOBS.append((key, bank))
    job(7, "columns")
    for l in range(DEPTH):
        if l == 0:
            for a in range(9):
                if a in ROW_SUMS:
                    job(4 + ROW_SUMS.index(a) % 2, "adarow", a)
                if a > 0:
                    job(2 + (a - 1) % 2, "ada", 0, a - 1)
        for j in range(4):
            job(j, "xT", l, j)
        for j in range(NIN):
            job(j % 2, "in", l, j)
            if l == 0:
                for a in ada_beside(j - 1):
                    job(2 + a % 2, "ada", 0, a)
            if j == 7:
                for n in range(4):
                    job(4 + n, "tr", l, n)
            if j == 9:
                for t in range(TT):
                    for par in range(2):
                        job(4 + 2 * t + par, "idx", l, t, par)
            if j == 10:
                job(4, "ukv", l)
                job(5, "pool", l)
                job(4, "kT", l)
                job(5, "yb", l)
            if 13 <= j < 13 + HC and j % 2 == 1:
                job(6, "yc", l, (j - 13) // 2)
            if 12 <= j < 12 + HC:
                job(4 + (j - 12) % 2, "stick2", l, j - 12)
            if 11 <= j < 11 + HC:
                job(4 + (j - 11) % 2, "stick", l, j - 11)
            if j == SOFTMAX[0]:
                job(7, "logit", l, 0, 0)
                job(4, "logit", l, 0, 1)
            if j == SOFTMAX[0] + 1:
                job(7, "pT", l, 0, 0, 0)
                job(4, "pT", l, 0, 0, 1)
            if j == SOFTMAX[0] + 2:
                job(2, "av", l, 0)
            if j == SOFTMAX[1]:
                for g in range(4):
                    job(4 + g, "logit", l, 1, g)
            if j == SOFTMAX[1] + 2:
                for kt in range(2):
                    for half in range(2):
                        job(4 + 2 * kt + half, "pT", l, 1, kt, half)
        if l == 0:
            for a in ada_beside(NIN - 1):
                job(2 + a % 2, "ada", 0, a)
        job(2, "av", l, 1)
        for i in range(3):
            for m in range(4):
                job(4 + m if i != 1 else m, "br", l, i, m)
        for b in range(4):
            job(b, "y", l, b)
        for j in range(4):
            job(4 + j, "hT", l, j)
        if l == 1:
            job(2, "route", l)
            job(2, "count", l)
        if l == 0:
            for n in range(DENSE_UNITS * NCH):
                u, ch = n // NCH, n % NCH
                if n > 0:
                    job(3, "ada", 1, 2 * n - 2)
                if ch == NCH - 1:
                    for b in range(4):
                        job(4 + b, "down", u, b)
            job(3, "ada", 1, NADA - 2)
    seen, ORD, BANK = [0] * 8, {}, {}
    for key, bank_no in JOBS:
        assert key not in ORD, key
        ORD[key], BANK[key] = seen[bank_no], bank_no
        seen[bank_no] += 1
    MOE_FIRST = list(seen)
    assert F_CHUNKS[-1][1] == P and HC == 4 and NIN == 20 and NADA == 24 and NCH * DENSE_UNITS * 2 == NADA

    ctx = ExitStack()
    with ctx:
        def sb(name, shape, dt=F32):
            return ctx.enter_context(nc.sbuf_tensor(name, shape, dt))

        def sem(name):
            return ctx.enter_context(nc.semaphore(name))

        NACC = 3
        ps = ctx.enter_context(nc.psum_tensor("ps", [P, 8, 512], F32))
        with ExitStack() as under:
            wl = under.enter_context(nc.sbuf_tensor("wl", [P, NS, SLOTW], F32R))
        ring = sb("ring", [P, NS, SLOTW])
        wh = sb("wh", [P, NP, SLOTW], F32R)
        with ExitStack() as under:
            def lower(name, shape):
                return under.enter_context(nc.sbuf_tensor(name, shape, F32R))
            hidh, hidl = lower("hidh", [P, 2, 512]), lower("hidl", [P, 2, 512])
            xgh, xgl = lower("xgh", [P, KD, P]), lower("xgl", [P, KD, P])
            sel = lower("sel", [P, TT, P])
            selT = lower("selT", [P, T])
        natP = sb("natP", [P, TT, NATW])
        vc = sb("vc", [P, TT, WC])
        qkc = sb("qkc", [P, 4, T])
        trs = sb("trs", [P, 8, P])
        cst = sb("cst", [P, consts.shape[1]])
        x = sb("x", [P, TT, D])
        with ExitStack() as under:
            xnl = lower("xnl", [P, TT, D])
        xn = sb("xn", [P, TT, D])
        hTh, hTl = sb("hTh", [P, KD, T], F32R), sb("hTl", [P, KD, T], F32R)
        big = sb("big", [P, 24 * T])
        gT = big[:, :].rearrange("p (m t) -> p m t", t=T)
        yacc = big[:, 0:TT * D].rearrange("p (t d) -> p t d", t=TT)
        sig = big[:, TT * D:TT * D + 512]
        gsig = big[:, TT * D + 512:TT * D + 1024]
        hid = big[:, TT * D + 1024:TT * D + 1536]
        resid = big[:, TT * D + 1536:2 * TT * D + 1536].rearrange("p (t d) -> p t d", t=TT)
        xraw = big[:, 5 * D:6 * D]
        hraw = big[:, 4 * D:6 * D].rearrange("p (j n) -> p j n", j=4)
        gtg = sb("gtg", [P, 3, D])
        acc = sb("acc", [P, NACC, 256])
        with ExitStack() as under:
            xnh = lower("xnh", [P, TT, D])
            ygh, ygl = lower("ygh", [P, D]), lower("ygl", [P, D])
        qT = sb("qT", [P, 3, T])
        kT = sb("kT", [P, T])
        va = sb("va", [P, TT, HEAD])
        yaT = sb("yaT", [P, 3, T])
        ybT = sb("ybT", [P, 2, T])
        ycT = sb("ycT", [P, 2, T])
        pT = sb("pT", [P, 2, HA * P])
        multi = sb("multi", [P, 3, 512])
        poolT = pT[:, :, 0:T]
        mraw = pT[:, :, 0:512]
        spl = pT[:, 0, :].rearrange("p (b n) -> p b n", b=2)
        rel = multi[:, :, :].rearrange("p a b -> p (a b)")[:, 0:768].rearrange("p (b n) -> p b n", b=2)
        aT = pT[:, 1, :].rearrange("p (b n) -> p b n", b=2)
        flat = xn[:, :, :].rearrange("p t d -> p (t d)")
        def tiled(at, width):
            return flat[:, at:at + TT * width].rearrange("p (t n) -> p t n", t=TT)
        kn = tiled(0, P)
        ki = tiled(TT * P, P)
        latn = tiled(2 * TT * P, LAT)
        score = tiled(3 * TT * P, T)
        lg = flat[:, 0:HA * T]
        take = tiled(HA * T, T)
        GAINS = DEPTH * 2 * KD
        cols_as_rows = sb("cols_as_rows", [KD + GAINS, P])
        cond = sb("cond", [P, KD])
        pos_i = sb("pos_i", [P, TT], I32)
        pos_f = sb("pos_f", [P, TT])
        ang = sb("ang", [P, TT, HALF])
        turns = sb("turns", [P, TT, 2, HALF])
        red = sb("red", [P, TT, 2, HALF])
        cs = sb("cs", [P, TT, 2, HALF])
        rot = sb("rot", [P, 4, TT * 6 * HALF])
        gcol = sb("gcol", [P, DEPTH, 2, KD])
        modc = sb("modc", [P, DEPTH, 4, KD])
        bias = sb("bias", [NADA, DEPTH, 256])
        glat = sb("glat", [P, DEPTH])
        pscale = sb("pscale", [P, DEPTH, 2])
        wukv = sb("wukv", [P, DEPTH, NOPE + HEAD])
        wpool = sb("wpool", [P, DEPTH, 2, P])
        wroute = sb("wroute", [P, KD, E])
        comb = sb("comb", [P, TT, E])
        ss = sb("ss", [P, DEPTH * 5, TT])
        var = sb("var", [P, DEPTH * 5, TT])
        guess = sb("guess", [P, DEPTH * 5, TT])
        newt = sb("newt", [P, 2, TT])
        rstd = sb("rstd", [P, DEPTH * 5, TT])
        nmax = sb("nmax", [P, DEPTH, TT, HA])
        psum_exp = sb("psum_exp", [P, DEPTH, TT, HA])
        pinv = sb("pinv", [P, DEPTH, TT, HA])
        top8 = sb("top8", [P, 8])
        rout = multi[:, :, :].rearrange("p a b -> p (a b)")[:, 768:768 + 3 * TT * E * E].rearrange("p (a n) -> p a n", a=3)
        rsm = sb("rsm", [P, 6, TT * E])
        picked = sb("picked", [P, TT, E])
        place_of = sb("place_of", [P, TT, E + 1])
        tokens_of = sb("tokens_of", [P, E], I32)

        def const(name):
            at, n = const_at[name]
            return cst[:, at:at + n]

        ident, ones = const("ident"), const("ones")


        loaded = [sem(f"slot_loaded{i}") for i in range(NS)]
        full = [sem(f"bank_full{i}") for i in range(8)]
        free = [sem(f"bank_emptied{i}") for i in range(8)]
        x_loaded = sem("x_loaded")
        c_loaded = sem("c_loaded")
        positions_loaded = sem("positions_loaded")
        small_loaded = sem("small_loaded")
        gain_loaded = [sem(f"gain_loaded{i}") for i in range(3)]
        cond_done = sem("condition")
        consts_loaded = sem("consts_loaded")
        zeroed = sem("zeroed")
        acc_done = sem("ada_chunk_summed")
        cond_sig = sem("cond_sigmoid")
        angles = sem("angles_reduced")
        tables = sem("rope_tables")
        ss_done = sem("square_sums")
        var_done = sem("variances")
        guess_done = sem("variance_roots")
        xn_done = sem("x_normed")
        qi_ready = sem("indexer_ready")
        lat_ready = sem("latent_normed")
        q_ready = sem("q_and_k_rope_ready")
        stick_abs = sem("stick_abs")
        stick_log = sem("stick_log")
        stick_sp = sem("stick_softplus")
        stick_av = sem("stick_av")
        gates_done = sem("gates_done")
        max_done = sem("neg_max")
        exp_done = sem("exp_done")
        prob_done = sem("prob_done")
        high = sem("weights_high_parts")
        low = {w: sem("weights_low_parts_by_" + w) for w in ("vector", "gpsimd")}
        hT_high = sem("h_high_parts")
        hT_low = sem("h_low_parts")
        br_used = sem("first_branch_weights_used")
        merged_raw = sem("merged_unsplit")
        merged_high = sem("merged_high_parts")
        merged = sem("merged")
        out_used = sem("out_rows_used")
        x_added = sem("x_added")
        acc0 = sem("expert_sum_cleared")
        sig_done = sem("sigmoid_done")
        gate_prod = sem("gate_product")
        down_used = sem("down_rows_used")
        route_d = sem("route_difference")
        route_e = sem("route_exp")
        picked_done = sem("picked")
        sel_ready = sem("selection_ready")
        sel_turned = sem("selection_turned")
        selT_ready = sem("turned_selection_ready")
        gathered = sem("tokens_gathered")
        xg_ready = sem("gathered_tokens_ready")
        gate_used = sem("gate_weights_used")
        up_used = sem("up_weights_used")
        hid_done = sem("hidden_unsplit")
        hid_high = sem("hidden_high_parts")
        hid_low = sem("hidden_low_parts")
        few_turned = sem("few_hidden_turned")
        xraw_ready = sem("gathered_tokens_unsplit")
        xg_high = sem("gathered_tokens_high_parts")
        few_sum = sem("few_down_products")
        few_high = sem("few_result_high_parts")
        few_yg = sem("few_result_split")
        xn_high = sem("normed_x_high_parts")
        xn_low = sem("normed_x_low_parts")
        v_chain = sem("vector_chain")
        a_chain = sem("scalar_chain")
        stored = sem("stored")

        block = ctx.enter_context(nc.Block())

        def slot(key):
            return load_number(key) % NS

        def wait_loaded(eng, key, turn=0):
            n = load_number(key)
            eng.wait_ge(loaded[n % NS], turn * 16 + 16 * (n // NS + 1))

        def wait_full(eng, *key):
            eng.wait_ge(full[BANK[key]], ORD[key] + 1)

        def wait_free(eng, *key):
            if ORD[key]:
                eng.wait_ge(free[BANK[key]], ORD[key])

        def wait_read(eng, *key):
            eng.wait_ge(free[BANK[key]], ORD[key] + 1)

        def bank(*key):
            return ps[:, BANK[key], :]

        def full_of(*key):
            return full[BANK[key]]

        def free_of(*key):
            return free[BANK[key]]

        def sums_to(l, a):
            return l * NADA + a + 1 - len([r for r in ROW_SUMS if l or r < a])

        def ada_job(l, a):
            return ("ada", l, a - a % 2 if l else a)

        def ada_bank(l, a):
            b = bank(*ada_job(l, a))
            return b[:, 256:512] if l and a % 2 else b[:, 0:256]

        def ada_index(l, a):
            return l * NADA + a

        GTG = {(0, 2): 0, (0, 5): 1, (1, 2): 0, (1, 5): 2}
        ROWS = {(0, 2): 1, (0, 5): 1, (1, 2): 2, (1, 5): 1}
        LOGIT_ORDER = (0, 2, 4, 1, 3, 5)

        def logit_place(t, i):
            nk = P * (t + 1)
            return (i // 3, (i % 3) * nk) if t == 0 else (2 * (i // 3) + (i % 3) // 2, (i % 3 % 2) * nk)

        def logit_groups(t):
            return [[i for i in range(HA) if logit_place(t, i)[0] == g] for g in range(2 if t == 0 else 4)]

        def count(un, per, k):
            return un[0] * per + (un[1] * per + k)

        def unit_of(key, e=0):
            return (e, DENSE_UNITS) if key[1] == "moe" else (key[1], 0)

        def wait_used(eng, key, e=0):
            kind, l, j = key
            if kind == "ada" and l == 0 and j in ROW_SUMS:
                wait_full(eng, "adarow", j)
            elif kind == "ada":
                eng.wait_ge(acc_done, sums_to(l, j))
            elif kind == "in":
                wait_full(eng, "in", l, j)
            elif kind == "br" and j == 0:
                eng.wait_ge(br_used, l + 1)
            elif kind == "br":
                wait_full(eng, "br", l, j - 1, 3)
            elif kind == "out" and j < 3:
                eng.wait_ge(out_used, 3 * l + j + 1)
            elif kind == "out":
                wait_full(eng, "y", l, 3)
            elif kind == "gate":
                eng.wait_ge(gate_used, count(unit_of(key, e), NCH, j + 1))
            elif kind == "up":
                eng.wait_ge(up_used, count(unit_of(key, e), NCH, j + 1))
            elif j < NCH - 1:
                eng.wait_ge(down_used, count(unit_of(key, e), NCH - 1, j + 1))
            elif l == "moe":
                eng.wait_ge(full[7], e + MOE_FIRST[7] + 1)
            else:
                wait_full(eng, "down", l, 3)

        def wait_split(eng, key, e=0):
            for w in lower_by(key):
                eng.wait_ge(low[w], e * LOWER_PER[w] + LOWER_NO[(w, key)])

        def width(key):
            if key[0] == "in":
                return KD * W_IN_SLOTS[key[2]][1]
            return SLOTW if key[0] == "out" else KD * F_CHUNKS[key[2]][1]

        def high_of(key):
            return wh[:, SPLITS.index(key) % NP, 0:width(key)]

        def low_of(key):
            return wl[:, slot(key), 0:width(key)]

        def lower_part(eng, w, key, e=0):
            a, b = [x * width(key) // KD for x in lower_by(key)[w]]
            eng.wait_ge(high, e * UNIT + SPLITS.index(key) + 1)
            eng.tensor_tensor(low_of(key)[:, a:b], ring[:, slot(key), a:b], high_of(key)[:, a:b].bitcast(F32), ALU.subtract)\
               .then_inc(low[w], 1)

        def relu_at(t, par):
            nk = P * (t + 1)
            m = multi[:, :, :].rearrange("p a b -> p (a b)")
            at = par * 2 * nk if t == 0 else 512 + par * 2 * nk
            return m[:, at:at + 2 * nk]

        GATHER_AT = 2

        def stand_in(eng, signals):
            for s, n in signals:
                eng.sem_inc(s, n)

        def has_many(eng, e):
            return eng.value_load(tokens_of[0:1, bass.ds(e, 1)], min_val=0, max_val=T) > P

        FIRST = const_at["band00"][0]
        as_rows = [(cols_as_rows[0:KD, :], c[0])]
        small = [(cst[:, FIRST:], consts[:, FIRST:])]
        for l in range(DEPTH):
            for n in range(2):
                at = KD * (1 + 2 * l + n)
                as_rows.append((cols_as_rows[at:at + KD, :], norm_gains[l, 2 * n]))
            small.append((glat[:, l:l + 1], g_kv_latent[l].rearrange("(p a) -> p a", a=1)))
            small.append((pscale[:, l, :], pool_scale[l].rearrange("(k p) -> p k", p=P)))
            small.append((wukv[:, l, 0:NOPE], w_uk[l]))
            small.append((wukv[:, l, NOPE:NOPE + HEAD], w_uv[l]))
            for g in range(4):
                r = slice(HEAD * (g % 2), HEAD * (g % 2) + HEAD)
                small.append((wpool[r, l, g // 2, r], w_pool[l, g]))
        small.append((wroute[:, :, :], w_router[0].rearrange("(k p) e -> p k e", p=P)))
        SMALL = 16 * len(small)

        def gain_row(sp, l, seg):
            b = GTG[(l, seg)]
            row = norm_gains[l, 1 if seg == 2 else 3]
            sp.dma_start(gtg[:, b, :], row.rearrange("(a n) -> a n", a=1).to_broadcast([P, D])).then_inc(gain_loaded[b], 16)

        @block.sync
        def _(sp):
            def place(s, w, n=KD):
                return ring[:, s, 0:n * w].rearrange("p (k n) -> p k n", k=n)

            def columns(s, matrix, c0, w):
                return sp.dma_start(place(s, w), matrix[:, c0:c0 + w].rearrange("(k p) n -> p k n", p=P))

            def rows(s, matrix, r0, n):
                return sp.dma_start(place(s, D, n), matrix[r0:r0 + n * P, :].rearrange("(k p) n -> p k n", p=P))

            for dst, row in as_rows:
                sp.dma_start(dst, row.rearrange("(k p) -> k p", p=P)).then_inc(c_loaded, 16)
            sp.dma_start(cst[:, 0:FIRST], consts[:, 0:FIRST]).then_inc(consts_loaded, 16)
            sp.dma_start(bias[:, :, :], b_ada.rearrange("l (a n) -> a l n", a=NADA)).then_inc(consts_loaded, 16)
            for n, key in enumerate(LOADS):
                s = n % NS
                if n >= NS:
                    wait_used(sp, LOADS[n - NS])
                kind, l, j = key
                if kind == "ada":
                    d = columns(s, w_ada[l], 256 * j, 256)
                elif kind == "in":
                    d = columns(s, w_in[l], *W_IN_SLOTS[j])
                elif kind == "br":
                    m, r0, k = [(w_br_a, 0, 2), (w_br_a, 2 * P, 1), (w_br_b, 0, 2), (w_br_c, 0, 2)][j]
                    d = rows(s, m[l], r0, k)
                elif kind == "out":
                    d = rows(s, w_out[l], 2 * P * j, 2)
                elif kind == "down":
                    c0, w = F_CHUNKS[j]
                    d = rows(s, w_down_dense[0], FE * l + c0, w // P)
                else:
                    c0, w = F_CHUNKS[j]
                    d = columns(s, (w_gate_dense if kind == "gate" else w_up_dense)[0], FE * l + c0, w)
                d.then_inc(loaded[s], 16)
                if key == ("in", 0, 1):
                    gain_row(sp, 0, 2)
                    sp.wait_ge(zeroed, 2)
                    for dst, src in small:
                        sp.dma_start(dst, src, allow_slow_non_contiguous=True).then_inc(small_loaded, 16)
                if key == ("in", 0, 6):
                    gain_row(sp, 0, 5)
                    gain_row(sp, 1, 5)
                if key == ("gate", 0, 3):
                    sp.wait_ge(x_added, TT)
                    gain_row(sp, 1, 2)

            def expert_load(i, e):
                kind, ch = ORDER[i]
                c0, w = F_CHUNKS[ch]
                s = slot((kind, "moe", ch))
                if kind == "down":
                    src = w_down_moe[0].rearrange("e f n -> (e f) n")[bass.ds(e * FE + c0, w), :]
                    dst = place(s, D, w // P)
                else:
                    m = w_gate_moe if kind == "gate" else w_up_moe
                    src = m[0].rearrange("e d f -> (e d) f")[bass.ds(e * D, D), c0:c0 + w]
                    dst = place(s, w)
                sp.dma_start(dst, src.rearrange("(k p) n -> p k n", p=P)).then_inc(loaded[s], 16)

            def moe_key(i):
                kind, ch = ORDER[i]
                return kind, "moe", ch

            for i in range(NS):
                wait_used(sp, LOADS[EXPERT0 + i - NS])
                expert_load(i, 0)
            with sp.Fori(0, E - 1) as e:
                for i in range(NS, UNIT):
                    wait_used(sp, moe_key(i - NS), e)
                    expert_load(i, e)
                for i in range(NS):
                    wait_used(sp, moe_key(i - NS), e)
                    expert_load(i, e + 1)
            for i in range(NS, UNIT):
                wait_used(sp, moe_key(i - NS), E - 1)
                expert_load(i, E - 1)

            for t in range(TT):
                sp.wait_ge(x_added, TT * (2 * DEPTH - 1) + t + 1)
                sp.dma_start(out[0, t * P:(t + 1) * P, :], x[:, t, :]).then_inc(stored, 16)
            sp.wait_ge(stored, 16 * TT)

        @block.gpsimd
        def _(pool):
            pool.dma_start(x[:, :, :], x_in[0].rearrange("(t p) d -> p t d", p=P)).then_inc(x_loaded, 16)
            pool.dma_start(pos_i[:, :], positions[0].rearrange("(t p) -> p t", p=P), allow_slow_non_contiguous=True).then_inc(positions_loaded, 16)
            pool.memset(wpool[:, :, :, :], 0.0).then_inc(zeroed, 1)
            pool.memset(comb[:, :, :], 1.0).then_inc(zeroed, 1)
            def clear_expert_sum(l):
                pool.wait_ge(merged, 4 * l + 4)
                pool.memset(yacc, 0.0).then_inc(acc0, 1)

            def lower_parts(keys):
                for key in keys:
                    if "gpsimd" in lower_by(key):
                        lower_part(pool, "gpsimd", key)

            for l in range(DEPTH):
                lower_parts([("in", l, j) for j in range(NIN)] + [("out", l, j) for j in range(4)])
                clear_expert_sum(l)
                if l == 0:
                    for u in range(DENSE_UNITS):
                        lower_parts([(kind, u, ch) for kind, ch in ORDER])
            with pool.Fori(0, E) as e:
                for kind, ch in ORDER:
                    lower_part(pool, "gpsimd", (kind, "moe", ch), e)

        @block.tensor
        def _(pe):
            def mm(o, a, b, start, stop, **kw):
                return pe.matmul(o, a, b, start=start, stop=stop, **kw)

            def w_tile(key, w, n=KD):
                return ring[:, slot(key), 0:n * w].rearrange("p (k n) -> p k n", k=n)

            def pair_tile(key, w, n=KD):
                return [t[:, 0:n * w].rearrange("p (k n) -> p k n", k=n) for t in (high_of(key), low_of(key))]

            def mm3(o, a, b, start, stop, **kw):
                mm(o, a[0], b[0], start, False, **kw)
                mm(o, a[0], b[1], False, False, **kw)
                return mm(o, a[1], b[0], False, stop, **kw)

            def tokens(k, cols):
                return hTh[:, k, cols], hTl[:, k, cols]

            def half_rows(h):
                return slice(HEAD * (h % 2), HEAD * (h % 2) + HEAD)

            def ada_product(l, a):
                n = ada_index(l, a)
                pick = ident[0:NADA, a:a + 1]
                if l == 0 or a % 2 == 0:
                    wait_free(pe, *ada_job(l, a))
                b = ada_bank(l, a)
                if l == 0 and a in ROW_SUMS:
                    wait_read(pe, "adarow", a)
                    for m in range(2):
                        last = mm(b[:, m:m + 1], acc[0:1, a % NACC, m * P:(m + 1) * P], ones[0:1, 0:1], True, True)
                    last.then_inc(full_of("ada", l, a), 1)
                    return
                pe.wait_ge(acc_done, sums_to(l, a))
                if a // 4 in (2, 5):
                    mm(b[:, 0:256], ones, acc[:, n % NACC, :], True, False)
                    last = mm(b[:, 0:256], pick.to_broadcast([NADA, P]), bias[:, l, :], False, True)
                else:
                    for m in range(2):
                        cols = slice(m * P, (m + 1) * P)
                        mm(b[:, m:m + 1], acc[:, n % NACC, cols], ones[:, 0:1], True, False)
                        last = mm(b[:, m:m + 1], bias[:, l, cols], pick, False, True)
                if l == 0 or a % 2:
                    last.then_inc(full_of(*ada_job(l, a)), 1)

            def ada_row(a):
                wait_loaded(pe, ("ada", 0, a))
                wait_free(pe, "adarow", a)
                w, o = w_tile(("ada", 0, a), 256), bank("adarow", a)[0:1, 0:256]
                for k in range(KD):
                    mm(o, cond[:, k:k + 1], w[:, k, :], k == 0, False)
                mm(o, ident[0:NADA, a:a + 1], bias[:, 0, :], False, True).then_inc(full_of("adarow", a), 1)

            def transpose_x(name, l):
                for t in range(TT):
                    pe.wait_ge(xn_done, TT * (2 * l + (name == "hT")) + t + 1)
                    for j in range(4):
                        if t == 0:
                            wait_free(pe, name, l, j)
                        for i in range(2):
                            k = 2 * j + i
                            last = pe.transpose(bank(name, l, j)[:, (2 * i + t) * P:(2 * i + t + 1) * P], xn[:, t, k * P:(k + 1) * P], ident)
                        if t == TT - 1:
                            last.then_inc(full_of(name, l, j), 1)

            def transposes(l):
                groups = [[natP[:, t, C_QI + P * h:C_QI + P * (h + 1)] for h in range(2) for t in range(TT)],
                          [ki[:, t, :] for t in range(TT)] + [latn[:, t, :] for t in range(TT)],
                          [natP[:, t, P * h:P * (h + 1)] for h in range(2) for t in range(TT)],
                          [natP[:, t, 2 * P:3 * P] for t in range(TT)]]
                ready = [qi_ready, lat_ready, q_ready, q_ready]
                for n, group in enumerate(groups):
                    pe.wait_ge(ready[n], l + 1)
                    wait_free(pe, "tr", l, n)
                    for i, src in enumerate(group):
                        last = pe.transpose(bank("tr", l, n)[:, i * P:(i + 1) * P], src, ident)
                    last.then_inc(full_of("tr", l, n), 1)

            def indexer(l):
                wait_read(pe, "tr", l, 0)
                wait_read(pe, "tr", l, 1)
                keys = trs[:, 4:6, :].rearrange("p a b -> p (a b)")
                for t in range(TT):
                    nk = P * (t + 1)
                    for par in range(2):
                        wait_free(pe, "idx", l, t, par)
                        r = half_rows(par)
                        for h in range(2):
                            last = mm(bank("idx", l, t, par)[:, h * nk:(h + 1) * nk], trs[r, 2 * h + t, :], keys[r, 0:nk], True, True)
                        last.then_inc(full_of("idx", l, t, par), 1)

            def latent_and_pool(l):
                wait_free(pe, "ukv", l)
                for t in range(TT):
                    last = mm(bank("ukv", l)[:, t * P:t * P + NOPE + HEAD], trs[:, 6 + t, :], wukv[:, l, :], True, True)
                last.then_inc(full_of("ukv", l), 1)
                wait_read(pe, "in", l, 4)
                wait_free(pe, "pool", l)
                for g in range(4):
                    for s in range(TT):
                        last = mm(bank("pool", l)[half_rows(g), (g // 2) * T:(g // 2 + 1) * T],
                                  natP[:, s, C_U + HEAD * g:C_U + HEAD * (g + 1)], const(f"band{s}{g}"), s == 0, s == 1)
                last.then_inc(full_of("pool", l), 1)
                wait_read(pe, "ukv", l)
                wait_free(pe, "kT", l)
                for t in range(TT):
                    last = pe.transpose(bank("kT", l)[:, t * P:(t + 1) * P], kn[:, t, :], ident)
                last.then_inc(full_of("kT", l), 1)
                wait_read(pe, "pool", l)
                wait_free(pe, "yb", l)
                for g in range(2):
                    last = mm(bank("yb", l)[:, g * T:(g + 1) * T], wpool[:, l, g, :], poolT[:, g, :], True, True)
                last.then_inc(full_of("yb", l), 1)

            def stick_logits(l, h):
                if h == 0:
                    wait_read(pe, "in", l, 5)
                    wait_read(pe, "in", l, 6)
                    wait_read(pe, "in", l, 7)
                wait_free(pe, "stick", l, h)
                b, r, ft = bank("stick", l, h), half_rows(h), h // 2
                mm(b[:, 0:T], qkc[r, 2 + ft, 0:P], qkc[r, ft, :], True, False, skip_group_check=True)
                mm(b[:, T:T + P], qkc[r, 2 + ft, P:T], qkc[r, ft, P:T], False, False, skip_group_check=True)
                mm(b[:, 0:P], ident, const("before"), False, False, skip_group_check=True)
                mm(b[:, T:T + P], ident, const("before"), False, True, skip_group_check=True).then_inc(full_of("stick", l, h), 1)

            def stick_sums(l, h):
                pe.wait_ge(stick_sp, HC * l + h + 1)
                wait_free(pe, "stick2", l, h)
                b, s = bank("stick2", l, h), spl[:, h % 2, :]
                mm(b[:, 0:T], const("neg_from"), s[:, 0:T], False, False, skip_group_check=True)
                mm(b[:, P:T], const("neg_ones"), s[:, T:T + P], False, False, skip_group_check=True)
                mm(b[:, T:T + P], const("neg_from"), s[:, T:T + P], False, True, skip_group_check=True).then_inc(full_of("stick2", l, h), 1)

            def stick_values(l, h):
                wait_read(pe, "stick2", l, h)
                key = ("yc", l, h // 2)
                if h % 2 == 0:
                    wait_free(pe, *key)
                o, a = bank(*key)[half_rows(h), :], aT[:, h % 2, :]
                mm(o[:, 0:T], vc[:, 0, h * HEAD:(h + 1) * HEAD], a[:, 0:T], True, False, skip_group_check=True)
                last = mm(o[:, P:T], vc[:, 1, h * HEAD:(h + 1) * HEAD], a[:, T:T + P], False, True, skip_group_check=True)
                last.then_inc(stick_av if h % 2 == 0 else full_of(*key), 1)

            def logits(l, t):
                nk = P * (t + 1)
                if t == 0:
                    wait_read(pe, "tr", l, 2)
                    wait_read(pe, "tr", l, 3)
                    wait_read(pe, "kT", l)
                for g, heads in enumerate(logit_groups(t)):
                    wait_free(pe, "logit", l, t, g)
                    for i in heads:
                        h, at = LOGIT_ORDER[i], logit_place(t, i)[1]
                        r = half_rows(h)
                        last = mm(bank("logit", l, t, g)[:, at:at + nk], qT[r, h // 2, t * P:(t + 1) * P], kT[r, 0:nk], True, True)
                    last.then_inc(full_of("logit", l, t, g), 1)

            def turn_probabilities(l, t):
                nk = P * (t + 1)
                for kt in range(t + 1):
                    for half in (0, 1):
                        if kt == 0:
                            pe.wait_ge(prob_done, 2 * (TT * l + t) + half + 1)
                        wait_free(pe, "pT", l, t, kt, half)
                        for i in range(3):
                            at = (3 * half + i) * nk + kt * P
                            last = pe.transpose(bank("pT", l, t, kt, half)[:, i * P:(i + 1) * P], lg[:, at:at + P], ident)
                        last.then_inc(full_of("pT", l, t, kt, half), 1)

            def weigh_values(l, t):
                wait_free(pe, "av", l, t)
                for kt in range(t + 1):
                    for half in (0, 1):
                        wait_read(pe, "pT", l, t, kt, half)
                for i, h in enumerate(LOGIT_ORDER):
                    for kt in range(t + 1):
                        last = mm(bank("av", l, t)[half_rows(h), (h // 2) * P:(h // 2 + 1) * P],
                                  va[:, kt, :], pT[:, kt, i * P:(i + 1) * P], kt == 0, kt == t)
                last.then_inc(full_of("av", l, t), 1)

            def unit(name, e):
                un = unit_of((None, name), e)
                e = e if name == "moe" else 0

                def gate_up(ch):
                    w = F_CHUNKS[ch][1]
                    for half, kind in enumerate(("gate", "up")):
                        wait_split(pe, (kind, name, ch), e)
                        wt = pair_tile((kind, name, ch), w)
                        for r in range(w // P):
                            f = 2 * ch + r
                            if half == 0 and not (name == 0 and ch == 0):
                                pe.wait_ge(hid_done, count(un, NCH, ch - 1 + r))
                            for k in range(KD):
                                if name == 0 and ch == 0 and half == 0 and r == 0:
                                    wait_h(0, 1, k)
                                last = mm3(ps[:, f % 3, half * T:(half + 1) * T], [x[:, k, r * P:(r + 1) * P] for x in wt],
                                           tokens(k, slice(0, T)), k == 0, k == KD - 1)
                        last.then_inc(up_used if half else gate_used, 1)

                def down(ch):
                    n = F_CHUNKS[ch][1] // P
                    wait_split(pe, ("down", name, ch), e)
                    w = pair_tile(("down", name, ch), D, n)
                    pe.wait_ge(hid_low, count(un, NCH, ch + 1))
                    if ch == 0:
                        for b in range(4):
                            if name == "moe":
                                pe.wait_ge(free[4 + b], e + MOE_FIRST[4 + b])
                            else:
                                wait_free(pe, "down", name, b)
                    for r in range(n):
                        for b in range(4):
                            t, half = b // 2, b % 2
                            h = [x[:, ch % 2, r * T + t * P:r * T + (t + 1) * P] for x in (hidh, hidl)]
                            last = mm3(ps[:, 4 + b, :], h, [x[:, r, half * 512:(half + 1) * 512] for x in w],
                                       ch == 0 and r == 0, ch == NCH - 1 and r == n - 1)
                            if ch == NCH - 1:
                                last.then_inc(full[4 + b], 1)
                    if ch < NCH - 1:
                        last.then_inc(down_used, 1)

                for ch in range(NCH):
                    if name != "moe":
                        for a in ada_of_step(name * NCH + ch - 1):
                            ada_product(1, a)
                    gate_up(ch)
                    if ch > 0:
                        down(ch - 1)
                down(NCH - 1)

            def gather(e, b0):
                pe.wait_ge(sel_ready, e + 1)
                for k in range(KD):
                    for t in range(TT):
                        for i, part in enumerate((xnh, xnl)):
                            last = mm(ps[:, b0 + k // 4, (k % 4) * P:(k % 4 + 1) * P], part[:, t, k * P:(k + 1) * P], sel[:, t, :],
                                      t == 0 and i == 0, t == 1 and i == 1)
                last.then_inc(gathered, 1)

            def few_tokens(e):
                un = (e, DENSE_UNITS)

                def products(kind, ch):
                    w, half = F_CHUNKS[ch][1], int(kind == "up")
                    wait_split(pe, (kind, "moe", ch), e)
                    wt = pair_tile((kind, "moe", ch), w)
                    for k in range(KD):
                        last = mm3(ps[:, ch % 2, half * 256:half * 256 + w], (xgh[:, k, :], xgl[:, k, :]), [x[:, k, :] for x in wt], k == 0, k == KD - 1)
                    last.then_inc(up_used if half else gate_used, 1)

                def turn_hidden(ch):
                    pe.wait_ge(hid_done, count(un, NCH, ch + 1))
                    for r in range(F_CHUNKS[ch][1] // P):
                        last = pe.transpose(ps[:, 2, r * P:(r + 1) * P], hid[:, r * P:(r + 1) * P], ident)
                    last.then_inc(few_turned, 1)

                def down(ch):
                    n = F_CHUNKS[ch][1] // P
                    wait_split(pe, ("down", "moe", ch), e)
                    w = pair_tile(("down", "moe", ch), D, n)
                    pe.wait_ge(hid_low, count(un, NCH, ch + 1))
                    if ch == 0:
                        pe.wait_ge(free[7], e + MOE_FIRST[7])
                        pe.wait_ge(selT_ready, e + 1)
                    for half, b in enumerate((3, 7)):
                        for r in range(n):
                            last = mm3(ps[:, b, :], [x[:, ch % 2, r * P:(r + 1) * P] for x in (hidh, hidl)],
                                       [x[:, r, half * 512:(half + 1) * 512] for x in w], ch == 0 and r == 0, ch == NCH - 1 and r == n - 1)
                        if ch == NCH - 1:
                            last.then_inc(few_sum, 1)
                    if ch < NCH - 1:
                        last.then_inc(down_used, 1)

                for ch in range(NCH):
                    pe.wait_ge(hid_done, count(un, NCH, ch - 1))
                    products("gate", ch)
                    if ch > 0:
                        turn_hidden(ch - 1)
                    products("up", ch)
                    if ch > 0:
                        down(ch - 1)
                    if ch == GATHER_AT:
                        for b in (4, 5):
                            pe.wait_ge(free[b], e + MOE_FIRST[b])
                        gather(e + 1, 4)
                turn_hidden(NCH - 1)
                down(NCH - 1)
                pe.wait_ge(xraw_ready, 2 * e + 4)
                for half in range(2):
                    pe.wait_ge(few_yg, 2 * e + half + 1)
                    for t in range(TT):
                        b = 4 + 2 * t + half
                        pe.wait_ge(free[b], e + MOE_FIRST[b])
                        for i, part in enumerate((ygh, ygl)):
                            last = mm(ps[:, b, :], selT[:, t * P:(t + 1) * P], part[:, half * 512:(half + 1) * 512], i == 0, i == 1)
                        last.then_inc(full[b], 1)

            def wait_h(l, which, k):
                if k % 2 == 0:
                    pe.wait_ge(hT_low, 4 * (2 * l + which) + k // 2 + 1)

            pe.wait_ge(consts_loaded, 32)
            pe.wait_ge(c_loaded, 16 * len(as_rows))
            n = KD + GAINS
            pe.transpose(bank("columns")[:, 0:n], cols_as_rows[:, :], ident[0:n, 0:n]).then_inc(full_of("columns"), 1)
            pe.wait_ge(cond_done, 1)
            for l in range(DEPTH):
                if l == 0:
                    for a in range(9):
                        if a in ROW_SUMS:
                            ada_row(a)
                        if a > 0:
                            ada_product(0, a - 1)
                transpose_x("xT", l)
                for j, (c0, w) in enumerate(W_IN_SLOTS):
                    wait_split(pe, ("in", l, j))
                    wait_free(pe, "in", l, j)
                    wt, b = pair_tile(("in", l, j), w), bank("in", l, j)
                    for m in range(2):
                        for k in range(KD):
                            if j == 0 and m == 0:
                                wait_h(l, 0, k)
                            if j <= 4 or j == 7:
                                last = mm3(b[:, m * 256:m * 256 + w], tokens(k, slice(m * P, (m + 1) * P)), [x[:, k, :] for x in wt], k == 0, k == KD - 1)
                            else:
                                last = mm3(b[:, m * T:(m + 1) * T], [x[:, k, m * P:(m + 1) * P] for x in wt], tokens(k, slice(0, T)), k == 0, k == KD - 1)
                    last.then_inc(full_of("in", l, j), 1)
                    if l == 0:
                        for a in ada_beside(j - 1):
                            ada_product(0, a)
                    if j == 7:
                        transposes(l)
                        pe.wait_ge(small_loaded, SMALL)
                    if j == 9:
                        indexer(l)
                    if j == 10:
                        latent_and_pool(l)
                    if 13 <= j < 13 + HC:
                        stick_values(l, j - 13)
                    if 12 <= j < 12 + HC:
                        stick_sums(l, j - 12)
                    if 11 <= j < 11 + HC:
                        stick_logits(l, j - 11)
                    if j == SOFTMAX[0]:
                        logits(l, 0)
                    if j == SOFTMAX[0] + 1:
                        turn_probabilities(l, 0)
                    if j == SOFTMAX[0] + 2:
                        weigh_values(l, 0)
                    if j == SOFTMAX[1]:
                        logits(l, 1)
                    if j == SOFTMAX[1] + 2:
                        turn_probabilities(l, 1)
                if l == 0:
                    for a in ada_beside(NIN - 1):
                        ada_product(0, a)
                weigh_values(l, 1)

                for t in range(TT):
                    wait_read(pe, "av", l, t)
                wait_read(pe, "yb", l)
                wait_read(pe, "yc", l, 1)
                branches = [[(("br", l, 0), 2, 0, yaT[:, 0, :]), (("br", l, 0), 2, 1, yaT[:, 1, :]), (("br", l, 1), 1, 0, yaT[:, 2, :])],
                            [(("br", l, 2), 2, k, ybT[:, k, :]) for k in range(2)],
                            [(("br", l, 3), 2, k, ycT[:, k, :]) for k in range(2)]]
                for i, parts in enumerate(branches):
                    for n_part, (key, n, k, y) in enumerate(parts):
                        first, final = n_part == 0, n_part == len(parts) - 1
                        wait_loaded(pe, key)
                        for m in range(4):
                            if first:
                                wait_free(pe, "br", l, i, m)
                            for half in range(2):
                                d0 = (2 * m + half) * P
                                last = mm(bank("br", l, i, m)[:, half * T:(half + 1) * T], w_tile(key, D, n)[:, k, d0:d0 + P], y,
                                          first and half == 0, final and half == 1, skip_group_check=True)
                            if final:
                                last.then_inc(full_of("br", l, i, m), 1)
                        if key[2] == 0 and k == 1:
                            last.then_inc(br_used, 1)
                for b in range(4):
                    wait_free(pe, "y", l, b)
                for j in range(4):
                    wait_split(pe, ("out", l, j))
                    pe.wait_ge(merged, 4 * l + j + 1)
                    w = pair_tile(("out", l, j), D, 2)
                    for b in range(4):
                        t, half = b // 2, b % 2
                        for k in range(2):
                            last = mm3(ps[:, b, :], tokens(2 * j + k, slice(t * P, (t + 1) * P)),
                                       [x[:, k, half * 512:(half + 1) * 512] for x in w], j == 0 and k == 0, j == 3 and k == 1)
                        if j == 3:
                            last.then_inc(full[b], 1)
                    if j < 3:
                        last.then_inc(out_used, 1)

                transpose_x("hT", l)
                if l == 0:
                    for u in range(DENSE_UNITS):
                        unit(u, u)
                    for a in ada_of_step(DENSE_UNITS * NCH - 1):
                        ada_product(1, a)
                else:
                    wait_free(pe, "route", l)
                    for t in range(TT):
                        for k in range(KD):
                            wait_h(l, 1, k)
                            for i, h in enumerate(tokens(k, slice(t * P, (t + 1) * P))):
                                last = mm(bank("route", l)[:, t * E:(t + 1) * E], h.bitcast(F32), wroute[:, k, :], k == 0 and i == 0, k == KD - 1 and i == 1)
                    last.then_inc(full_of("route", l), 1)
                    pe.wait_ge(picked_done, 1)
                    o = bank("count", l)
                    for t in range(TT):
                        if t == 1:
                            mm(o[:, E:2 * E], ones, picked[:, 0, :], True, False)
                        mm(o[:, t * E:(t + 1) * E], const("earlier"), picked[:, t, :], t == 0, True)
                    for t in range(TT):
                        last = mm(o[:, 2 * E:3 * E], ones, picked[:, t, :], t == 0, t == 1)
                    last.then_inc(full_of("count", l), 1)
                    pe.wait_ge(xn_low, TT)
                    gather(0, 0)
                    wait_read(pe, "count", 1)
                    with pe.Fori(0, E) as e:
                        pe.wait_ge(xg_ready, e + 1)
                        for t in range(TT):
                            last = pe.transpose(ps[:, 3, t * P:(t + 1) * P], sel[:, t, :].bitcast(F32), ident)
                        last.then_inc(sel_turned, 1)
                        with pe.If(has_many(pe, e)):
                            unit("moe", e)
                            gather(e + 1, 0)
                            pe.wait_ge(selT_ready, e + 1)
                            stand_in(pe, [(few_turned, NCH), (few_sum, 2)])
                        with pe.Else():
                            few_tokens(e)

        @block.scalar
        def _(act):
            chain = [0]

            def link(ins):
                chain[0] += 1
                ins.then_inc(a_chain, 1)
                act.wait_ge(a_chain, chain[0])

            def squares(n, t, src, junk):
                act.activation(junk, src, ACT.Square, accum_out=ss[:, n, t:t + 1]).then_inc(ss_done, 1)

            def root(n, t, tiles=1):
                act.wait_ge(var_done, TT * n + t + tiles)
                act.activation(guess[:, n, t:t + tiles], var[:, n, t:t + tiles], ACT.Sqrt).then_inc(guess_done, tiles)

            def modulate(name, l, which):
                for j in (1, 3):
                    wait_full(act, name, l, j)
                    for m in range(2):
                        k = 2 * j + m
                        last = act.activation(hraw[:, j, m * T:(m + 1) * T], bank(name, l, j)[:, m * T:(m + 1) * T], ACT.Identity,
                                              scale=modc[:, l, 2 * which + 1, k:k + 1], bias=modc[:, l, 2 * which, k:k + 1])
                    last.then_inc(free_of(name, l, j), 1)
                    for i in (j - 1, j):
                        wait_read(act, name, l, i)
                        act.activation(hTh[:, 2 * i:2 * i + 2, :].rearrange("p a t -> p (a t)"), hraw[:, i, :], ACT.Copy).then_inc(hT_high, 1)

            def high_part(key, e=0, after_expert=False):
                n = SPLITS.index(key)
                wait_loaded(act, key, e * TURNS if key[1] == "moe" else 0)
                if key[1] == "moe" and n - NP >= SPLIT0:
                    wait_used(act, SPLITS[n - NP], e)
                elif key[1] == "moe" and after_expert:
                    wait_used(act, SPLITS[n - NP + UNIT], e - 1)
                elif n >= NP:
                    wait_used(act, SPLITS[n - NP])
                act.activation(high_of(key), ring[:, slot(key), 0:width(key)], ACT.Copy).then_inc(high, 1)

            def high_after(key, e=0):
                high_part(SPLITS[SPLITS.index(key) + NP], e)

            def high_next(e, i):
                with act.If(e < E - 1):
                    high_part(SPLITS[SPLIT0 + i], e + 1, after_expert=True)

            def gathered_high(e):
                for half in range(2):
                    act.wait_ge(xraw_ready, 2 * e + half + 1)
                    act.activation(xgh[:, 4 * half:4 * half + 4, :].rearrange("p k s -> p (k s)"), xraw[:, half * 512:(half + 1) * 512], ACT.Copy)\
                       .then_inc(xg_high, 1)

            def walk(name, e, few=False):
                un = unit_of((None, name), e)
                e = e if name == "moe" else 0
                for i, (kind, ch) in enumerate(ORDER):
                    w = F_CHUNKS[ch][1]
                    if few and (kind == "gate" and ch > 0 or i == UNIT - 1):
                        turned = ch - 1 if kind == "gate" else ch
                        n = F_CHUNKS[turned][1]
                        act.wait_ge(few_turned, e * NCH + turned + 1)
                        act.activation(hidh[:, turned % 2, 0:n], ps[:, 2, 0:n], ACT.Copy).then_inc(hid_high, 1)
                    if kind == "up":
                        act.wait_ge(up_used, count(un, NCH, ch + 1))
                        if few:
                            last = act.activation(sig[:, 0:w], ps[:, ch % 2, 0:w], ACT.Sigmoid)
                        else:
                            for r in range(w // P):
                                last = act.activation(sig[:, r * T:(r + 1) * T], ps[:, (2 * ch + r) % 3, 0:T], ACT.Sigmoid)
                        last.then_inc(sig_done, 1)
                    if name != "moe" or i + NP < UNIT:
                        high_after((kind, name, ch), e)
                    elif i + 1 < UNIT and not (few and kind == "down"):
                        high_next(e, i + NP - UNIT)
                    if few and (kind, ch) == ("up", NCH - 1):
                        gathered_high(e + 1)
                    if few and i == UNIT - 1:
                        for half, b in enumerate((3, 7)):
                            act.wait_ge(few_sum, 2 * e + half + 1)
                            act.activation(ygh[:, half * 512:(half + 1) * 512], ps[:, b, :], ACT.Copy).then_inc(few_high, 1)
                        high_next(e, NP - 2)
                    if kind == "up" and not few:
                        n = w // P * T
                        act.wait_ge(hid_done, count(un, NCH, ch + 1))
                        act.activation(hidh[:, ch % 2, 0:n], hid[:, 0:n], ACT.Copy).then_inc(hid_high, 1)

            def copy_out(key, dst, src, scale=1.0):
                wait_full(act, *key)
                act.activation(dst, src, ACT.Copy, scale=scale).then_inc(free_of(*key), 1)

            def pairs(b, w=256, n=2, step=256):
                return b[:, 0:n * step].rearrange("p (m n) -> p m n", m=n)[:, :, 0:w]

            wait_full(act, "columns")
            act.activation(cond[:, :], bank("columns")[:, 0:KD], ACT.Sigmoid).then_inc(cond_sig, 1)
            for l in range(DEPTH):
                if l == 0:
                    act.wait_ge(x_loaded, 16)
                for t in range(TT):
                    if l > 0:
                        act.wait_ge(x_added, TT * (2 * l - 1) + t + 1)
                    squares(5 * l, t, x[:, t, :], xn[:, t, :])
                    if l > 0:
                        root(5 * l, t)
                if l == 0:
                    root(5 * l, 0, TT)
                if l == 0:
                    for a in ROW_SUMS:
                        copy_out(("adarow", a), acc[0:1, a % NACC, :], bank("adarow", a)[0:1, 0:256])
                if l == 0:
                    high_part(SPLITS[0])
                    high_part(SPLITS[1])
                for a in range(8):
                    wait_read(act, *ada_job(l, a))
                modulate("xT", l, 0)
                if l == 0:
                    high_part(SPLITS[2])
                if l == 0:
                    act.wait_ge(angles, 1)
                    act.activation(cs[:, :, :, :], red[:, :, :, :], ACT.Sin).then_inc(tables, 1)
                for j in range(20):
                    key = ("in", l, j)
                    b = bank(*key)
                    if j < 5:
                        c0, w = W_IN_SLOTS[j]
                        copy_out(key, natP[:, :, c0:c0 + w], pairs(b, w))
                        if j == 1:
                            act.wait_ge(free_of(*key), ORD[key] + 1)
                            for t in range(TT):
                                squares(5 * l + 1, t, natP[:, t, C_LAT:C_LAT + LAT], latn[:, t, :])
                            root(5 * l + 1, 0, TT)
                    elif j == 5:
                        copy_out(key, qkc[:, 0:2, :], pairs(b), HEAD ** -0.5)
                    elif j == 6:
                        copy_out(key, qkc[:, 2:4, :], pairs(b))
                    elif j == 7:
                        copy_out(key, vc[:, :, :], pairs(b))
                    else:
                        copy_out(key, gT[:, 2 * (j - 8):2 * (j - 8) + 2, :], pairs(b))
                    if j < NIN - 1:
                        high_after(key)
                    if j == 7:
                        act.wait_ge(small_loaded, SMALL)
                        copy_out(("tr", l, 0), trs[:, 0:4, :], pairs(bank("tr", l, 0), P, 4, P))
                        wait_full(act, "tr", l, 1)
                        act.activation(trs[:, 4:6, :], pairs(bank("tr", l, 1), P, 2, P), ACT.Copy)
                        act.activation(trs[:, 6:8, :], pairs(bank("tr", l, 1)[:, T:], P, 2, P), ACT.Copy,
                                       scale=glat[:, l:l + 1]).then_inc(free_of("tr", l, 1), 1)
                        copy_out(("tr", l, 2), qT[:, 0:2, :], pairs(bank("tr", l, 2)))
                        copy_out(("tr", l, 3), qT[:, 2, :], bank("tr", l, 3)[:, 0:T])
                    if j == 9:
                        for t in range(TT):
                            nk = P * (t + 1)
                            for par in range(2):
                                wait_full(act, "idx", l, t, par)
                                act.activation(relu_at(t, par), bank("idx", l, t, par)[:, 0:2 * nk], ACT.Relu)\
                                   .then_inc(free_of("idx", l, t, par), 1)
                    if j == 10:
                        wait_full(act, "ukv", l)
                        u = pairs(bank("ukv", l), NOPE + HEAD, 2, P)
                        act.wait_ge(q_ready, l + 1)
                        act.activation(kn[:, :, ROPE:HEAD], u[:, :, 0:NOPE], ACT.Copy)
                        act.activation(kn[:, :, HEAD + ROPE:P], u[:, :, 0:NOPE], ACT.Copy)
                        act.activation(va[:, :, :], u[:, :, NOPE:NOPE + HEAD], ACT.Copy).then_inc(free_of("ukv", l), 1)
                        copy_out(("pool", l), poolT[:, :, :], pairs(bank("pool", l)))
                        copy_out(("kT", l), kT[:, :], bank("kT", l)[:, 0:T])
                        wait_full(act, "yb", l)
                        for g in range(2):
                            last = act.activation(ybT[:, g, :], bank("yb", l)[:, g * T:(g + 1) * T], ACT.Copy, scale=pscale[:, l, g:g + 1])
                        last.then_inc(free_of("yb", l), 1)
                    if 12 <= j < 12 + HC:
                        h = j - 12
                        wait_full(act, "stick2", l, h)
                        act.activation(aT[:, h % 2, :], bank("stick2", l, h)[:, 0:384], ACT.Exp).then_inc(free_of("stick2", l, h), 1)
                    if 11 <= j < 11 + HC:
                        h = j - 11
                        wait_full(act, "stick", l, h)
                        s = spl[:, h % 2, :]
                        act.activation(s, bank("stick", l, h)[:, 0:384], ACT.Abs).then_inc(stick_abs, 1)
                        act.wait_ge(stick_abs, HC * l + h + 1)
                        link(act.activation(s, s, ACT.Exp, scale=-1.0))
                        act.activation(s, s, ACT.Ln, bias=1.0).then_inc(stick_log, 1)
                    for t in range(TT):
                        if j == SOFTMAX[0] + 2 and t == 0:
                            copy_out(("av", l, 0), yaT[:, :, 0:P], pairs(bank("av", l, 0), P, 3, P))
                        if j == SOFTMAX[t]:
                            nk = P * (t + 1)
                            act.wait_ge(max_done, TT * l + t + 1)
                            for i in range(HA):
                                s = lg[:, i * nk:(i + 1) * nk]
                                last = act.activation(s, s, ACT.Exp, bias=nmax[:, l, t, i:i + 1], accum_out=psum_exp[:, l, t, i:i + 1])
                            last.then_inc(exp_done, 1)
                        if j == SOFTMAX[t] + 1 + t:
                            for kt in range(t + 1):
                                copy_out(("pT", l, t, kt, 1), pT[:, kt, 3 * P:6 * P], bank("pT", l, t, kt, 1)[:, 0:3 * P])
                wait_read(act, "in", l, NIN - 1)
                act.activation(big[:, :], big[:, :], ACT.Sigmoid).then_inc(gates_done, 1)
                copy_out(("av", l, 1), yaT[:, :, P:2 * P], pairs(bank("av", l, 1), P, 3, P))
                high_part(("out", l, 2))
                for m in range(4):
                    act.wait_ge(merged_raw, 4 * l + m + 1)
                    act.activation(hTh[:, 2 * m:2 * m + 2, :].rearrange("p a t -> p (a t)"), mraw[:, m % 2, :], ACT.Copy).then_inc(merged_high, 1)
                for j in range(3):
                    high_after(("out", l, j))
                for t in range(TT):
                    wait_full(act, "y", l, 2 * t)
                    wait_full(act, "y", l, 2 * t + 1)
                    squares(5 * l + 2, t, ps[:, 2 * t:2 * t + 2, :].rearrange("p a b -> p (a b)"), xn[:, t, :])
                    root(5 * l + 2, t)
                for t in range(TT):
                    act.wait_ge(x_added, TT * 2 * l + t + 1)
                    squares(5 * l + 3, t, x[:, t, :], xn[:, t, :])
                    root(5 * l + 3, t)
                for a in range(12, 20):
                    wait_read(act, *ada_job(l, a))
                modulate("hT", l, 1)
                high_after(("out", l, 3))
                if l == 0:
                    for u in range(DENSE_UNITS):
                        walk(u, u)
                else:
                    for t in range(TT):
                        act.activation(xnh[:, t, :], xn[:, t, :], ACT.Copy).then_inc(xn_high, 1)
                    act.wait_ge(route_d, 1)
                    act.activation(rsm[:, 5, 0:TT], rsm[:, 4, 0:TT], ACT.Exp).then_inc(route_e, 1)

                    gathered_high(0)
                    wait_read(act, "count", 1)
                    with act.Fori(0, E) as e:
                        act.wait_ge(sel_turned, e + 1)
                        act.activation(selT[:, :], ps[:, 3, 0:T], ACT.Copy).then_inc(selT_ready, 1)
                        with act.If(has_many(act, e)):
                            walk("moe", e)
                            gathered_high(e + 1)
                            stand_in(act, [(few_high, 2)])
                        with act.Else():
                            walk("moe", e, few=True)
                        high_next(e, NP - 1)
                for t in range(TT):
                    if l == 0:
                        wait_read(act, "down", DENSE_UNITS - 1, 2 * t)
                        wait_read(act, "down", DENSE_UNITS - 1, 2 * t + 1)
                    else:
                        act.wait_ge(free[4 + 2 * t], MOE_FIRST[4 + 2 * t] + E)
                        act.wait_ge(free[5 + 2 * t], MOE_FIRST[5 + 2 * t] + E)
                    squares(5 * l + 4, t, yacc[:, t, :], xn[:, t, :])
                    root(5 * l + 4, t)

        @block.vector
        def _(dve):
            chain = [0]

            def link(ins):
                chain[0] += 1
                ins.then_inc(v_chain, 1)
                dve.wait_ge(v_chain, chain[0])

            def variance(n, t, width, tiles=1):
                dve.wait_ge(ss_done, TT * n + t + tiles)
                dve.tensor_scalar(var[:, n, t:t + tiles], ss[:, n, t:t + tiles], 1.0 / width, EPS, ALU.mult, ALU.add).then_inc(var_done, tiles)

            def newton(n, t, tiles=1):
                dve.wait_ge(guess_done, TT * n + t + tiles)
                g, a, b = guess[:, n, t:t + tiles], newt[:, 0, t:t + tiles], newt[:, 1, t:t + tiles]
                link(dve.reciprocal(g, g))
                link(dve.tensor_tensor(a, g, g, ALU.mult))
                link(dve.tensor_tensor(b, a, var[:, n, t:t + tiles], ALU.mult))
                link(dve.tensor_scalar(a, b, -0.5, 1.5, ALU.mult, ALU.add))
                link(dve.tensor_tensor(rstd[:, n, t:t + tiles], g, a, ALU.mult))

            def normalize_x(n):
                if n == 0:
                    variance(n, 0, D, TT)
                    newton(n, 0, TT)
                for t in range(TT):
                    if n > 0:
                        variance(n, t, D)
                        newton(n, t)
                    dve.tensor_scalar(xn[:, t, :], x[:, t, :], rstd[:, n, t:t + 1], None, ALU.mult).then_inc(xn_done, 1)

            def modulate(name, l, which):
                for j in (0, 2):
                    wait_full(dve, name, l, j)
                    for m in range(2):
                        k = 2 * j + m
                        last = dve.tensor_scalar(hraw[:, j, m * T:(m + 1) * T], bank(name, l, j)[:, m * T:(m + 1) * T],
                                                 modc[:, l, 2 * which + 1, k:k + 1], modc[:, l, 2 * which, k:k + 1], ALU.mult, ALU.add)
                    last.then_inc(free_of(name, l, j), 1)
                for j in range(4):
                    dve.wait_ge(hT_high, 4 * (2 * l + which) + j + 1)
                    h = [x[:, 2 * j:2 * j + 2, :].rearrange("p a t -> p (a t)") for x in (hTh, hTl)]
                    dve.tensor_tensor(h[1], hraw[:, j, :], h[0].bitcast(F32), ALU.subtract).then_inc(hT_low, 1)

            def ada_sum(l, a):
                n = ada_index(l, a)
                if n >= NACC:
                    wait_full(dve, *ada_job((n - NACC) // NADA, (n - NACC) % NADA))
                wait_loaded(dve, ("ada", l, a))
                w = ring[:, slot(("ada", l, a)), :].rearrange("p (k n) -> p k n", k=KD)
                o = acc[:, n % NACC, :]
                for k in range(KD):
                    if k == 0:
                        i = dve.tensor_scalar(o, w[:, k, :], cond[:, k:k + 1], None, ALU.mult)
                    else:
                        i = dve.scalar_tensor_tensor(out=o, in0=w[:, k, :], scalar=cond[:, k:k + 1], in1=o, op0=ALU.mult, op1=ALU.add)
                    if k < KD - 1:
                        link(i)
                    else:
                        i.then_inc(acc_done, 1)

            def ada_read(l, a):
                seg, q = a // 4, a % 4
                wait_full(dve, *ada_job(l, a))
                b = ada_bank(l, a)
                if seg in (2, 5):
                    g = GTG[(l, seg)]
                    dve.wait_ge(gain_loaded[g], 16 * ROWS[(l, seg)])
                    r = gtg[:, g, 256 * q:256 * (q + 1)]
                    i = dve.tensor_tensor(r, b[:, 0:256], r, ALU.mult)
                else:
                    which = 0 if seg < 2 else 1
                    scale = seg in (1, 4)
                    o = modc[:, l, 2 * which + scale, 2 * q:2 * q + 2]
                    if scale:
                        i = dve.scalar_tensor_tensor(out=o, in0=b[:, 0:2], scalar=1.0, in1=gcol[:, l, which, 2 * q:2 * q + 2],
                                                     op0=ALU.add, op1=ALU.mult)
                    else:
                        i = dve.tensor_copy(o, b[:, 0:2])
                if l == 0 or a % 2:
                    i.then_inc(free_of(*ada_job(l, a)), 1)

            def rope(view, heads):
                def tab(i):
                    return cs[:, :, i:i + 1, :].to_broadcast([P, TT, heads, HALF])
                x1, x2 = view[:, :, :, 0:HALF], view[:, :, :, HALF:ROPE]
                r = [rot[:, i, 0:TT * heads * HALF].rearrange("p (t h c) -> p t h c", t=TT, h=heads) for i in range(4)]
                dve.tensor_tensor(r[0], x1, tab(0), ALU.mult)
                dve.tensor_tensor(r[1], x2, tab(1), ALU.mult)
                dve.tensor_tensor(r[2], x2, tab(0), ALU.mult)
                link(dve.tensor_tensor(r[3], x1, tab(1), ALU.mult))
                dve.tensor_tensor(x1, r[0], r[1], ALU.subtract)
                return dve.tensor_tensor(x2, r[2], r[3], ALU.add)

            def heads_view(c0, n, w=HEAD):
                return natP[:, :, c0:c0 + n * w].rearrange("p t (h c) -> p t h c", h=n)

            def choose(l, t):
                nk = P * (t + 1)
                s, tk = score[:, t, 0:nk], take[:, t, 0:nk]
                for i, h in enumerate((0, 1, 2, 3)):
                    wait_read(dve, "idx", l, t, h % 2)
                    r = relu_at(t, h % 2)[:, (h // 2) * nk:(h // 2 + 1) * nk]
                    w = natP[:, t, C_WI + h:C_WI + h + 1]
                    if i == 0:
                        link(dve.tensor_scalar(s, r, w, None, ALU.mult))
                    else:
                        link(dve.scalar_tensor_tensor(out=s, in0=r, scalar=w, in1=s, op0=ALU.mult, op1=ALU.add))
                diag = score[:, t, nk - P:nk]
                link(dve.tensor_tensor(diag, diag, const("not_causal"), ALU.add))
                for _ in range(TOPK // 8):
                    link(dve.max(top8[:, :], s))
                    link(dve.match_replace(s, top8[:, :], s, TAKEN))
                link(dve.tensor_scalar(tk, s, TAKEN, None, ALU.is_equal))
                diag = take[:, t, nk - P:nk]
                link(dve.tensor_tensor(diag, diag, const("causal"), ALU.mult))
                link(dve.tensor_scalar(tk, tk, -FAR, FAR, ALU.mult, ALU.add))

            def stick(l, h):
                dve.wait_ge(stick_abs, HC * l + h + 1)
                r, s = rel[:, h % 2, :], spl[:, h % 2, :]
                dve.tensor_scalar(r, bank("stick", l, h)[:, 0:384], 0.0, None, ALU.max).then_inc(free_of("stick", l, h), 1)
                dve.wait_ge(free_of("stick", l, h), ORD[("stick", l, h)] + 1)
                dve.wait_ge(stick_log, HC * l + h + 1)
                dve.tensor_tensor(s, r, s, ALU.add).then_inc(stick_sp, 1)

            def softmax(l, t):
                nk = P * (t + 1)
                for g, idx in enumerate(logit_groups(t)):
                    key = ("logit", l, t, g)
                    wait_full(dve, *key)
                    n = len(idx)
                    o = lg[:, idx[0] * nk:(idx[0] + n) * nk].rearrange("p (h k) -> p h k", h=n)
                    i = bank(*key)[:, 0:n * nk].rearrange("p (h k) -> p h k", h=n)
                    dve.scalar_tensor_tensor(out=o, in0=i, scalar=HEAD ** -0.5, in1=take[:, t:t + 1, 0:nk].to_broadcast([P, n, nk]),
                                             op0=ALU.mult, op1=ALU.add).then_inc(free_of(*key), 1)
                    wait_read(dve, *key)
                v = lg[:, 0:HA * nk].rearrange("p (h k) -> p h k", h=HA)
                dve.tensor_reduce(nmax[:, l, t, :], v, AX.X, ALU.max, negate=True).then_inc(max_done, 1)
                dve.wait_ge(exp_done, TT * l + t + 1)
                link(dve.reciprocal(pinv[:, l, t, :], psum_exp[:, l, t, :]))
                for half in range(2):
                    o = v[:, 3 * half:3 * half + 3, :]
                    dve.tensor_tensor(o, o, pinv[:, l, t, 3 * half:3 * half + 3].unsqueeze(2).to_broadcast([P, 3, nk]), ALU.mult)\
                       .then_inc(prob_done, 1)

            def turned_probabilities(l, t):
                for kt in range(t + 1):
                    wait_full(dve, "pT", l, t, kt, 0)
                    dve.tensor_copy(pT[:, kt, 0:3 * P], bank("pT", l, t, kt, 0)[:, 0:3 * P]).then_inc(free_of("pT", l, t, kt, 0), 1)

            def merge(l):
                def gate(i, m):
                    return gT[:, 8 * i + 2 * m:8 * i + 2 * m + 2, :].rearrange("p a t -> p (a t)")

                def low_merged(m):
                    dve.wait_ge(merged_high, 4 * l + m + 1)
                    h = [x[:, 2 * m:2 * m + 2, :].rearrange("p a t -> p (a t)") for x in (hTh, hTl)]
                    dve.tensor_tensor(h[1], mraw[:, m % 2, :], h[0].bitcast(F32), ALU.subtract).then_inc(merged, 1)

                dve.wait_ge(gates_done, l + 1)
                for i in range(3):
                    for m in range(4):
                        wait_full(dve, "br", l, i, m)
                        dve.tensor_tensor(gate(i, m), bank("br", l, i, m), gate(i, m), ALU.mult).then_inc(free_of("br", l, i, m), 1)
                        if i > 0:
                            wait_read(dve, "br", l, i, m)
                        if i == 1:
                            link(dve.tensor_tensor(gate(0, m), gate(0, m), gate(1, m), ALU.add))
                        if i == 2:
                            if m > 1:
                                dve.wait_ge(merged, 4 * l + m - 1)
                            dve.tensor_tensor(mraw[:, m % 2, :], gate(0, m), gate(2, m), ALU.add).then_inc(merged_raw, 1)
                            if m > 0:
                                low_merged(m - 1)
                low_merged(3)

            def add_residual(n, t, halves, g):
                variance(n, t, D)
                for half, (src, raises) in enumerate(halves):
                    c = slice(512 * half, 512 * half + 512)
                    i = dve.tensor_tensor(resid[:, t, c], src, gtg[:, g, c], ALU.mult)
                    if raises is None:
                        link(i)
                    else:
                        i.then_inc(raises[0], 1)
                        dve.wait_ge(*raises)
                newton(n, t)
                dve.scalar_tensor_tensor(out=x[:, t, :], in0=resid[:, t, :], scalar=rstd[:, n, t:t + 1], in1=x[:, t, :],
                                         op0=ALU.mult, op1=ALU.add).then_inc(x_added, 1)
                dve.wait_ge(x_added, TT * ((n // 5) * 2 + (1 if n % 5 == 4 else 0)) + t + 1)

            def route():
                wait_full(dve, "route", 1)
                lgt = rsm[:, 0, :]
                dve.tensor_copy(lgt, bank("route", 1)[:, 0:TT * E]).then_inc(free_of("route", 1), 1)
                wait_read(dve, "route", 1)
                l3 = lgt.rearrange("p (t e) -> p t e", t=TT)
                v4 = [rout[:, i, :].rearrange("p (t e o) -> p t e o", t=TT, e=E) for i in range(2)]
                other = l3.unsqueeze(2).to_broadcast([P, TT, E, E])
                own = l3.unsqueeze(3).to_broadcast([P, TT, E, E])
                early = const("earlier8").rearrange("p (a e o) -> p a e o", a=1, e=E).to_broadcast([P, TT, E, E])
                dve.tensor_tensor(v4[0], other, own, ALU.is_gt)
                link(dve.tensor_tensor(v4[1], other, own, ALU.is_equal))
                link(dve.tensor_tensor(v4[1], v4[1], early, ALU.mult))
                link(dve.tensor_tensor(v4[0], v4[0], v4[1], ALU.add))
                rank = rsm[:, 1, :]
                link(dve.tensor_reduce(rank, v4[0].rearrange("p t e o -> p (t e) o"), AX.X, ALU.add))
                pick = [rsm[:, 2 + i, :] for i in range(2)]
                for i in range(2):
                    link(dve.tensor_scalar(pick[i], rank, float(i), None, ALU.is_equal))
                both = [rout[:, 2, TT * E * i:TT * E * (i + 1)] for i in range(2)]
                vals = rout[:, 2, 4 * TT * E:4 * TT * E + 2 * TT].rearrange("p (i t) -> p i t", i=2)
                for i in range(2):
                    if i == 0:
                        dve.tensor_tensor(picked[:, :, :].rearrange("p t e -> p (t e)"), pick[0], pick[1], ALU.add).then_inc(picked_done, 1)
                    link(dve.tensor_tensor(both[i], pick[i], lgt, ALU.mult))
                    link(dve.tensor_reduce(vals[:, i, :], both[i].rearrange("p (t e) -> p t e", t=TT), AX.X, ALU.add))
                dve.tensor_tensor(rsm[:, 4, 0:TT], vals[:, 1, :], vals[:, 0, :], ALU.subtract).then_inc(route_d, 1)
                dve.wait_ge(route_e, 1)
                e2, p1, p2 = rsm[:, 5, 0:TT], rsm[:, 5, TT:2 * TT], rsm[:, 5, 2 * TT:3 * TT]
                link(dve.tensor_scalar(p2, e2, 1.0, None, ALU.add))
                link(dve.reciprocal(p1, p2))
                link(dve.tensor_tensor(p2, e2, p1, ALU.mult))
                for i, p in enumerate((p1, p2)):
                    link(dve.tensor_tensor(both[i].rearrange("p (t e) -> p t e", t=TT), pick[i].rearrange("p (t e) -> p t e", t=TT),
                                           p.unsqueeze(2).to_broadcast([P, TT, E]), ALU.mult))
                link(dve.tensor_tensor(comb[:, :, :], both[0].rearrange("p (t e) -> p t e", t=TT),
                                       both[1].rearrange("p (t e) -> p t e", t=TT), ALU.add))
                wait_full(dve, "count", 1)
                before = bank("count", 1)[:, 0:TT * E].rearrange("p (t e) -> p t e", t=TT)
                own = place_of[:, :, 0:E]
                link(dve.scalar_tensor_tensor(out=own, in0=before, scalar=1.0, in1=picked[:, :, :], op0=ALU.add, op1=ALU.mult))
                link(dve.tensor_scalar(own, own, -1.0, None, ALU.add))
                dve.tensor_copy(tokens_of[:, :], bank("count", 1)[:, 2 * E:3 * E]).then_inc(free_of("count", 1), 1)

            def select(e):
                for t in range(TT):
                    last = dve.tensor_scalar(sel[:, t, :], const("place"), place_of[:, t, bass.ds(e, 1)], None, ALU.is_equal)
                last.then_inc(sel_ready, 1)

            def hidden(un, ch, few=False):
                w = F_CHUNKS[ch][1]
                dve.wait_ge(sig_done, count(un, NCH, ch + 1))
                if few:
                    tiles = [(ps[:, ch % 2, 0:w], ps[:, ch % 2, 256:256 + w], slice(0, w))]
                else:
                    tiles = [(ps[:, (2 * ch + r) % 3, 0:T], ps[:, (2 * ch + r) % 3, T:2 * T], slice(r * T, (r + 1) * T)) for r in range(w // P)]
                for g, _, c in tiles:
                    last = dve.tensor_tensor(gsig[:, c], g, sig[:, c], ALU.mult)
                last.then_inc(gate_prod, 1)
                dve.wait_ge(gate_prod, count(un, NCH, ch + 1))
                for _, u, c in tiles:
                    last = dve.tensor_tensor(hid[:, c], u, gsig[:, c], ALU.mult)
                last.then_inc(hid_done, 1)

            def hidden_low(un, ch, few=False):
                w = F_CHUNKS[ch][1]
                n = w if few else w // P * T
                dve.wait_ge(hid_high, count(un, NCH, ch + 1))
                src = ps[:, 2, 0:n] if few else hid[:, 0:n]
                dve.tensor_tensor(hidl[:, ch % 2, 0:n], src, hidh[:, ch % 2, 0:n].bitcast(F32), ALU.subtract).then_inc(hid_low, 1)

            def low_next(e, kind):
                with dve.If(e < E - 1):
                    lower_part(dve, "vector", (kind, "moe", 0), e + 1)

            def gathered_raw(e, b0):
                dve.wait_ge(gathered, e + 1)
                for k in range(KD):
                    last = dve.tensor_scalar(xraw[:, k * P:(k + 1) * P], ps[:, b0 + k // 4, (k % 4) * P:(k % 4 + 1) * P],
                                             modc[:, 1, 3, k:k + 1], modc[:, 1, 2, k:k + 1], ALU.mult, ALU.add)
                    if k % 4 == 3:
                        last.then_inc(xraw_ready, 1)

            def gathered_low(e):
                for half in range(2):
                    dve.wait_ge(xg_high, 2 * e + half + 1)
                    h = [x[:, 4 * half:4 * half + 4, :].rearrange("p k s -> p (k s)") for x in (xgh, xgl)]
                    last = dve.tensor_tensor(h[1], xraw[:, half * 512:(half + 1) * 512], h[0].bitcast(F32), ALU.subtract)
                last.then_inc(xg_ready, 1)

            def add_unit(b, e):
                t, half = b // 2, b % 2
                o = yacc[:, t, half * 512:(half + 1) * 512]
                dve.scalar_tensor_tensor(out=o, in0=ps[:, 4 + b, :], scalar=comb[:, t, bass.ds(e, 1)],
                                         in1=o, op0=ALU.mult, op1=ALU.add).then_inc(free[4 + b], 1)

            def reduce_angles():
                dve.wait_ge(consts_loaded, 32)
                dve.wait_ge(positions_loaded, 16)
                link(dve.tensor_copy(pos_f[:, :], pos_i[:, :]))
                for t in range(TT):
                    link(dve.tensor_scalar(ang[:, t, :], const("inv_freq"), pos_f[:, t:t + 1], None, ALU.mult))
                for i, quarter in enumerate((0.25, 0.0)):
                    link(dve.tensor_scalar(turns[:, :, i, :], ang[:, :, :], 1.0 / (2.0 * np.pi), quarter, ALU.mult, ALU.add))
                link(dve.tensor_scalar(turns[:, :, :, :], turns[:, :, :, :], ROUNDER, None, ALU.add))
                link(dve.tensor_scalar(turns[:, :, :, :], turns[:, :, :, :], -ROUNDER, None, ALU.add))
                for i, shift in enumerate((np.pi / 2, 0.0)):
                    src = ang[:, :, :]
                    for part in TWO_PI:
                        link(dve.scalar_tensor_tensor(out=red[:, :, i, :], in0=turns[:, :, i, :], scalar=-part, in1=src, op0=ALU.mult, op1=ALU.add))
                        src = red[:, :, i, :]
                    link(dve.tensor_scalar(red[:, :, i, :], red[:, :, i, :], shift, None, ALU.add))
                dve.tensor_scalar(red[:, :, :, :], red[:, :, :, :], PI_BELOW, -PI_BELOW, ALU.min, ALU.max).then_inc(angles, 1)

            dve.wait_ge(cond_sig, 1)
            dve.tensor_tensor(cond[:, :], cond[:, :], bank("columns")[:, 0:KD], ALU.mult).then_inc(cond_done, 1)
            dve.tensor_copy(gcol[:, :, :, :].rearrange("p l n k -> p (l n k)"), bank("columns")[:, KD:KD + GAINS]).then_inc(free_of("columns"), 1)
            wait_read(dve, "columns")
            dve.wait_ge(cond_done, 1)
            for l in range(DEPTH):
                def sum_beside(j):
                    if l == 0:
                        for a in ada_beside(j):
                            ada_sum(0, a)

                def read_beside(j):
                    if l == 0:
                        for a in ada_beside(j):
                            ada_read(0, a)

                if l == 0:
                    ada_sum(0, 2)
                normalize_x(5 * l)
                if l == 0:
                    for a in range(8):
                        if a == 3:
                            ada_sum(0, 5)
                        if a == 5:
                            ada_sum(0, 7)
                        ada_read(0, a)
                modulate("xT", l, 0)
                if l == 0:
                    reduce_angles()
                sum_beside(0)
                sum_beside(1)
                dve.wait_ge(tables, 1)
                read_beside(0)
                wait_read(dve, "in", l, 1)
                variance(5 * l + 1, 0, LAT, TT)
                newton(5 * l + 1, 0, TT)
                for t in range(TT):
                    last = dve.tensor_scalar(latn[:, t, :], natP[:, t, C_LAT:C_LAT + LAT], rstd[:, 5 * l + 1, t:t + 1], None, ALU.mult)
                last.then_inc(lat_ready, 1)
                link(rope(heads_view(C_QA, HA), HA))
                sum_beside(2)
                read_beside(1)
                wait_read(dve, "in", l, 2)
                link(rope(natP[:, :, C_KR:C_KR + ROPE].unsqueeze(2), 1))
                dve.tensor_copy(kn[:, :, 0:ROPE], natP[:, :, C_KR:C_KR + ROPE])
                dve.tensor_copy(kn[:, :, HEAD:HEAD + ROPE], natP[:, :, C_KR:C_KR + ROPE]).then_inc(q_ready, 1)
                sum_beside(3)
                read_beside(2)
                wait_read(dve, "in", l, 3)
                link(rope(heads_view(C_QI, HI + 1), HI + 1))
                dve.tensor_copy(ki[:, :, 0:HEAD], natP[:, :, C_KI:C_KI + HEAD])
                dve.tensor_copy(ki[:, :, HEAD:P], natP[:, :, C_KI:C_KI + HEAD]).then_inc(qi_ready, 1)
                for j in range(4, 9):
                    sum_beside(j)
                    read_beside(j - 1)
                for t in range(TT):
                    choose(l, t)
                sum_beside(11)
                sum_beside(12)
                for j in range(11, NIN):
                    if j > 11:
                        sum_beside(j + 1)
                    if 11 <= j < 11 + HC:
                        stick(l, j - 11)
                    read_beside(j - 1)
                    if 13 <= j < 13 + HC and j % 2 == 0:
                        g = (j - 14) // 2
                        wait_full(dve, "yc", l, g)
                        dve.tensor_copy(ycT[:, g, :], bank("yc", l, g)[:, 0:T]).then_inc(free_of("yc", l, g), 1)
                    for t in range(TT):
                        if j == SOFTMAX[t] + 1 + t:
                            turned_probabilities(l, t)
                        if j == SOFTMAX[t]:
                            softmax(l, t)
                read_beside(NIN - 1)
                merge(l)
                lower_part(dve, "vector", ("gate", 0 if l == 0 else "moe", 0))
                if l == 1:
                    lower_part(dve, "vector", ("up", "moe", 0))
                for t in range(TT):
                    add_residual(5 * l + 2, t, [(ps[:, 2 * t + h, :], (free[2 * t + h], ORD[("y", l, 2 * t + h)] + 1)) for h in range(2)], GTG[(l, 2)])
                normalize_x(5 * l + 3)
                modulate("hT", l, 1)
                dve.wait_ge(acc0, l + 1)
                if l == 0:
                    for u in range(DENSE_UNITS):
                        for ch in range(NCH):
                            n = u * NCH + ch
                            for a in ada_of_step(n):
                                ada_sum(1, a)
                            if ch < NCH - 1:
                                lower_part(dve, "vector", ("gate", u, ch + 1))
                            hidden((u, 0), ch)
                            for a in ada_of_step(n - 1):
                                ada_read(1, a)
                            hidden_low((u, 0), ch)
                        if u < DENSE_UNITS - 1:
                            lower_part(dve, "vector", ("gate", u + 1, 0))
                        for b in range(4):
                            wait_full(dve, "down", u, b)
                            add_unit(b, u)
                    for a in ada_of_step(DENSE_UNITS * NCH - 1):
                        ada_read(1, a)
                else:
                    for t in range(TT):
                        dve.wait_ge(xn_high, t + 1)
                        dve.tensor_tensor(xnl[:, t, :], xn[:, t, :], xnh[:, t, :].bitcast(F32), ALU.subtract).then_inc(xn_low, 1)
                    link(dve.memset(place_of[:, :, E:E + 1], -1.0))
                    route()
                    wait_read(dve, "count", 1)
                    select(0)
                    gathered_raw(0, 0)
                    gathered_low(0)
                    with dve.Fori(0, E) as e:
                        un = (e, DENSE_UNITS)

                        dve.wait_ge(sel_turned, e + 1)
                        select(e + 1)
                        with dve.If(has_many(dve, e)):
                            for ch in range(NCH):
                                if ch < NCH - 1:
                                    lower_part(dve, "vector", ("gate", "moe", ch + 1), e)
                                hidden(un, ch)
                                if ch < NCH - 1:
                                    lower_part(dve, "vector", ("up", "moe", ch + 1), e)
                                hidden_low(un, ch)
                                lower_part(dve, "vector", ("down", "moe", ch), e)
                            low_next(e, "gate")
                            gathered_raw(e + 1, 0)
                            gathered_low(e + 1)
                            stand_in(dve, [(few_yg, 2)])
                        with dve.Else():
                            for ch in range(NCH):
                                if ch > 0:
                                    hidden_low(un, ch - 1, few=True)
                                if ch < NCH - 1:
                                    lower_part(dve, "vector", ("gate", "moe", ch + 1), e)
                                hidden(un, ch, few=True)
                                if ch < NCH - 1:
                                    lower_part(dve, "vector", ("up", "moe", ch + 1), e)
                                lower_part(dve, "vector", ("down", "moe", ch), e)
                                if ch == GATHER_AT:
                                    gathered_raw(e + 1, 4)
                            low_next(e, "gate")
                            hidden_low(un, NCH - 1, few=True)
                            gathered_low(e + 1)
                            for half, b in enumerate((3, 7)):
                                dve.wait_ge(few_high, 2 * e + half + 1)
                                c = slice(half * 512, (half + 1) * 512)
                                dve.tensor_tensor(ygl[:, c], ps[:, b, :], ygh[:, c].bitcast(F32), ALU.subtract).then_inc(few_yg, 1)
                        low_next(e, "up")
                        for b in range(4):
                            dve.wait_ge(full[4 + b], e + MOE_FIRST[4 + b] + 1)
                            add_unit(b, e)
                for t in range(TT):
                    add_residual(5 * l + 4, t, [(yacc[:, t, 512 * h:512 * h + 512], None) for h in range(2)], GTG[(l, 5)])


_NAMES = ["x", "c", "positions", "w_ada", "b_ada", "norm_gains", "w_in", "g_kv_latent", "w_uk", "w_uv", "w_pool",
          "pool_scale", "w_br_a", "w_br_b", "w_br_c", "w_out", "w_gate_dense", "w_up_dense", "w_down_dense",
          "w_router", "w_gate_moe", "w_up_moe", "w_down_moe"]


def kernel(**inputs):
    import concourse.bacc as bacc
    from concourse.bass_utils import run_bass_kernel_spmd

    nc = bacc.Bacc("TRN2", target_bir_lowering=False, num_devices=1)
    arrays, aps = {}, []
    consts, const_at = shape_constants()
    for name in _NAMES + ["consts"]:
        a = consts if name == "consts" else np.ascontiguousarray(inputs[name])
        arrays["in_" + name] = a
        aps.append(nc.dram_tensor("in_" + name, a.shape, mybir.dt.from_np(a.dtype), kind="ExternalInput").ap())
    y = nc.dram_tensor("y", inputs["x"].shape, F32, kind="ExternalOutput").ap()
    build_trunk(nc, *aps, const_at, y)
    r = run_bass_kernel_spmd(nc, [arrays], core_ids=[0])
    return r.results[0]["y"]
```
